# Optimizing a Trainium2 kernel written in Bass

```python
import jax, jax.numpy as jnp
from jax import lax
import numpy as np
import math

D_MODEL = 1024
BATCH = 1
SEQ = 512
DEPTH = 2

GRID_W = 64
CTX_LEN = 256
EPS = 1e-6

FOURIER_HEADS = 4
FOURIER_HEAD_DIM = D_MODEL // 8
FOURIER_WIDTH = FOURIER_HEADS * FOURIER_HEAD_DIM
HEAD_DIM = 64
N_Q_HEADS = (D_MODEL // 2) // HEAD_DIM
N_KV_HEADS = 2
GQA_GROUP = N_Q_HEADS // N_KV_HEADS
ATTN_WIDTH = N_Q_HEADS * HEAD_DIM
KV_WIDTH = N_KV_HEADS * HEAD_DIM
Q_END = FOURIER_WIDTH + ATTN_WIDTH
IN_WIDTH = Q_END + 2 * KV_WIDTH
MIX_WIDTH = FOURIER_WIDTH + ATTN_WIDTH
WINDOW = 128
BLOCK = 128
ROPE_THETA = 10000.0
POOL_WINDOWS = (2, 4, 8, 16)
POOL_GROUP = D_MODEL // len(POOL_WINDOWS)
FFN_HIDDEN = ((-(-8 * D_MODEL // 3)) + 255) // 256 * 256
N_EVEN = (DEPTH + 1) // 2
N_ODD = DEPTH // 2


def rms_norm(x, g):
    xf = x.astype(jnp.float32)
    y = xf * lax.rsqrt(jnp.mean(xf * xf, axis=-1, keepdims=True) + EPS)
    return (y * g.astype(jnp.float32)).astype(x.dtype)

def ada_mod(cond, w, b):
    m = jax.nn.silu(cond) @ w + b
    return jnp.split(m[..., None, :], 6, axis=-1)

def modulate(h, shift, scale):
    return h * (1 + scale) + shift

def axial_rope_tables(n_tokens):
    rows = n_tokens // GRID_W
    row = jnp.repeat(jnp.arange(rows, dtype=jnp.float32), GRID_W)
    col = jnp.tile(jnp.arange(GRID_W, dtype=jnp.float32), rows)
    n_freq = HEAD_DIM // 4
    inv = ROPE_THETA ** (-jnp.arange(n_freq, dtype=jnp.float32) / n_freq)
    ang = jnp.concatenate([row[:, None] * inv[None], col[:, None] * inv[None]], axis=-1)
    return jnp.cos(ang), jnp.sin(ang)

def apply_rope(x, cos, sin):
    xf = x.astype(jnp.float32).reshape(*x.shape[:-1], HEAD_DIM // 2, 2)
    x1, x2 = xf[..., 0], xf[..., 1]
    c, s = cos[:, None, :], sin[:, None, :]
    out = jnp.stack([x1 * c - x2 * s, x1 * s + x2 * c], axis=-1).reshape(x.shape)
    return out.astype(x.dtype)

def fourier_mix(u):
    B, N, _ = u.shape
    uh = u.astype(jnp.float32).reshape(B, N, FOURIER_HEADS, FOURIER_HEAD_DIM)
    y = jnp.fft.fftn(uh, axes=(1, 3), norm='ortho').real
    return y.reshape(B, N, FOURIER_WIDTH).astype(u.dtype)

def sink_logits(sink, lead_shape):
    s = sink.astype(jnp.float32).reshape(1, N_KV_HEADS, GQA_GROUP, 1, 1)
    return jnp.broadcast_to(s, lead_shape + (1,))

def window_attention(q, k, v, k_ctx, v_ctx, sink):
    B, S = q.shape[:2]
    L = k_ctx.shape[1]
    nb = S // BLOCK
    scale = HEAD_DIM ** -0.5
    pad = ((0, 0), (BLOCK, BLOCK), (0, 0), (0, 0))
    kp, vp = jnp.pad(k, pad), jnp.pad(v, pad)
    qb = q.reshape(B, nb, BLOCK, N_KV_HEADS, GQA_GROUP, HEAD_DIM).transpose(1, 0, 2, 3, 4, 5)

    def one_block(args):
        i, q_i = args
        start = i * BLOCK
        k_i = lax.dynamic_slice_in_dim(kp, start, 3 * BLOCK, axis=1)
        v_i = lax.dynamic_slice_in_dim(vp, start, 3 * BLOCK, axis=1)
        qpos = start + jnp.arange(BLOCK)
        kpos = start - BLOCK + jnp.arange(3 * BLOCK)
        valid = (jnp.abs(kpos[None, :] - qpos[:, None]) <= WINDOW) & (kpos[None, :] >= 0) & (kpos[None, :] < S)
        s_win = jnp.einsum('bqkgd,bjkd->bkgqj', q_i, k_i).astype(jnp.float32) * scale
        s_win = jnp.where(valid[None, None, None], s_win, -jnp.inf)
        s_ctx = jnp.einsum('bqkgd,bckd->bkgqc', q_i, k_ctx).astype(jnp.float32) * scale
        logits = jnp.concatenate([s_win, s_ctx, sink_logits(sink, s_win.shape[:-1])], axis=-1)
        p = jax.nn.softmax(logits, axis=-1)
        p_win = p[..., :3 * BLOCK].astype(v.dtype)
        p_ctx = p[..., 3 * BLOCK:3 * BLOCK + L].astype(v.dtype)
        return (jnp.einsum('bkgqj,bjkd->bqkgd', p_win, v_i)
                + jnp.einsum('bkgqc,bckd->bqkgd', p_ctx, v_ctx))

    o = lax.map(one_block, (jnp.arange(nb), qb))
    return o.transpose(1, 0, 2, 3, 4, 5).reshape(B, S, ATTN_WIDTH)

def context_attention(q_c, k_c, v_c, sink):
    B, L = q_c.shape[:2]
    qg = q_c.reshape(B, L, N_KV_HEADS, GQA_GROUP, HEAD_DIM)
    s = jnp.einsum('bqkgd,bckd->bkgqc', qg, k_c).astype(jnp.float32) * HEAD_DIM ** -0.5
    p = jax.nn.softmax(jnp.concatenate([s, sink_logits(sink, s.shape[:-1])], axis=-1), axis=-1)
    p = p[..., :L].astype(v_c.dtype)
    return jnp.einsum('bkgqc,bckd->bqkgd', p, v_c).reshape(B, L, ATTN_WIDTH)

def even_mixer(xn, xcn, w_in, w_out, sink, cos, sin, with_ctx_out):
    B, S, _ = xn.shape
    L = xcn.shape[1]
    proj = xn @ w_in
    f_in = proj[..., :FOURIER_WIDTH]
    q = proj[..., FOURIER_WIDTH:Q_END].reshape(B, S, N_Q_HEADS, HEAD_DIM)
    k = proj[..., Q_END:Q_END + KV_WIDTH].reshape(B, S, N_KV_HEADS, HEAD_DIM)
    v = proj[..., Q_END + KV_WIDTH:].reshape(B, S, N_KV_HEADS, HEAD_DIM)
    q = apply_rope(q, cos, sin)
    k = apply_rope(k, cos, sin)
    kv_c = xcn @ w_in[:, Q_END:]
    k_c = kv_c[..., :KV_WIDTH].reshape(B, L, N_KV_HEADS, HEAD_DIM)
    v_c = kv_c[..., KV_WIDTH:].reshape(B, L, N_KV_HEADS, HEAD_DIM)
    attn = window_attention(q, k, v, k_c, v_c, sink)
    y = jnp.concatenate([fourier_mix(f_in), attn], axis=-1) @ w_out
    if not with_ctx_out:
        return y, None
    fq_c = xcn @ w_in[:, :Q_END]
    f_c = fq_c[..., :FOURIER_WIDTH]
    q_c = fq_c[..., FOURIER_WIDTH:].reshape(B, L, N_Q_HEADS, HEAD_DIM)
    attn_c = context_attention(q_c, k_c, v_c, sink)
    y_c = jnp.concatenate([fourier_mix(f_c), attn_c], axis=-1) @ w_out
    return y, y_c

def pool_mix(h, w_pool, scale):
    B, N, _ = h.shape
    hf = h.astype(jnp.float32)
    csum = jnp.pad(jnp.cumsum(hf, axis=1), ((0, 0), (1, 0), (0, 0)))
    t = np.arange(N)
    outs = []
    for g, w in enumerate(POOL_WINDOWS):
        lo = np.clip(t - w // 2, 0, N)
        hi = np.clip(t + w // 2, 0, N)
        sl = slice(g * POOL_GROUP, (g + 1) * POOL_GROUP)
        cg = csum[..., sl]
        count = jnp.asarray(hi - lo, dtype=jnp.float32)[None, :, None]
        outs.append((cg[:, hi] - cg[:, lo]) / count - hf[..., sl])
    y = jnp.stack(outs, axis=2).astype(h.dtype)
    y = jnp.einsum('bngc,gcd->bngd', y, w_pool).reshape(B, N, D_MODEL)
    return y * scale

def swiglu(h, w1, w3, w2):
    return (jax.nn.silu(h @ w1) * (h @ w3)) @ w2

def first_inputs(seed: int = 0) -> dict:
    key = jax.random.key(seed)
    ks = jax.random.split(key, 18)
    f32 = jnp.float32

    def nrm(k, shape, s=1.0):
        return s * jax.random.normal(k, shape, f32)

    return {
        'x': nrm(ks[0], (BATCH, SEQ, D_MODEL)),
        'c': nrm(ks[1], (BATCH, D_MODEL)),
        'ctx': nrm(ks[2], (BATCH, CTX_LEN, D_MODEL)),
        'c_ctx': nrm(ks[3], (D_MODEL,)),
        'ada_w': nrm(ks[4], (DEPTH, D_MODEL, 6 * D_MODEL), 0.5 * D_MODEL ** -0.5),
        'ada_b': nrm(ks[5], (DEPTH, 6 * D_MODEL), 0.02),
        'norm_mix_g': 1.0 + nrm(ks[6], (DEPTH, D_MODEL), 0.05),
        'norm_ffn_g': 1.0 + nrm(ks[7], (DEPTH, D_MODEL), 0.05),
        'mix_in_w': nrm(ks[8], (N_EVEN, D_MODEL, IN_WIDTH), D_MODEL ** -0.5),
        'mix_out_w': nrm(ks[9], (N_EVEN, MIX_WIDTH, D_MODEL), MIX_WIDTH ** -0.5),
        'attn_sink': nrm(ks[10], (N_EVEN, N_Q_HEADS), 0.5),
        'pool_w': nrm(ks[11], (N_ODD, len(POOL_WINDOWS), POOL_GROUP, POOL_GROUP), POOL_GROUP ** -0.5),
        'pool_scale': 1.0 + nrm(ks[12], (N_ODD, D_MODEL), 0.1),
        'ffn_w1': nrm(ks[13], (DEPTH, D_MODEL, FFN_HIDDEN), D_MODEL ** -0.5),
        'ffn_w3': nrm(ks[14], (DEPTH, D_MODEL, FFN_HIDDEN), D_MODEL ** -0.5),
        'ffn_w2': nrm(ks[15], (DEPTH, FFN_HIDDEN, D_MODEL), FFN_HIDDEN ** -0.5),
        'final_g': 1.0 + nrm(ks[16], (D_MODEL,), 0.05),
    }

def first_block(x, c, ctx, c_ctx, ada_w, ada_b, norm_mix_g, norm_ffn_g, mix_in_w, mix_out_w,
              attn_sink, pool_w, pool_scale, ffn_w1, ffn_w3, ffn_w2, final_g):
    n_tokens = x.shape[1]
    cos, sin = axial_rope_tables(n_tokens)
    last_ctx_reader = max(range(0, DEPTH, 2))
    h, hc = x, ctx
    for layer in range(DEPTH):
        sh1, sc1, g1, sh2, sc2, g2 = ada_mod(c, ada_w[layer], ada_b[layer])
        update_ctx = layer < last_ctx_reader
        need_ctx_in = update_ctx or (layer % 2 == 0 and layer <= last_ctx_reader)
        if need_ctx_in:
            csh1, csc1, cg1, csh2, csc2, cg2 = ada_mod(c_ctx, ada_w[layer], ada_b[layer])
            xcn = modulate(rms_norm(hc, norm_mix_g[layer]), csh1, csc1)
        xn = modulate(rms_norm(h, norm_mix_g[layer]), sh1, sc1)
        j = layer // 2
        if layer % 2 == 0:
            y, y_c = even_mixer(xn, xcn, mix_in_w[j], mix_out_w[j], attn_sink[j], cos, sin, update_ctx)
        else:
            y = pool_mix(xn, pool_w[j], pool_scale[j])
            y_c = pool_mix(xcn, pool_w[j], pool_scale[j]) if update_ctx else None
        h = h + g1 * y
        hn = modulate(rms_norm(h, norm_ffn_g[layer]), sh2, sc2)
        h = h + g2 * swiglu(hn, ffn_w1[layer], ffn_w3[layer], ffn_w2[layer])
        if update_ctx:
            hc = hc + cg1 * y_c
            hcn = modulate(rms_norm(hc, norm_ffn_g[layer]), csh2, csc2)
            hc = hc + cg2 * swiglu(hcn, ffn_w1[layer], ffn_w3[layer], ffn_w2[layer])
    return rms_norm(h, final_g)


DEPTH_2 = 1

MEM_LEN = 256
NSA_HEADS = 8
NSA_KV_HEADS = 2
NSA_GROUP = NSA_HEADS // NSA_KV_HEADS
SB_HEADS = 8
MIX_WIDTH_2 = (NSA_HEADS + SB_HEADS) * HEAD_DIM
CMP_LEN = 32
CMP_STRIDE = 16
CMP_HIDDEN = 256
SEL_BLOCK = 64
SEL_TOPK = 16
WINDOW_2 = 512
Q_BLOCK = 128
ROT_DIM = HEAD_DIM // 4
ROPE_THETA_2 = 500000.0
MEM_HEADS = 4
D_FF = 2816
NORM_EPS = 1e-6
NEG = -1e30
FORCE_SCORE = 1e4

KV_W = NSA_KV_HEADS * HEAD_DIM
IN_SPLITS = [NSA_HEADS * HEAD_DIM, KV_W, KV_W, KV_W, KV_W, KV_W, KV_W, NSA_HEADS * 3,
             SB_HEADS * HEAD_DIM, SB_HEADS * HEAD_DIM, SB_HEADS * HEAD_DIM]
IN_COLS = sum(IN_SPLITS)


def rms_norm_2(x, g):
    x32 = x.astype(jnp.float32)
    y = x32 * lax.rsqrt(jnp.mean(x32 * x32, axis=-1, keepdims=True) + NORM_EPS)
    return (y * g.astype(jnp.float32)).astype(x.dtype)

def rope_angles(pos):
    freqs = ROPE_THETA_2 ** (-jnp.arange(0, ROT_DIM, 2, dtype=jnp.float32) / ROT_DIM)
    return pos.astype(jnp.float32)[..., None] * freqs

def apply_rope_2(x, ang):
    half = ROT_DIM // 2
    x1, x2, xp = x[..., :half], x[..., half:ROT_DIM], x[..., ROT_DIM:]
    c = jnp.cos(ang).astype(x.dtype)
    s = jnp.sin(ang).astype(x.dtype)
    return jnp.concatenate([x1 * c - x2 * s, x2 * c + x1 * s, xp], axis=-1)

def masked_softmax(s, mask):
    s = jnp.where(mask, s.astype(jnp.float32), NEG)
    m = jnp.max(s, axis=-1, keepdims=True)
    p = jnp.where(mask, jnp.exp(s - m), 0.0)
    return p / jnp.maximum(jnp.sum(p, axis=-1, keepdims=True), 1e-30)

def swiglu_2(h, wg, wu, wd):
    return (jax.nn.silu(h @ wg) * (h @ wu)) @ wd

def overlap_matrix(n_cmp, n_sel):
    cs = np.arange(n_cmp)[:, None] * CMP_STRIDE
    ss = np.arange(n_sel)[None, :] * SEL_BLOCK
    ov = np.minimum(cs + CMP_LEN, ss + SEL_BLOCK) - np.maximum(cs, ss)
    return jnp.asarray(np.clip(ov, 0, None).astype(np.float32) / CMP_LEN)

def compress(t, pe, w1, w2):
    B, H, T, dk = t.shape
    ratio = CMP_LEN // CMP_STRIDE
    n_chunks = T // CMP_STRIDE
    n_cmp = n_chunks - ratio + 1
    chunks = t.reshape(B, H, n_chunks, CMP_STRIDE, dk)
    blocks = jnp.concatenate([chunks[:, :, r:r + n_cmp] for r in range(ratio)], axis=3)
    blocks = blocks + pe
    flat = blocks.reshape(B, H, n_cmp, CMP_LEN * dk)
    return jax.nn.gelu(flat @ w1) @ w2

def nsa_mixer(q, k_cmp, v_cmp, k_sel, v_sel, k_win, v_win, gates, pos,
              pe_k, w1_k, w2_k, pe_v, w1_v, w2_v, g_q, g_kc, g_ks, g_kw):
    B, T = q.shape[:2]
    dk = HEAD_DIM
    scale = dk ** -0.5
    ang = rope_angles(pos)
    q = q.reshape(B, T, NSA_KV_HEADS, NSA_GROUP, dk).transpose(0, 2, 3, 1, 4)
    q = apply_rope_2(rms_norm_2(q, g_q), ang[:, None, None])

    def heads(t):
        return t.reshape(B, T, NSA_KV_HEADS, dk).transpose(0, 2, 1, 3)

    n_cmp = (T - CMP_LEN) // CMP_STRIDE + 1
    cmp_end = jnp.arange(n_cmp) * CMP_STRIDE + CMP_LEN - 1
    ang_c = rope_angles(pos[:, cmp_end])
    kc = apply_rope_2(rms_norm_2(compress(heads(k_cmp), pe_k, w1_k, w2_k), g_kc), ang_c[:, None])
    vc = compress(heads(v_cmp), pe_v, w1_v, w2_v)
    n_sel = T // SEL_BLOCK
    top_n = min(SEL_TOPK, n_sel)
    ks_blocks = apply_rope_2(rms_norm_2(heads(k_sel), g_ks), ang[:, None]).reshape(B, NSA_KV_HEADS, n_sel, SEL_BLOCK, dk)
    vs_blocks = heads(v_sel).reshape(B, NSA_KV_HEADS, n_sel, SEL_BLOCK, dk)
    w_ov = overlap_matrix(n_cmp, n_sel)
    pad = ((0, 0), (0, 0), (WINDOW_2, 0), (0, 0))
    kw_pad = jnp.pad(apply_rope_2(rms_norm_2(heads(k_win), g_kw), ang[:, None]), pad)
    vw_pad = jnp.pad(heads(v_win), pad)
    gates = jax.nn.sigmoid(gates.reshape(B, T, NSA_KV_HEADS, NSA_GROUP, 3).transpose(0, 2, 3, 1, 4))

    bi = jnp.arange(B)[:, None, None, None]
    hi = jnp.arange(NSA_KV_HEADS)[None, :, None, None]
    jblk = jnp.arange(n_sel)

    def block_fn(i):
        s0 = i * Q_BLOCK
        tq = s0 + jnp.arange(Q_BLOCK)
        qb = lax.dynamic_slice_in_dim(q, s0, Q_BLOCK, axis=3)
        gb = lax.dynamic_slice_in_dim(gates, s0, Q_BLOCK, axis=3)
        m_c = cmp_end[None, :] <= tq[:, None]
        p_c = masked_softmax(jnp.einsum('bhgqd,bhnd->bhgqn', qb, kc) * scale, m_c)
        o_c = jnp.einsum('bhgqn,bhnd->bhgqd', p_c, vc)
        imp = jnp.einsum('bhgqn,nj->bhqj', p_c, w_ov)
        cur = tq // SEL_BLOCK
        valid = jblk[None, :] * SEL_BLOCK <= tq[:, None]
        forced = (jblk[None, :] == 0) | (jblk[None, :] == cur[:, None]) | (jblk[None, :] == cur[:, None] - 1)
        score = jnp.where(valid & forced, FORCE_SCORE, jnp.where(valid, imp, -1.0))
        _, idx = lax.top_k(score, top_n)
        ksb = ks_blocks[bi, hi, idx].reshape(B, NSA_KV_HEADS, Q_BLOCK, top_n * SEL_BLOCK, dk)
        vsb = vs_blocks[bi, hi, idx].reshape(B, NSA_KV_HEADS, Q_BLOCK, top_n * SEL_BLOCK, dk)
        kpos = (idx[..., None] * SEL_BLOCK + jnp.arange(SEL_BLOCK)).reshape(B, NSA_KV_HEADS, Q_BLOCK, -1)
        m_s = (kpos <= tq[:, None])[:, :, None]
        p_s = masked_softmax(jnp.einsum('bhgqd,bhqkd->bhgqk', qb, ksb) * scale, m_s)
        o_s = jnp.einsum('bhgqk,bhqkd->bhgqd', p_s, vsb)
        kwb = lax.dynamic_slice_in_dim(kw_pad, s0, Q_BLOCK + WINDOW_2, axis=2)
        vwb = lax.dynamic_slice_in_dim(vw_pad, s0, Q_BLOCK + WINDOW_2, axis=2)
        kpos_w = s0 - WINDOW_2 + jnp.arange(Q_BLOCK + WINDOW_2)
        diff = tq[:, None] - kpos_w[None, :]
        m_w = (kpos_w[None, :] >= 0) & (diff >= 0) & (diff < WINDOW_2)
        p_w = masked_softmax(jnp.einsum('bhgqd,bhkd->bhgqk', qb, kwb) * scale, m_w)
        o_w = jnp.einsum('bhgqk,bhkd->bhgqd', p_w, vwb)
        o = gb[..., 0:1] * o_c + gb[..., 1:2] * o_s + gb[..., 2:3] * o_w
        return o.astype(q.dtype)

    out = lax.map(block_fn, jnp.arange(T // Q_BLOCK))
    return out.transpose(1, 0, 4, 2, 3, 5).reshape(B, T, NSA_HEADS * dk)

def stick_breaking(q, k, v):
    B, T = q.shape[:2]
    dk = HEAD_DIM
    scale = dk ** -0.5

    def heads(t):
        return t.reshape(B, T, SB_HEADS, dk).transpose(0, 2, 1, 3)

    q, k, v = heads(q), heads(k), heads(v)
    kpos = jnp.arange(T)

    def block_fn(i):
        s0 = i * Q_BLOCK
        tq = s0 + jnp.arange(Q_BLOCK)
        qb = lax.dynamic_slice_in_dim(q, s0, Q_BLOCK, axis=2)
        z = jnp.einsum('bhqd,bhkd->bhqk', qb, k).astype(jnp.float32) * scale
        mask = kpos[None, :] < tq[:, None]
        log_rem = jnp.where(mask, jax.nn.log_sigmoid(-z), 0.0)
        suffix = lax.cumsum(log_rem, axis=3, reverse=True) - log_rem
        a = jnp.where(mask, jnp.exp(jax.nn.log_sigmoid(z) + suffix), 0.0)
        return jnp.einsum('bhqk,bhkd->bhqd', a, v).astype(q.dtype)

    out = lax.map(block_fn, jnp.arange(T // Q_BLOCK))
    return out.transpose(1, 0, 3, 2, 4).reshape(B, T, SB_HEADS * dk)

def memory_cross_attention(h, mem_n, wq, wk, wv, wo, g_q, g_k):
    B, T = h.shape[:2]
    M = mem_n.shape[1]
    q = rms_norm_2((h @ wq).reshape(B, T, MEM_HEADS, HEAD_DIM), g_q)
    k = rms_norm_2((mem_n @ wk).reshape(B, M, MEM_HEADS, HEAD_DIM), g_k)
    v = (mem_n @ wv).reshape(B, M, MEM_HEADS, HEAD_DIM)
    s = jnp.einsum('bqhd,bkhd->bhqk', q, k).astype(jnp.float32) * HEAD_DIM ** -0.5
    p = jax.nn.softmax(s, axis=-1)
    o = jnp.einsum('bhqk,bkhd->bqhd', p, v).astype(h.dtype).reshape(B, T, MEM_HEADS * HEAD_DIM)
    return o @ wo

def second_inputs(seed: int = 0) -> dict:
    key = jax.random.key(seed)
    ks = iter(jax.random.split(key, 40))

    def dense(shape, fan_in):
        return jax.random.normal(next(ks), (DEPTH_2,) + shape, jnp.float32) * fan_in ** -0.5

    def gain(n):
        return 1.0 + 0.05 * jax.random.normal(next(ks), (DEPTH_2, n), jnp.float32)

    x = jax.random.normal(next(ks), (BATCH, SEQ, D_MODEL), jnp.float32)
    mem = jax.random.normal(next(ks), (BATCH, MEM_LEN, D_MODEL), jnp.float32)
    start = jax.random.randint(next(ks), (BATCH, 1), 0, 4096, dtype=jnp.int32)
    positions = (start + jnp.arange(SEQ, dtype=jnp.int32)[None, :]).astype(jnp.int32)
    return {
        "x": x, "mem": mem, "positions": positions,
        "ffn1_norm": gain(D_MODEL),
        "ffn1_wg": dense((D_MODEL, D_FF), D_MODEL),
        "ffn1_wu": dense((D_MODEL, D_FF), D_MODEL),
        "ffn1_wd": dense((D_FF, D_MODEL), D_FF),
        "mix_norm": gain(D_MODEL),
        "w_in": dense((D_MODEL, IN_COLS), D_MODEL),
        "nsa_q_norm": gain(HEAD_DIM),
        "nsa_kc_norm": gain(HEAD_DIM),
        "nsa_ks_norm": gain(HEAD_DIM),
        "nsa_kw_norm": gain(HEAD_DIM),
        "cmp_pos_k": 0.1 * jax.random.normal(next(ks), (DEPTH_2, CMP_LEN, HEAD_DIM), jnp.float32),
        "cmp_w1_k": dense((CMP_LEN * HEAD_DIM, CMP_HIDDEN), CMP_LEN * HEAD_DIM),
        "cmp_w2_k": dense((CMP_HIDDEN, HEAD_DIM), CMP_HIDDEN),
        "cmp_pos_v": 0.1 * jax.random.normal(next(ks), (DEPTH_2, CMP_LEN, HEAD_DIM), jnp.float32),
        "cmp_w1_v": dense((CMP_LEN * HEAD_DIM, CMP_HIDDEN), CMP_LEN * HEAD_DIM),
        "cmp_w2_v": dense((CMP_HIDDEN, HEAD_DIM), CMP_HIDDEN),
        "w_out": dense((MIX_WIDTH_2, D_MODEL), MIX_WIDTH_2),
        "mem_x_norm": gain(D_MODEL),
        "mem_kv_norm": gain(D_MODEL),
        "mem_wq": dense((D_MODEL, MEM_HEADS * HEAD_DIM), D_MODEL),
        "mem_wk": dense((D_MODEL, MEM_HEADS * HEAD_DIM), D_MODEL),
        "mem_wv": dense((D_MODEL, MEM_HEADS * HEAD_DIM), D_MODEL),
        "mem_q_norm": gain(HEAD_DIM),
        "mem_k_norm": gain(HEAD_DIM),
        "mem_wo": dense((MEM_HEADS * HEAD_DIM, D_MODEL), MEM_HEADS * HEAD_DIM),
        "ffn2_norm": gain(D_MODEL),
        "ffn2_wg": dense((D_MODEL, D_FF), D_MODEL),
        "ffn2_wu": dense((D_MODEL, D_FF), D_MODEL),
        "ffn2_wd": dense((D_FF, D_MODEL), D_FF),
    }

def second_block(x, mem, positions, ffn1_norm, ffn1_wg, ffn1_wu, ffn1_wd, mix_norm, w_in,
              nsa_q_norm, nsa_kc_norm, nsa_ks_norm, nsa_kw_norm,
              cmp_pos_k, cmp_w1_k, cmp_w2_k, cmp_pos_v, cmp_w1_v, cmp_w2_v, w_out,
              mem_x_norm, mem_kv_norm, mem_wq, mem_wk, mem_wv, mem_q_norm, mem_k_norm, mem_wo,
              ffn2_norm, ffn2_wg, ffn2_wu, ffn2_wd):
    split_at = [int(c) for c in np.cumsum(IN_SPLITS)[:-1]]
    for l in range(DEPTH_2):
        x = x + 0.5 * swiglu_2(rms_norm_2(x, ffn1_norm[l]), ffn1_wg[l], ffn1_wu[l], ffn1_wd[l])
        h = rms_norm_2(x, mix_norm[l])
        (q_n, kc, vc, ksl, vsl, kwn, vwn, gts, q_s, k_s, v_s) = jnp.split(h @ w_in[l], split_at, axis=-1)
        o_nsa = nsa_mixer(q_n, kc, vc, ksl, vsl, kwn, vwn, gts, positions,
                          cmp_pos_k[l], cmp_w1_k[l], cmp_w2_k[l], cmp_pos_v[l], cmp_w1_v[l], cmp_w2_v[l],
                          nsa_q_norm[l], nsa_kc_norm[l], nsa_ks_norm[l], nsa_kw_norm[l])
        o_sb = stick_breaking(q_s, k_s, v_s)
        x = x + jnp.concatenate([o_nsa, o_sb], axis=-1) @ w_out[l]
        x = x + memory_cross_attention(rms_norm_2(x, mem_x_norm[l]), rms_norm_2(mem, mem_kv_norm[l]),
                                       mem_wq[l], mem_wk[l], mem_wv[l], mem_wo[l],
                                       mem_q_norm[l], mem_k_norm[l])
        x = x + 0.5 * swiglu_2(rms_norm_2(x, ffn2_norm[l]), ffn2_wg[l], ffn2_wu[l], ffn2_wd[l])
    return x


def setup_inputs(seed=0):
    out = dict(first_inputs(seed))
    for name, value in second_inputs(seed + 1).items():
        if name != "x":
            out[name + "_2"] = value
    return out


def reference(
    x, c, ctx, c_ctx, ada_w, ada_b, norm_mix_g, norm_ffn_g, mix_in_w, mix_out_w, attn_sink,
    pool_w, pool_scale, ffn_w1, ffn_w3, ffn_w2, final_g, mem_2, positions_2, ffn1_norm_2,
    ffn1_wg_2, ffn1_wu_2, ffn1_wd_2, mix_norm_2, w_in_2, nsa_q_norm_2, nsa_kc_norm_2,
    nsa_ks_norm_2, nsa_kw_norm_2, cmp_pos_k_2, cmp_w1_k_2, cmp_w2_k_2, cmp_pos_v_2, cmp_w1_v_2,
    cmp_w2_v_2, w_out_2, mem_x_norm_2, mem_kv_norm_2, mem_wq_2, mem_wk_2, mem_wv_2,
    mem_q_norm_2, mem_k_norm_2, mem_wo_2, ffn2_norm_2, ffn2_wg_2, ffn2_wu_2, ffn2_wd_2,
):
    x = first_block(
        x, c, ctx, c_ctx, ada_w, ada_b, norm_mix_g, norm_ffn_g, mix_in_w, mix_out_w, attn_sink,
        pool_w, pool_scale, ffn_w1, ffn_w3, ffn_w2, final_g,
    )
    return second_block(
        x, mem_2, positions_2, ffn1_norm_2, ffn1_wg_2, ffn1_wu_2, ffn1_wd_2, mix_norm_2, w_in_2,
        nsa_q_norm_2, nsa_kc_norm_2, nsa_ks_norm_2, nsa_kw_norm_2, cmp_pos_k_2, cmp_w1_k_2,
        cmp_w2_k_2, cmp_pos_v_2, cmp_w1_v_2, cmp_w2_v_2, w_out_2, mem_x_norm_2, mem_kv_norm_2,
        mem_wq_2, mem_wk_2, mem_wv_2, mem_q_norm_2, mem_k_norm_2, mem_wo_2, ffn2_norm_2,
        ffn2_wg_2, ffn2_wu_2, ffn2_wd_2,
    )


_drawn_inputs = setup_inputs


def setup_inputs(seed=0):
    import zlib

    import numpy as np

    out = dict(_drawn_inputs(seed))
    spreads = {}
    factors = {'ctx': 3.263,
     'norm_mix_g': 3.261,
     'attn_sink': 64.0,
     'nsa_q_norm_2': 8.0,
     'nsa_kc_norm_2': 8.0,
     'nsa_ks_norm_2': 8.0,
     'nsa_kw_norm_2': 8.0,
     'cmp_pos_k_2': 8.0,
     'cmp_pos_v_2': 3.285,
     'mem_x_norm_2': 8.0,
     'mem_kv_norm_2': 8.0,
     'mem_q_norm_2': 8.0,
     'mem_k_norm_2': 8.0,
     'ffn2_norm_2': 3.237}
    for name, (base, spread) in spreads.items():
        noise = np.random.default_rng([zlib.crc32(name.encode()), seed]).standard_normal(out[name].shape)
        drawn = base * np.exp(spread * noise) if base else spread * noise
        out[name] = __import__('jax').numpy.asarray(drawn.astype(out[name].dtype))
    for name, factor in factors.items():
        out[name] = (out[name] * factor).astype(out[name].dtype)
    return out
```

```python
from contextlib import ExitStack

import numpy as np

import concourse.bass as bass
from concourse import mybir

ALU = mybir.AluOpType
ACT = mybir.ActivationFunctionType
AXX = mybir.AxisListType.X
F32 = mybir.dt.float32
F32R = mybir.dt.float32r
BF16 = mybir.dt.bfloat16
I32 = mybir.dt.int32

P = 128
T = 512
NC = 8
D = 1024
FF = 2816
NF = FF // P
LC = 256
NCMP = 31
SLOT = 2048
NEG = -1e30
EPS = 1e-6


class Tok:

    def __init__(self, sem, value=None):
        self.sem, self.value, self.used = sem, value, value is not None


class Queue:

    def __init__(self, sem):
        self.sem, self.ops, self.last = sem, [], None

    def __call__(self, fn, *after):
        tok = Tok(self.sem)
        need = []
        stack = list(after)
        while stack:
            x = stack.pop()
            if isinstance(x, Tok):
                x.used = True
                need.append(x)
            elif x:
                stack.extend(x)
        self.ops.append((fn, need, tok))
        self.last = tok
        return tok

    def number(self):
        n = 0
        for _, _, tok in self.ops:
            if tok.used and tok.value is None:
                n += 1
                tok.value = n

    def emit(self, eng):
        seen = {}
        for fn, need, tok in self.ops:
            most = {}
            for x in need:
                most[x.sem] = max(most.get(x.sem, 0), x.value)
            for sem, value in most.items():
                if seen.get(sem, 0) < value:
                    eng.wait_ge(sem, value)
                    seen[sem] = value
            ins = fn(eng)
            if tok.used and tok.sem is self.sem:
                ins.then_inc(self.sem, 1)


VEC = {}
_at = 0
for _n, _w in (("c", 8), ("cc", 8), ("ab0", 48), ("ab1", 48), ("gm0", 8), ("gm1", 8), ("gf0", 8), ("gf1", 8),
               ("pscale", 8), ("fin", 8), ("n1", 8), ("mixg", 8), ("memx", 8), ("memkv", 8), ("n2", 8),
               ("gq", 1), ("gkc", 1), ("gks", 1), ("gkw", 1), ("gmq", 1), ("gmk", 1), ("sink", 8),
               ("pek", 32), ("pev", 32)):
    VEC[_n] = (_at, _w)
    _at += _w
NVEC = _at

CST = {"ident": 0, "ones": 128, "bd": 256, "eps": 384, "one": 385, "freq": 386, "valid": 387, "zero": 388, "half": 389}
NCST = 390
BCS = {"ident": 0, "diag": 128, "prev": 256, "sbm": 384, "cmp": 512}
NBCS = 512 + 4 * 32
B1C = {"rot": 0, "cos": 128, "sin": 640, "cd": 1152, "cn": 1408, "sn": 1408 + 2048}
NB1C = 1408 + 4096
B2C = {"rot": 0, "tri": 128, "neg1": 256, "sb01": 384}
NB2C = 512


def program(nc, A, out):
    ctx = ExitStack()
    with ctx:
        def sem(name):
            return ctx.enter_context(nc.semaphore(name))

        V, S, G, M = (Queue(sem(n)) for n in ("s_vec", "s_act", "s_pool", "s_pe"))
        SP = Queue(sem("s_sp"))
        dsem = {}

        def load(q, key, dst, src, *after):
            if key not in dsem:
                dsem[key] = [sem("d_" + key), 0]
            s = dsem[key]
            s[1] += 16
            sm, val = s[0], s[1]
            last = q.last
            q(lambda e: e.dma_start(dst, src).then_inc(sm, 16), *after)
            q.last = last
            return Tok(sm, val)

        def sb(name, shape, dt=F32, stack=ctx):
            return stack.enter_context(nc.sbuf_tensor(name, shape, dt))

        ps = ctx.enter_context(nc.psum_tensor("ps", [P, 8 * 512], F32))
        pb = [ps[:, i * 512:(i + 1) * 512] for i in range(8)]
        bf = [[] for _ in range(8)]

        xT = sb("xT", [P, NC, T])
        xh = sb("xh", [P, NC, T], F32R)
        xl = sb("xl", [P, NC, T], F32R)
        raw = [sb(f"raw{i}", [P, SLOT]) for i in range(2)]
        wh = [sb(f"wh{i}", [P, SLOT], F32R) for i in range(2)]
        wl = [sb(f"wl{i}", [P, SLOT], F32R) for i in range(2)]
        acc = sb("acc", [P, 1024])
        vec = sb("vec", [P, NVEC])
        cst = sb("cst", [P, NCST])
        bcs = sb("bcs", [P, NBCS], BF16)
        ada = [sb("ada0", [P, 48]), sb("ada1", [P, 48])]
        adac = sb("adac", [P, 16])
        sc = sb("sc", [P, 16])
        cf = sb("cf", [P, 48])
        kmT = sb("kmT", [P, 2, LC])
        vm = sb("vm", [P, 2, LC])
        tmp = [sb(f"tmp{i}", [P, 512]) for i in range(4)]
        ssum = sb("ssum", [P, 512])
        sm = sb("sm", [P, 2, 16])
        free = {}

        ident = cst[:, 0:128]
        ones = cst[:, 128:256]
        bd = cst[:, 256:384]

        def v_(name, c=0, w=1):
            return vec[:, VEC[name][0] + c:VEC[name][0] + c + w]

        def k_(name):
            return cst[:, CST[name]:CST[name] + 1]

        def b_(name, w=128, o=0):
            return bcs[:, BCS[name] + o:BCS[name] + o + w]

        def fence():
            return [q.last for q in (V, S, G, M) if q.last]

        units = []

        def w_unit(src, kc, cols):
            units.append(("w", src, kc, cols))

        def w_cols(w, c0, cols, k0=0, kc=NC):
            w_unit(w[k0 * P:(k0 + kc) * P, c0:c0 + cols].rearrange("(k p) n -> p k n", p=P), kc, cols)

        ada_w = A["ada_w"]

        def ada_units(layer, j):
            for k in range(4):
                src = ada_w[layer, k * 256:(k + 1) * 256, j * 1024:(j + 1) * 1024]
                units.append(("ada", src.rearrange("(k p) n -> p k n", p=P), layer, j, k))

        w_cols(A["mem_wk_2"][0], 0, 256)
        w_cols(A["mem_wv_2"][0], 0, 256)
        ada_units(0, 0)
        ada_units(0, 1)
        for c in range(5):
            w_cols(A["mix_in_w"][0], c * 256, 256)
        ada_units(0, 2)
        for c in range(4):
            w_cols(A["mix_out_w"][0], c * 256, 256)
        ada_units(0, 3)
        ada_units(0, 4)
        ada_units(0, 5)

        def ffn_units(w1, w3, w2, extra=()):
            for g in range(NF // 2):
                w_cols(w1, g * 256, 256)
                w_cols(w3, g * 256, 256)
                if g < len(extra):
                    ada_units(*extra[g])
            for g in range(4):
                for k0, kc in ((0, 8), (8, 7), (15, 7)):
                    w_cols(w2, g * 256, 256, k0, kc)

        ffn_units(A["ffn_w1"][0], A["ffn_w3"][0], A["ffn_w2"][0], [(1, j) for j in range(6)])
        w_unit(A["pool_w"][0].rearrange("g (c p) n -> p (g c) n", p=P), 8, 256)
        ffn_units(A["ffn_w1"][1], A["ffn_w3"][1], A["ffn_w2"][1])
        ffn_units(A["ffn1_wg_2"][0], A["ffn1_wu_2"][0], A["ffn1_wd_2"][0])
        wi2 = A["w_in_2"][0]
        for c0, cols in ((0, 256), (256, 256), (512, 256)):
            w_cols(wi2, c0, cols)
        for k in range(2):
            w_cols(A["cmp_w1_k_2"][0], 0, 256, 8 * k)
        for k in range(2):
            w_cols(A["cmp_w1_v_2"][0], 0, 256, 8 * k)
        for c0, cols in ((768, 256), (1024, 128), (1152, 152), (1304, 256), (1560, 256), (1816, 256), (2072, 256),
                         (2328, 256), (2584, 256)):
            w_cols(wi2, c0, cols)
        for c in range(4):
            w_cols(A["w_out_2"][0], c * 256, 256)
        w_cols(A["mem_wq_2"][0], 0, 256)
        w_unit(A["mem_wo_2"][0].rearrange("(k p) n -> p k n", p=P), 2, 1024)
        ffn_units(A["ffn2_wg_2"][0], A["ffn2_wu_2"][0], A["ffn2_wd_2"][0])

        rawtok = {}
        rawfree = [[], []]
        ready = {}
        wdone = [[], []]
        st = {"dma": 0, "prep": 0, "w": 0, "use": 0}
        accdone = {"t": [], "a": [], "fin": []}
        adatok = {}
        worder = [i for i, u in enumerate(units) if u[0] == "w"]

        def dma_unit():
            u = st["dma"]
            if u >= len(units):
                return
            st["dma"] += 1
            src = units[u][1]
            kc, cols = src.shape[1], src.shape[2]
            dst = raw[u % 2][:, 0:kc * cols].rearrange("p (k n) -> p k n", k=kc)
            rawtok[u] = load(SP, f"raw{u % 2}", dst, src, rawfree[u % 2])

        accc = {}

        def prep_unit():
            u = st["prep"]
            st["prep"] += 1
            r = raw[u % 2]
            if units[u][0] == "w":
                _, _, kc, cols = units[u]
                n, s = kc * cols, st["w"] % 2
                st["w"] += 1
                hi, lo = wh[s][:, 0:n], wl[s][:, 0:n]
                a = S(lambda e: e.copy(hi, r[:, 0:n]), rawtok[u], wdone[s])
                b = V(lambda e: e.tensor_tensor(lo, r[:, 0:n], hi.bitcast(F32), ALU.subtract), a, wdone[s])
                ready[u] = (s, [a, b])
                rawfree[u % 2] = [a, b]
            else:
                _, _, layer, j, k = units[u]
                toks = []
                for kk in range(2):
                    kc = 2 * k + kk
                    w = r[:, kk * 1024:(kk + 1) * 1024]
                    for who, dst in (("c", acc),) + ((("cc", accc["t"]),) if layer == 0 and j < 2 else ()):
                        col = sc[:, kc + (8 if who == "cc" else 0):kc + 1 + (8 if who == "cc" else 0)]
                        key = (who, layer, j)
                        if kc == 0:
                            t = V(lambda e, dst=dst, w=w, col=col: e.tensor_scalar(dst[:, :], w, col, None, ALU.mult),
                                  rawtok[u], sctok, accdone["fin"])
                        else:
                            t = V(lambda e, dst=dst, w=w, col=col: e.scalar_tensor_tensor(
                                out=dst[:, :], in0=w, scalar=col, in1=dst[:, :], op0=ALU.mult, op1=ALU.add),
                                rawtok[u], adatok[key])
                        adatok[key] = t
                        toks.append(t)
                rawfree[u % 2] = toks
                if k == 3:
                    ada_finish(layer, j)
            dma_unit()

        def ada_finish(layer, j):
            done = []
            for who, src in (("c", acc),) + ((("cc", accc["t"]),) if layer == 0 and j < 2 else ()):
                bank = 7 if who == "c" else 6
                for c in range(8):
                    t = M(lambda e, c=c, src=src, bank=bank: e.matmul(
                        pb[bank][:, c:c + 1], src[:, c * P:(c + 1) * P], k_("one"), start=True, stop=True),
                        adatok[(who, layer, j)], bf[bank], ctok)
                done.append(t)
                dst = ada[layer] if who == "c" else adac
                bias = v_("ab1" if layer else "ab0", j * 8, 8)
                t2 = V(lambda e, dst=dst, bank=bank, bias=bias: e.tensor_tensor(
                    dst[:, j * 8:j * 8 + 8], pb[bank][:, 0:8], bias, ALU.add), t)
                bf[bank] = [t2]
                adatok[("m", who, layer, j)] = t2
            accdone["fin"] = done

        def w_next():
            u = worder[st["use"]]
            st["use"] += 1
            while st["prep"] <= u:
                prep_unit()
            s, toks = ready[u]
            kc, cols = units[u][2], units[u][3]
            hi = wh[s][:, 0:kc * cols].rearrange("p (k n) -> p k n", k=kc)
            lo = wl[s][:, 0:kc * cols].rearrange("p (k n) -> p k n", k=kc)

            def done(tok):
                wdone[s] = [tok]

            def ahead():
                if st["use"] < len(worder):
                    while st["prep"] <= worder[st["use"]]:
                        prep_unit()

            return hi, lo, toks, done, ahead

        def mm3(dst, ah, al, bh, bl, start, stop, *after, skip=False):
            M(lambda e: e.matmul(dst, ah, bh, start=start, stop=False, skip_group_check=skip), *after)
            M(lambda e: e.matmul(dst, ah, bl, start=False, stop=False, skip_group_check=skip))
            return M(lambda e: e.matmul(dst, al, bh, start=False, stop=stop, skip_group_check=skip))

        def proj(bank, hi, lo, col, toks, src_h, src_l, srctoks, nk=NC, k0=0, start=True, stop=True, n=T):
            t = None
            for k in range(nk):
                t = mm3(pb[bank][:, 0:n], hi[:, k, col:col + P], lo[:, k, col:col + P],
                        src_h[:, k0 + k, 0:n], src_l[:, k0 + k, 0:n],
                        start and k == 0, stop and k == nk - 1,
                        toks, srctoks(k0 + k), bf[bank] if start and k == 0 else None)
            return t

        def proj_tok(bank, hi, lo, c0, cols, toks, src_h, src_l, srctoks, tb, o=0):
            t = None
            for k in range(NC):
                sl = slice(tb * P, (tb + 1) * P)
                t = mm3(pb[bank][:, o:o + cols], src_h[:, k, sl], src_l[:, k, sl], hi[:, k, c0:c0 + cols],
                        lo[:, k, c0:c0 + cols], k == 0, k == NC - 1, toks, srctoks(k), bf[bank])
            return t

        def use(name, *toks):
            free[name] = list(toks)

        def was(name):
            return free.get(name, [])

        def square_in(c, src, n, after):
            if c == 0:
                t = S(lambda e: e.activation(ssum[:, 0:n], src, ACT.Square), after, was("ssum"))
            else:
                a = S(lambda e: e.activation(tmp[3][:, 0:n], src, ACT.Square), after, was("tmp3"))
                t = V(lambda e: e.tensor_tensor(ssum[:, 0:n], ssum[:, 0:n], tmp[3][:, 0:n], ALU.add), a, free["ss"])
                use("tmp3", t)
            free["ss"] = [t]
            return t

        def rstd_of(tok, n, bank=7):
            m = M(lambda e: e.matmul(pb[bank][:, 0:n], ones, ssum[:, 0:n], start=True, stop=True), tok, bf[bank], ctok)
            use("ssum", m)
            a = S(lambda e: e.activation(tmp[2][:, 0:n], pb[bank][:, 0:n], ACT.Sqrt, bias=k_("eps"), scale=1.0 / D),
                  m, was("tmp2"))
            bf[bank] = [a]
            return V(lambda e: e.reciprocal(tmp[2][:, 0:n], tmp[2][:, 0:n]), a)

        def norm(src, n, factor, shift, dh, dl, after, ftoks):
            r = rstd_of(free["ss"], n)
            toks = []
            for c in range(NC):
                i = c % 2
                t = V(lambda e, c=c, i=i: e.scalar_tensor_tensor(
                    out=tmp[i][:, 0:n], in0=src[:, c, 0:n], scalar=factor(c), in1=tmp[2][:, 0:n],
                    op0=ALU.mult, op1=ALU.mult), r, was(f"tmp{i}"), ftoks)
                if shift is None:
                    a = S(lambda e, c=c, i=i: e.copy(dh[:, c, 0:n], tmp[i][:, 0:n]), t, after)
                    b = V(lambda e, c=c, i=i: e.tensor_tensor(
                        dl[:, c, 0:n], tmp[i][:, 0:n], dh[:, c, 0:n].bitcast(F32), ALU.subtract), a)
                else:
                    a = S(lambda e, c=c, i=i: e.activation(dh[:, c, 0:n], tmp[i][:, 0:n], ACT.Identity,
                                                           bias=shift(c)), t, after)
                    b = V(lambda e, c=c, i=i: e.scalar_tensor_tensor(
                        out=dl[:, c, 0:n], in0=tmp[i][:, 0:n], scalar=shift(c), in1=dh[:, c, 0:n].bitcast(F32),
                        op0=ALU.add, op1=ALU.subtract), a)
                use(f"tmp{i}", a, b)
                toks.append([a, b])
            use("tmp2", t)
            return lambda k: toks[k]

        xtok = [None] * NC

        def residual(c, bank, coef, tok, ctoks, keep=True):
            t = V(lambda e: e.scalar_tensor_tensor(out=xT[:, c, :], in0=pb[bank][:, :], scalar=coef, in1=xT[:, c, :],
                                                   op0=ALU.mult, op1=ALU.add), tok, ctoks, xtok[c])
            bf[bank] = [t]
            xtok[c] = t
            if keep:
                square_in(c, xT[:, c, :], T, t)
            return t

        for name, dst, src in (("vec", vec, A["vecs"]), ("cst", cst, A["consts"])):
            load(SP, "c0", dst[:, :], src)
        ctok = [Tok(dsem["c0"][0], 32)]

        s0 = ExitStack()
        mh = sb("mh", [P, NC, LC], F32R, s0)
        ml = sb("ml", [P, NC, LC], F32R, s0)
        a1 = ExitStack()
        ctT = sb("ctT", [P, NC, LC], F32, a1)
        mmT = sb("mmT", [P, NC, LC], F32, a1)
        bst = sb("bst", [P, NBCS], F32, a1)
        accc["t"] = sb("accc", [P, 1024], F32, a1)
        mtok = load(SP, "mm", mmT[:, :, :], A["memT"].rearrange("(c p) t -> p c t", p=P))
        dma_unit()
        dma_unit()
        cttok = load(SP, "ct", ctT[:, :, :], A["ctxT"].rearrange("(c p) t -> p c t", p=P))
        xtk = load(SP, "x", xT[:, :, :], A["xT"].rearrange("(c p) t -> p c t", p=P))
        btok = load(SP, "bs", bst[:, :], A["masks"])
        for c in range(NC):
            xtok[c] = xtk

        sctok = [S(lambda e: e.activation(sc[:, :], vec[:, 0:16], ACT.Silu), ctok)]
        bctok = [V(lambda e: e.tensor_copy(bcs[:, :], bst[:, :]), btok)]

        for c in range(NC):
            square_in(c, mmT[:, c, :], LC, mtok)
        mt = norm(mmT, LC, lambda c: v_("memkv", c), None, mh, ml, [], ctok)

        def head_norm(src, srctok, gain, n, dst, scale, bank, after, i=0):
            a = S(lambda e: e.activation(tmp[i][:, 0:n], src, ACT.Square), srctok, was(f"tmp{i}"))
            m = M(lambda e: e.matmul(pb[bank][:, 0:n], bd, tmp[i][:, 0:n], start=True, stop=True), a, bf[bank])
            a2 = S(lambda e: e.activation(tmp[i][:, 0:n], pb[bank][:, 0:n], ACT.Sqrt, bias=k_("eps"), scale=1.0 / 64), m)
            bf[bank] = [a2]
            r = V(lambda e: e.reciprocal(tmp[i][:, 0:n], tmp[i][:, 0:n]), a2)
            t = V(lambda e: e.scalar_tensor_tensor(out=dst, in0=src, scalar=gain, in1=tmp[i][:, 0:n],
                                                   op0=ALU.mult, op1=ALU.mult), r, after)
            use(f"tmp{i}", t)
            return t

        hi, lo, wt, done, ahead = w_next()
        kmtok = []
        for c in range(2):
            t = proj(c, hi, lo, c * P, wt, mh, ml, mt, n=LC)
            a = S(lambda e, c=c: e.copy(kmT[:, c, :], pb[c][:, 0:LC]), t)
            bf[c] = [a]
            kmtok.append(head_norm(kmT[:, c, :], a, v_("gmk"), LC, kmT[:, c, :], None, 5, [], i=c))
        done(t)
        ahead()
        hi, lo, wt, done, ahead = w_next()
        vmtok = []
        for tb in range(2):
            t = proj_tok(2 + tb, hi, lo, 0, 256, wt, mh, ml, mt, tb)
            a = S(lambda e, tb=tb: e.copy(vm[:, tb, :], pb[2 + tb][:, 0:256]), t)
            bf[2 + tb] = [a]
            vmtok.append(a)
        done(t)
        memlast = t

        ahead()
        def factors(o, g, src, j, toks):
            return [V(lambda e: e.scalar_tensor_tensor(out=cf[:, o:o + 8], in0=src[:, j * 8:j * 8 + 8], scalar=1.0,
                                                       in1=g, op0=ALU.add, op1=ALU.mult), toks)]

        f0 = factors(0, v_("gm0", 0, 8), ada[0], 1, [adatok[("m", "c", 0, 1)], adatok[("m", "c", 0, 0)]])
        fc = factors(8, v_("gm0", 0, 8), adac, 1, [adatok[("m", "cc", 0, 1)], adatok[("m", "cc", 0, 0)]])
        for c in range(NC):
            square_in(c, ctT[:, c, :], LC, cttok)
        ct = norm(ctT, LC, lambda c: cf[:, 8 + c:9 + c], lambda c: adac[:, c:c + 1], mh, ml, [memlast], fc)
        for c in range(NC):
            square_in(c, xT[:, c, :], T, xtk)
        xt = norm(xT, T, lambda c: cf[:, c:c + 1], lambda c: ada[0][:, c:c + 1], xh, xl, [], f0)

        a1.close()
        a1 = ExitStack()
        b1c = sb("b1c", [P, NB1C], F32, a1)
        fT = sb("fT", [P, 4, T], F32, a1)
        qT = sb("qT", [P, 4, T], F32, a1)
        kT = sb("kT", [P, T], F32, a1)
        kTs = sb("kTs", [P, T], F32, a1)
        kcT = sb("kcT", [P, LC], F32, a1)
        kcTs = sb("kcTs", [P, LC], F32, a1)
        vt = sb("vt", [P, 4, 256], F32, a1)
        vct = sb("vct", [P, 2, 256], F32, a1)
        AB = sb("AB", [P, 4, 256], F32, a1)
        pr = sb("pr", [P, 2, 2, 640], F32, a1)
        pt = sb("pt", [P, 6, 256], F32, a1)
        b1tok = [load(G, "b1c", b1c[:, :], A["b1c"], fence())]

        def b1(name, w=128, o=0):
            return b1c[:, B1C[name] + o:B1C[name] + o + w]

        def rope(src, srctok, cos, sin, rot, scale, dst, bank, ctoks, after=(), n=T):
            m = M(lambda e: e.matmul(pb[bank][:, 0:n], rot, src, start=True, stop=True), srctok, bf[bank], ctoks)
            b = V(lambda e: e.scalar_tensor_tensor(out=tmp[1][:, 0:n], in0=pb[bank][:, 0:n], scalar=scale, in1=sin,
                                                   op0=ALU.mult, op1=ALU.mult), m, was("tmp1"), ctoks)
            bf[bank] = [b]
            a = V(lambda e: e.scalar_tensor_tensor(out=dst, in0=src, scalar=scale, in1=cos,
                                                   op0=ALU.mult, op1=ALU.mult), m, srctok, after)
            t = V(lambda e: e.tensor_tensor(dst, dst, tmp[1][:, 0:n], ALU.add), a, b)
            use("tmp1", t)
            return t

        def swap(dst, src, key, tok, after=()):
            load(G, key, dst[0:64], src[64:128], tok, after)
            return load(G, key, dst[64:128], src[0:64], tok, after)

        def twice(bank, o=0):
            return pb[bank][:, o:o + P].rearrange("p (j d) -> p j d", j=2).unsqueeze(2).broadcast_to([P, 2, 2, 64])

        def dup(dst):
            return dst.rearrange("p (j a d) -> p j a d", j=2, a=2)

        ft, qt = [], []
        for u in range(4):
            hi, lo, wt, done, ahead = w_next()
            for cc in range(2):
                c = 2 * u + cc
                t = proj(c % 2, hi, lo, cc * P, wt, xh, xl, xt)
                dst = fT[:, c, :] if c < 4 else qT[:, c - 4, :]
                a = S(lambda e, dst=dst, c=c: e.copy(dst, pb[c % 2]), t, b1tok)
                bf[c % 2] = [a]
                if c < 4:
                    ft.append(a)
                else:
                    qt.append(rope(dst, a, b1("cos", T), b1("sin", T), b1("rot"), 0.125, dst, 2, b1tok))
            done(t)
            ahead()
        hi, lo, wt, done, ahead = w_next()
        t = proj(0, hi, lo, 0, wt, xh, xl, xt)
        a = S(lambda e: e.copy(kT[:, :], pb[0]), t, b1tok)
        bf[0] = [a]
        kt = rope(kT[:, :], a, b1("cos", T), b1("sin", T), b1("rot"), 1.0, kT[:, :], 2, b1tok)
        kst = swap(kTs, kT, "kTs", kt)
        t = proj(1, hi, lo, 0, wt, mh, ml, ct, n=LC)
        kct = S(lambda e: e.copy(kcT[:, :], pb[1][:, 0:LC]), t)
        bf[1] = [kct]
        kcst = swap(kcTs, kcT, "kcTs", kct)
        vtt, vctt = [], []
        for tb in range(4):
            bank = 3 + tb % 2
            t = proj_tok(bank, hi, lo, P, P, wt, xh, xl, xt, tb)
            a = S(lambda e, tb=tb, bank=bank: e.copy(dup(vt[:, tb, :]), twice(bank)), t)
            bf[bank] = [a]
            vtt.append(a)
        for tb in range(2):
            bank = 3 + tb % 2
            t = proj_tok(bank, hi, lo, P, P, wt, mh, ml, ct, tb)
            a = S(lambda e, tb=tb, bank=bank: e.copy(dup(vct[:, tb, :]), twice(bank)), t)
            bf[bank] = [a]
            vctt.append(a)
        done(t)
        xlast = t
        ahead()

        mixt = [[] for _ in range(NC)]

        def put(bank, rows, cols, dst_h, dst_l, tok, c):
            a = S(lambda e: e.copy(dst_h, cols), tok, xlast)
            b = V(lambda e: e.tensor_tensor(dst_l, cols, dst_h.bitcast(F32), ALU.subtract), a)
            mixt[c] += [a, b]
            return [a, b]

        for c in range(4):
            abt = []
            for tb in range(4):
                bank = 5 + tb % 2
                m = M(lambda e, c=c, tb=tb, bank=bank: e.matmul(
                    pb[bank][:, 0:256], fT[:, c, tb * P:(tb + 1) * P], b1("cd", 256), start=True, stop=True),
                    ft[c], bf[bank], b1tok)
                w = V(lambda e, tb=tb, bank=bank: e.tensor_copy(AB[:, tb, :], pb[bank][:, 0:256]), m, was("AB"))
                bf[bank] = [w]
                abt.append(w)
            bank = c % 2
            for tb in range(4):
                for z, tab in ((0, "cn"), (1, "sn")):
                    m = M(lambda e, tb=tb, z=z, tab=tab, bank=bank: e.matmul(
                        pb[bank], AB[:, tb, z * P:(z + 1) * P], b1(tab, T, tb * T),
                        start=(tb == 0 and z == 0), stop=(tb == 3 and z == 1)),
                        abt[tb], bf[bank] if tb == 0 and z == 0 else None)
            use("AB", m)
            bf[bank] = put(bank, None, pb[bank], xh[:, c, :], xl[:, c, :], m, c)

        seq = {"n": 0, "pt": 0}

        def soft_a(nh, qk, masks, width, span, prob, after, sink=None, gate=None, gtok=(), valid=None, wide=False):
            par = seq["n"] % 2
            seq["n"] += 1
            nm, rs, es = sm[:, par, 0:nh], sm[:, par, 4:4 + nh], sm[:, par, 8:8 + nh]
            base = {}
            toks = []
            for g in range(nh):
                o = span(g)
                banks = sorted({o // 512, (o + width - 1) // 512})
                t = None
                for q, k, col, w in qk(g):
                    mk = [x for x in masks if x[0] == col]
                    t = M(lambda e, q=q, k=k, a=o + col, w=w, mk=mk: e.matmul(
                        ps[:, a:a + w], q, k, start=True, stop=not mk, skip_group_check=True),
                        after, [bf[b] for b in banks])
                    for col2, w2, mask in mk:
                        t = M(lambda e, a=o + col2, w=w2, mask=mask: e.matmul(
                            ps[:, a:a + w], b_("ident"), mask, start=False, stop=True, skip_group_check=True), bctok)
                toks.append((t, banks, o))
            red = []
            for g in range(nh):
                t, banks, o = toks[g]
                red.append(V(lambda e, g=g, o=o: e.tensor_reduce(nm[:, g:g + 1], ps[:, o:o + width], AXX, ALU.max,
                                                                 negate=sink is None), t, was(f"sm{par}")))
            if sink is not None:
                red = [V(lambda e: e.tensor_tensor(nm, nm, sink, ALU.max), red)]
                red = [V(lambda e: e.tensor_scalar(nm, nm, -1.0, None, ALU.mult), red)]
            ex = []
            for g in range(nh):
                t, banks, o = toks[g]
                a = S(lambda e, g=g, o=o: e.activation(prob[:, g, 0:width], ps[:, o:o + width], ACT.Exp,
                                                       bias=nm[:, g:g + 1], accum_out=rs[:, g:g + 1]),
                      red, was(f"prob{par}"))
                for b in banks:
                    bf[b] = [x for x in bf[b] if x in ex] + [a]
                ex.append(a)
            last = ex
            if sink is not None:
                d = V(lambda e: e.tensor_tensor(es, sink, nm, ALU.add), red)
                d = S(lambda e: e.activation(es, es, ACT.Exp), d)
                last = [V(lambda e: e.tensor_tensor(rs, rs, es, ALU.add), d, ex)]
            r = V(lambda e: e.reciprocal(rs, rs), last)
            if gate is not None:
                r = V(lambda e: e.tensor_tensor(rs, rs, gate, ALU.mult), r, gtok)
            if valid is not None:
                r = V(lambda e: e.tensor_scalar(rs, rs, valid, None, ALU.mult), r)
            out = []
            for g in range(nh):
                out.append(V(lambda e, g=g: e.tensor_scalar(prob[:, g, 0:width], prob[:, g, 0:width], rs[:, g:g + 1],
                                                            None, ALU.mult), r))
            use(f"sm{par}", *out)
            return par, out

        def soft_b(nh, prob, ptok, par, blocks, ptile, obank, first, last, pbanks=(4, 5)):
            per = max(1, 4 // nh)
            t = None
            evs = []
            for b0 in range(0, len(blocks), per):
                grp = blocks[b0:b0 + per]
                bank = pbanks[seq["pt"] % len(pbanks)]
                for bi, (col, w, v, vtk) in enumerate(grp):
                    for g in range(nh):
                        o = (bi * nh + g) * P
                        t = M(lambda e, o=o, g=g, col=col, w=w, bank=bank: e.transpose(
                            pb[bank][0:w, o:o + P], prob[:, g, col:col + w], ident), ptok, bf[bank], ctok)
                w = grp[0][1]
                n = len(grp) * nh * P
                dst = ptile[0:w, b0 * nh * P:b0 * nh * P + n]
                if seq["pt"] % 2:
                    ev = V(lambda e, dst=dst, bank=bank, w=w, n=n: e.tensor_copy(dst, pb[bank][0:w, 0:n]), t, was("pt"))
                else:
                    ev = S(lambda e, dst=dst, bank=bank, w=w, n=n: e.copy(dst, pb[bank][0:w, 0:n]), t, was("pt"))
                bf[bank] = [ev]
                seq["pt"] += 1
                evs += [ev] * len(grp)
            use(f"prob{par}", t)
            for bi, (col, w, v, vtk) in enumerate(blocks):
                t = M(lambda e, bi=bi, v=v, w=w: e.matmul(
                    pb[obank][:, 0:nh * P], v, ptile[0:w, bi * nh * P:(bi + 1) * nh * P],
                    start=first and bi == 0, stop=last and bi == len(blocks) - 1),
                    evs[bi], vtk, bf[obank] if first and bi == 0 else None)
            use("pt", t)
            return t

        def first_attention():
            jobs = [(i, j, h2) for i in range(4) for j in range(2) for h2 in range(2)]

            def a_stage(i, j, h2):
                nb = [b for b in (i - 1, i, i + 1) if 0 <= b < 4]
                width = len(nb) * P + LC
                off = 512 - len(nb) * P

                def qk(g):
                    h = 4 * j + 2 * h2 + g
                    r = slice((h % 2) * 64, (h % 2) * 64 + 64)
                    kk, kc_ = (kT, kcT) if h % 2 == j else (kTs, kcTs)
                    q = qT[r, h // 2, i * P:(i + 1) * P]
                    return [(q, kk[r, b * P:(b + 1) * P], n * P, P) for n, b in enumerate(nb)] + \
                        [(q, kc_[r, :], len(nb) * P, LC)]

                masks = [(n * P, P, b_("prev") if b < i else b_("diag"))
                         for n, b in enumerate(nb) if b != i]
                par = seq["n"] % 2
                sink = v_("sink", 4 * j + 2 * h2, 2)
                par, tok = soft_a(2, qk, masks, width, lambda g: g * 1024 + off, pr[:, par, :, :],
                                  [qt, kt, kst, kct, kcst], sink=sink)
                return par, tok, nb, width

            def b_stage(n, i, j, h2, par, tok, nb, width):
                vs = [(m * P, P, vt[:, b, j * P:(j + 1) * P], vtt[b]) for m, b in enumerate(nb)]
                vs += [((len(nb) + m) * P, P, vct[:, m, j * P:(j + 1) * P], vctt[m]) for m in range(2)]
                ob = 6 + n % 2
                t = soft_b(2, pr[:, par, :, :], tok, par, vs, pt[:, :, :].rearrange("p a b -> p (a b)"), ob, True, True)
                last = []
                for g in range(2):
                    c = 4 + (4 * j + 2 * h2) // 2
                    r = slice(g * 64, g * 64 + 64)
                    cols = slice(i * P, (i + 1) * P)
                    last += put(ob, r, pb[ob][r, g * P:(g + 1) * P], xh[r, c, cols], xl[r, c, cols], t, c)
                bf[ob] = last

            prev = None
            for n, job in enumerate(jobs):
                cur = (n, *job, *a_stage(*job))
                if prev:
                    b_stage(*prev)
                prev = cur
            b_stage(*prev)

        first_attention()

        def mix_out(coef, ctoks):
            for u in range(4):
                hi, lo, wt, done, ahead = w_next()
                for cc in range(2):
                    c = 2 * u + cc
                    t = proj(c % 2, hi, lo, cc * P, wt, xh, xl, lambda k: mixt[k])
                    residual(c, c % 2, coef(c), t, ctoks)
                done(t)
                ahead()
            return t

        mix_out(lambda c: ada[0][:, 16 + c:17 + c], adatok[("m", "c", 0, 2)])
        a1.close()
        s0.close()

        names = {"n": 0}

        def ffn(coef, ctoks, xtoks, arena, keep=True, final=None):
            names["n"] += 1
            hst = ExitStack()
            hh = sb(f"hh{names['n']}", [P, NF, T], F32R, hst)
            hl = sb(f"hl{names['n']}", [P, NF, T], F32R, hst)
            ht = []
            for g in range(NF // 2):
                hi, lo, wt, done, ahead = w_next()
                sg = []
                for cc in range(2):
                    t = proj(cc, hi, lo, cc * P, wt, xh, xl, xtoks)
                    sg.append(S(lambda e, cc=cc: e.activation(tmp[cc][:, :], pb[cc], ACT.Silu), t, was(f"tmp{cc}")))
                    bf[cc] = [sg[-1]]
                done(t)
                ahead()
                hi, lo, wt, done, ahead = w_next()
                for cc in range(2):
                    f = 2 * g + cc
                    t = proj(2 + cc, hi, lo, cc * P, wt, xh, xl, xtoks)
                    m = V(lambda e, cc=cc: e.tensor_tensor(tmp[cc][:, :], pb[2 + cc], tmp[cc][:, :], ALU.mult), t, sg[cc])
                    bf[2 + cc] = [m]
                    a = S(lambda e, f=f, cc=cc: e.copy(hh[:, f, :], tmp[cc][:, :]), m, arena)
                    b = V(lambda e, f=f, cc=cc: e.tensor_tensor(hl[:, f, :], tmp[cc][:, :], hh[:, f, :].bitcast(F32),
                                                                ALU.subtract), a)
                    use(f"tmp{cc}", a, b)
                    ht.append([a, b])
                done(t)
                ahead()
            for g in range(4):
                b0 = 2 * (g % 2)
                for k0, kc in ((0, 8), (8, 7), (15, 7)):
                    hi, lo, wt, done, ahead = w_next()
                    for cc in range(2):
                        t = proj(b0 + cc, hi, lo, cc * P, wt, hh, hl, lambda k: ht[k], kc, k0, k0 == 0, k0 + kc == NF)
                        if k0 + kc == NF:
                            r = residual(2 * g + cc, b0 + cc, coef(2 * g + cc), t, ctoks, keep)
                            if final:
                                final(2 * g + cc, r)
                    done(t)
                    ahead()
            hst.close()
            return t

        f1 = factors(16, v_("gf0", 0, 8), ada[0], 4, [adatok[("m", "c", 0, 4)], adatok[("m", "c", 0, 3)]])
        xn = norm(xT, T, lambda c: cf[:, 16 + c:17 + c], lambda c: ada[0][:, 24 + c:25 + c], xh, xl, fence(), f1)
        ffn(lambda c: ada[0][:, 40 + c:41 + c], adatok[("m", "c", 0, 5)], xn, fence())

        pst = ExitStack()
        xp = sb("xp", [P, NC, T + 16], F32, pst)
        sa = sb("sa", [P, 2, T + 16], F32, pst)
        icnt = sb("icnt", [P, 4, T], F32, pst)
        f2 = factors(24, v_("gm1", 0, 8), ada[1], 1, [adatok[("m", "c", 1, 1)], adatok[("m", "c", 1, 0)]])
        f2g = [V(lambda e: e.tensor_tensor(cf[:, 40:48], ada[1][:, 16:24], v_("pscale", 0, 8), ALU.mult),
                 adatok[("m", "c", 1, 2)])]
        after = fence()
        ictok = load(G, "icnt", icnt[:, :, :], A["icnt"], after)
        z = [G(lambda e: e.memset(xp[:, :, 0:8], 0.0), after), G(lambda e: e.memset(xp[:, :, T + 8:T + 16], 0.0), after)]
        r = rstd_of(free["ss"], T)
        pooled = []
        for c in range(NC):
            i = c % 2
            g = c // 2
            w = 2 << g
            t = V(lambda e, c=c, i=i: e.scalar_tensor_tensor(out=tmp[i][:, :], in0=xT[:, c, :], scalar=cf[:, 24 + c:25 + c],
                                                             in1=tmp[2][:, :], op0=ALU.mult, op1=ALU.mult),
                  r, was(f"tmp{i}"), f2)
            x_ = xp[:, c, :]
            a = S(lambda e, c=c, i=i: e.activation(xp[:, c, 8:T + 8], tmp[i][:, :], ACT.Identity,
                                                   bias=ada[1][:, c:c + 1]), t, after)
            use(f"tmp{i}", a)
            src, at, t, width = xp[:, c, :], 0, [a, z], 1
            step = 0
            while width < w:
                dst = sa[:, step % 2, :]
                n = T + 16 - 2 * width + 1
                t = [V(lambda e, src=src, dst=dst, width=width: e.tensor_tensor(
                    dst[:, 0:T + 17 - 2 * width], src[:, 0:T + 17 - 2 * width], src[:, width:T + 17 - width], ALU.add),
                    t, was(f"sa{step % 2}"), after)]
                src = dst
                width *= 2
                step += 1
            o = 8 - w // 2
            t = V(lambda e, src=src, o=o, g=g, i=i: e.tensor_tensor(tmp[i][:, :], src[:, o:o + T], icnt[:, g, :], ALU.mult),
                  t, ictok, was(f"tmp{i}"))
            use("sa0", t)
            use("sa1", t)
            t = V(lambda e, c=c, i=i: e.tensor_tensor(tmp[i][:, :], tmp[i][:, :], xp[:, c, 8:T + 8], ALU.subtract), t)
            a = S(lambda e, c=c, i=i: e.copy(xh[:, c, :], tmp[i][:, :]), t, after)
            b = V(lambda e, c=c, i=i: e.tensor_tensor(xl[:, c, :], tmp[i][:, :], xh[:, c, :].bitcast(F32), ALU.subtract), a)
            use(f"tmp{i}", a, b)
            pooled.append([a, b])
        use("tmp2", t)
        hi, lo, wt, done, ahead = w_next()
        for c in range(NC):
            g = c // 2
            bank = c % 4
            for k in range(2):
                t = mm3(pb[bank], hi[:, 2 * g + k, (c % 2) * P:(c % 2 + 1) * P], lo[:, 2 * g + k, (c % 2) * P:(c % 2 + 1) * P],
                        xh[:, 2 * g + k, :], xl[:, 2 * g + k, :], k == 0, k == 1, wt, pooled[2 * g + k],
                        bf[bank] if k == 0 else None)
            residual(c, bank, cf[:, 40 + c:41 + c], t, f2g)
        done(t)
        ahead()
        pst.close()
        f3 = factors(32, v_("gf1", 0, 8), ada[1], 4, [adatok[("m", "c", 1, 4)], adatok[("m", "c", 1, 3)]])
        xn = norm(xT, T, lambda c: cf[:, 32 + c:33 + c], lambda c: ada[1][:, 24 + c:25 + c], xh, xl, fence(), f3)
        ffn(lambda c: ada[1][:, 40 + c:41 + c], adatok[("m", "c", 1, 5)], xn, fence())

        r = rstd_of(free["ss"], T)
        for c in range(NC):
            xtok[c] = V(lambda e, c=c: e.scalar_tensor_tensor(out=xT[:, c, :], in0=xT[:, c, :], scalar=v_("fin", c),
                                                              in1=tmp[2][:, :], op0=ALU.mult, op1=ALU.mult), r, xtok[c])
            square_in(c, xT[:, c, :], T, xtok[c])
        use("tmp2", xtok[NC - 1])

        xn = norm(xT, T, lambda c: v_("n1", c), None, xh, xl, fence(), ctok)
        ffn(lambda c: k_("half"), ctok, xn, fence())

        n2 = ExitStack()
        b2c = sb("b2c", [P, NB2C], F32, n2)
        C2 = sb("C2", [P, T], F32, n2)
        S2 = sb("S2", [P, T], F32, n2)
        q2 = sb("q2", [P, 4, T], F32, n2)
        ksT = sb("ksT", [P, 2, T], F32, n2)
        kwT = sb("kwT", [P, 2, T], F32, n2)
        v2s = sb("v2s", [P, 4, 256], F32, n2)
        v2w = sb("v2w", [P, 4, 256], F32, n2)
        gts = sb("gts", [P, 4, 24], F32, n2)
        qsT = sb("qsT", [P, 4, T], F32, n2)
        ksbT = sb("ksbT", [P, 4, T], F32, n2)
        vsb = sb("vsb", [P, 4, T], F32, n2)
        kcC = sb("kcC", [P, 2 * NCMP], F32, n2)
        vcC = sb("vcC", [32, 256], F32, n2)
        w2c = sb("w2c", [P, 2, 2, P], F32, n2)
        hid = sb("hid", [P, 2, 2 * NCMP], F32, n2)
        n3 = ExitStack()
        kcr = sb("kcr", [P, 2, T], F32, n3)
        kb = sb("kb", [P, 16, 2 * NCMP], F32, n3)
        kbh = sb("kbh", [P, 16, 2 * NCMP], F32R, n3)
        kbl = sb("kbl", [P, 16, 2 * NCMP], F32R, n3)
        after2 = fence()
        b2tok = [load(G, "b2c", b2c[:, :], A["b2c"], after2)]
        w2tok = []
        for z, name in ((0, "cmp_w2_k_2"), (1, "cmp_w2_v_2")):
            for y in range(2):
                w2tok = [load(G, "w2c", w2c[:, z, :, y * 64:(y + 1) * 64],
                              A[name][0].rearrange("(c p) n -> p c n", p=P), after2)]

        def b2(name, w=128):
            return b2c[:, B2C[name]:B2C[name] + w]

        posi = kb[:, :, :].rearrange("p a b -> p (a b)")[:, 0:T].bitcast(I32)
        ang = kcr[:, 0, :]
        ni = kcr[:, 1, :].bitcast(I32)
        nf = C2[:, :]
        t = load(G, "pos", posi, A["positions_2"].partition_broadcast(P).rearrange("p a t -> p (a t)"), after2)
        t = V(lambda e: e.tensor_copy(ang, posi), t, after2)
        t = V(lambda e: e.tensor_scalar(ang, ang, k_("freq"), None, ALU.mult), t)
        for parts in turns():
            t = V(lambda e, parts=parts: e.tensor_scalar(ni, ang, float(parts[0]), None, ALU.mult), t)
            t = V(lambda e: e.tensor_copy(nf, ni), t)
            for p in parts[1:]:
                t = V(lambda e, p=p: e.scalar_tensor_tensor(out=ang, in0=nf, scalar=-float(p), in1=ang,
                                                            op0=ALU.mult, op1=ALU.add), t)
        pi = float(np.float32(3.1415925))
        t = V(lambda e: e.tensor_scalar(ang, ang, pi, -pi, ALU.min, ALU.max), t)
        s2t = S(lambda e: e.activation(S2[:, :], ang, ACT.Sin), t)
        t = V(lambda e: e.tensor_scalar(C2[:, :], ang, float(np.pi / 2), None, ALU.add), t)
        t = V(lambda e: e.tensor_scalar(kcr[:, 1, :], C2[:, :], pi, float(-2 * np.pi), ALU.is_gt, ALU.mult), t)
        t = V(lambda e: e.tensor_tensor(C2[:, :], C2[:, :], kcr[:, 1, :], ALU.add), t)
        t = V(lambda e: e.tensor_scalar(C2[:, :], C2[:, :], pi, -pi, ALU.min, ALU.max), t, s2t)
        c2t = S(lambda e: e.activation(C2[:, :], C2[:, :], ACT.Sin), t)
        cst2 = [s2t, c2t]

        xn = norm(xT, T, lambda c: v_("mixg", c), None, xh, xl, after2, ctok)

        def qk_chunk(bank, tok, gain, scale, dst, n=T, cos=None, sin=None):
            a = S(lambda e: e.copy(dst, pb[bank][:, 0:n]), tok, after2)
            bf[bank] = [a]
            t = head_norm(dst, a, gain, n, dst, None, 4, [])
            return rope(dst, t, C2[:, :] if cos is None else cos, S2[:, :] if sin is None else sin, b2("rot"), scale,
                        dst, 5, [b2tok, cst2], n=n)

        q2t = []
        for u in range(2):
            hi, lo, wt, done, ahead = w_next()
            for cc in range(2):
                c = 2 * u + cc
                t = proj(c % 2, hi, lo, cc * P, wt, xh, xl, xn)
                q2t.append(qk_chunk(c % 2, t, v_("gq"), 0.125, q2[:, c, :]))
            done(t)
            ahead()
        hi, lo, wt, done, ahead = w_next()
        kcrt = []
        for z in range(2):
            t = proj(z, hi, lo, z * P, wt, xh, xl, xn)
            a = S(lambda e, z=z: e.copy(kcr[:, z, :], pb[z]), t, cst2)
            bf[z] = [a]
            kcrt.append(a)
        done(t)
        ahead()
        for z in range(2):
            bt = []
            for j in range(2):
                rows = slice(j * 64, (j + 1) * 64)
                for par in range(2):
                    for hh_ in range(2):
                        src = kcr[rows, z, hh_ * 16:hh_ * 16 + 496].rearrange("p (n l two) -> p two l n", n=NCMP, two=2)
                        o = VEC["pev" if z else "pek"][0] + par * 16 + hh_ * 8
                        pe = vec[rows, o:o + 8].unsqueeze(2).broadcast_to([64, 8, NCMP])
                        dst = kb[par * 64:(par + 1) * 64, hh_ * 8:hh_ * 8 + 8, j * NCMP:(j + 1) * NCMP]
                        bt.append(V(lambda e, dst=dst, src=src, par=par, pe=pe: e.tensor_tensor(dst, src[:, par], pe, ALU.add),
                                    kcrt[z], was("kb"), cst2))
            a = S(lambda e: e.copy(kbh[:, :, :], kb[:, :, :]), bt, was("kbh"))
            b = V(lambda e: e.tensor_tensor(kbl[:, :, :], kb[:, :, :], kbh[:, :, :].bitcast(F32), ALU.subtract), a, was("kbh"))
            use("kb", a, b)
            for u in range(2):
                hi, lo, wt, done, ahead = w_next()
                for f in range(2):
                    for k in range(8):
                        t = mm3(pb[2 + f][:, 0:2 * NCMP], hi[:, k, f * P:(f + 1) * P], lo[:, k, f * P:(f + 1) * P],
                                kbh[:, 8 * u + k, :], kbl[:, 8 * u + k, :], u == 0 and k == 0, u == 1 and k == 7,
                                wt, [a, b], bf[2 + f] if u == 0 and k == 0 else None)
                done(t)
                ahead()
            use("kbh", t)
            ge = []
            for f in range(2):
                x = S(lambda e, f=f: e.activation(hid[:, f, :], pb[2 + f][:, 0:2 * NCMP], ACT.Gelu_apprx_tanh), t,
                      was("hid"), after2)
                bf[2 + f] = [x]
                ge.append(x)
            if z == 0:
                for f in range(2):
                    m = M(lambda e, f=f: e.matmul(pb[6][:, 0:2 * NCMP], w2c[:, 0, f, :], hid[:, f, :], start=f == 0,
                                                  stop=f == 1), ge, w2tok, bf[6])
                use("hid", m)
                x = S(lambda e: e.copy(kcC[:, :], pb[6][:, 0:2 * NCMP]), m)
                bf[6] = [x]
                x = head_norm(kcC[:, :], x, v_("gkc"), 2 * NCMP, kcC[:, :], None, 4, [])
                kct2 = [rope(kcC[:, j * NCMP:(j + 1) * NCMP], x, C2[:, 31:T:16], S2[:, 31:T:16], b2("rot"), 1.0,
                             kcC[:, j * NCMP:(j + 1) * NCMP], 5, [b2tok, cst2], n=NCMP) for j in range(2)]
            else:
                vct2 = []
                for j in range(2):
                    for f in range(2):
                        m = M(lambda e, f=f, j=j: e.matmul(pb[6][0:NCMP, j * P:(j + 1) * P], hid[:, f, j * NCMP:(j + 1) * NCMP],
                                                           w2c[:, 1, f, :], start=f == 0, stop=f == 1), ge, w2tok, bf[6])
                vct2 = [S(lambda e: e.copy(vcC[0:NCMP, :], pb[6][0:NCMP, 0:256]), m)]
                bf[6] = vct2

        hi, lo, wt, done, ahead = w_next()
        t = proj(0, hi, lo, 0, wt, xh, xl, xn)
        kst2 = qk_chunk(0, t, v_("gks"), 1.0, ksT[:, 0, :])
        kst2 = [kst2, swap(ksT[:, 1, :], ksT[:, 0, :], "ksT", kst2)]

        def tok_v(dst, c0):
            toks = []
            for tb in range(4):
                bank = 2 + tb % 2
                t = proj_tok(bank, hi, lo, c0, P, wt, xh, xl, xn, tb)
                a = S(lambda e, tb=tb, bank=bank: e.copy(dup(dst[:, tb, :]), twice(bank)), t, after2)
                bf[bank] = [a]
                toks.append(a)
            return toks, t

        v2st, t = tok_v(v2s, P)
        done(t)
        ahead()
        hi, lo, wt, done, ahead = w_next()
        t = proj(0, hi, lo, 0, wt, xh, xl, xn)
        done(t)
        kwt2 = qk_chunk(0, t, v_("gkw"), 1.0, kwT[:, 0, :])
        kwt2 = [kwt2, swap(kwT[:, 1, :], kwT[:, 0, :], "kwT", kwt2)]
        ahead()
        hi, lo, wt, done, ahead = w_next()
        v2wt, t = tok_v(v2w, 0)
        gtt = []
        for tb in range(4):
            t = proj_tok(6, hi, lo, P, 24, wt, xh, xl, xn, tb, tb * 24)
        gtt = [S(lambda e: e.activation(gts[:, :, :], pb[6][:, 0:96].rearrange("p (a b) -> p a b", a=4), ACT.Sigmoid), t, after2)]
        bf[6] = gtt
        done(t)
        ahead()
        qst, ksbt = [], []
        for u in range(4):
            hi, lo, wt, done, ahead = w_next()
            for cc in range(2):
                c = 2 * (u % 2) + cc
                t = proj(cc, hi, lo, cc * P, wt, xh, xl, xn)
                if u < 2:
                    a = S(lambda e, c=c, cc=cc: e.mul(qsT[:, c, :], pb[cc], 0.125), t, after2)
                    qst.append(a)
                else:
                    a = S(lambda e, c=c, cc=cc: e.copy(ksbT[:, c, :], pb[cc]), t, after2)
                    ksbt.append(a)
                bf[cc] = [a]
            done(t)
            ahead()
        vsbt = []
        for u in range(2):
            hi, lo, wt, done, ahead = w_next()
            for tb in range(4):
                bank = 2 + tb % 2
                t = proj_tok(bank, hi, lo, 0, 256, wt, xh, xl, xn, tb)
                a = S(lambda e, tb=tb, bank=bank, u=u: e.copy(vsb[:, tb, u * 256:(u + 1) * 256], pb[bank][:, 0:256]), t, after2)
                bf[bank] = [a]
                vsbt.append(a)
            done(t)
            ahead()
        xlast = t
        n3.close()
        n3 = ExitStack()
        pr2 = sb("pr2", [P, 2, 4, T], F32, n3)
        pt2 = sb("pt2", [P, 4 * T], F32, n3)
        after3 = fence()
        use("prob0", *after3)
        use("prob1", *after3)
        use("pt", *after3)
        mixt = [[] for _ in range(NC)]

        def nsa():
            jobs = [(i, j, br) for i in range(4) for j in range(2) for br in range(3)]

            def a_stage(i, j, br):
                par = seq["n"] % 2
                width = NCMP if br == 0 else (i + 1) * P

                def qk(g):
                    h = 4 * j + g
                    r = slice((h % 2) * 64, (h % 2) * 64 + 64)
                    q = q2[r, h // 2, i * P:(i + 1) * P]
                    if br == 0:
                        return [(q, kcC[r, j * NCMP:(j + 1) * NCMP], 0, NCMP)]
                    kk = ksT if br == 1 else kwT
                    sw = 0 if h % 2 == j else 1
                    full = [(q, kk[r, sw, 0:i * P], 0, i * P)] if i else []
                    return full + [(q, kk[r, sw, i * P:(i + 1) * P], i * P, P)]

                masks = [(0, NCMP, b_("cmp", NCMP, 32 * i))] if br == 0 else [(i * P, P, b_("diag"))]
                gate = gts[:, i, :].rearrange("p (j g b) -> p j b g", j=2, g=4)[:, j, br]
                return soft_a(4, qk, masks, width, lambda g: g * 512, pr2[:, par, :, :],
                              [q2t, kct2, kst2, kwt2], gate=gate, gtok=gtt,
                              valid=k_("valid") if br == 0 and i == 0 else None)

            def b_stage(i, j, br, par, tok):
                if br == 0:
                    vs = [(0, NCMP, vcC[0:NCMP, j * P:(j + 1) * P], vct2)]
                else:
                    v, vtk = (v2s, v2st) if br == 1 else (v2w, v2wt)
                    vs = [(b * P, P, v[:, b, j * P:(j + 1) * P], vtk[b]) for b in range(i + 1)]
                ob = 6 + (2 * i + j) % 2
                t = soft_b(4, pr2[:, par, :, :], tok, par, vs, pt2[:, :], ob, br == 0, br == 2)
                if br == 2:
                    last = []
                    for o in range(2):
                        r = slice(o * 64, o * 64 + 64)
                        cols = slice(i * P, (i + 1) * P)
                        src = pb[ob][r, :].rearrange("p (a o q) -> p o a q", o=2, q=P)[:, o]
                        tk = put(ob, r, src, xh[r, 2 * j:2 * j + 2, cols], xl[r, 2 * j:2 * j + 2, cols], t, 2 * j)
                        mixt[2 * j + 1] += tk
                        last += tk
                    bf[ob] = last

            prev = None
            for job in jobs:
                cur = (*job, *a_stage(*job))
                if prev:
                    b_stage(*prev)
                prev = cur
            b_stage(*prev)

        nsa()
        n3.close()
        n3 = ExitStack()
        ze = sb("ze", [P, 1536], F32, n3)
        zs = sb("zs", [P, 2, 1536], F32, n3)
        za = sb("za", [P, 2, 1536], F32, n3)
        after4 = fence()
        ZC = [0, 512, 1024, 896]
        ZW = [512, 384, 256, 128]

        def stick():
            def a_stage(h):
                base = 3 * (h % 2)
                r = slice((h % 2) * 64, (h % 2) * 64 + 64)
                c = h // 2
                zo = base * 512
                banks = [base, base + 1, base + 2]
                lastm = None
                for b in range(4):
                    lastm = M(lambda e, b=b: e.matmul(
                        ps[:, zo + ZC[b]:zo + ZC[b] + ZW[b]], ksbT[r, c, b * P:(b + 1) * P], qsT[r, c, b * P:T],
                        start=b < 3, stop=False, skip_group_check=True), qst, ksbt, [bf[x] for x in banks])
                zz = ps[:, zo:zo + 1280]
                par = h % 2
                e1 = S(lambda e: e.activation(ze[:, 0:1280], zz, ACT.Abs), lastm, was("ze"), after4)
                e1 = S(lambda e: e.activation(ze[:, 0:1280], ze[:, 0:1280], ACT.Exp, scale=-1.0), e1)
                e1 = S(lambda e: e.activation(ze[:, 0:1280], ze[:, 0:1280], ACT.Ln, bias=k_("one")), e1)
                s_ = V(lambda e: e.scalar_tensor_tensor(out=zs[:, par, 0:1280], in0=zz, scalar=0.0, in1=ze[:, 0:1280],
                                                        op0=ALU.max, op1=ALU.add), e1, was(f"zs{par}"), after4)
                use("ze", s_)
                ms = []
                for b in range(4):
                    ms.append(V(lambda e, b=b: e.tensor_tensor(zs[:, par, ZC[b]:ZC[b] + P], zs[:, par, ZC[b]:ZC[b] + P],
                                                               b2("sb01"), ALU.mult), s_, b2tok))
                for b in range(4):
                    for jb in range(b, 4):
                        lastm = M(lambda e, b=b, jb=jb: e.matmul(
                            ps[:, zo + ZC[b] + (jb - b) * P:zo + ZC[b] + ZW[b]], b2("tri") if jb == b else b2("neg1"),
                            zs[:, par, ZC[jb]:ZC[jb] + ZW[jb]], start=False, stop=False, skip_group_check=True), ms)
                    lastm = M(lambda e, b=b: e.matmul(ps[:, zo + ZC[b]:zo + ZC[b] + P], b_("ident"), b_("sbm"),
                                                      start=False, stop=True, skip_group_check=True))
                use(f"zs{par}", lastm)
                x = S(lambda e: e.activation(za[:, par, 0:1280], zz, ACT.Exp), lastm, was(f"za{par}"), after4)
                for k in banks:
                    bf[k] = [x, s_]
                return par, x

            def b_stage(h, par, tok):
                ob = 6 + h % 2
                r = slice((h % 2) * 64, (h % 2) * 64 + 64)
                c = h // 2
                for b in range(4):
                    t = M(lambda e, b=b: e.matmul(pb[ob][:, b * P:T], vsb[:, b, c * P:(c + 1) * P],
                                                  za[:, par, ZC[b]:ZC[b] + ZW[b]], start=b == 0, stop=b == 3,
                                                  skip_group_check=True), tok, vsbt, bf[ob] if b == 0 else None)
                use(f"za{par}", t)
                bf[ob] = put(ob, r, pb[ob][r, :], xh[r, 4 + c, :], xl[r, 4 + c, :], t, 4 + c)

            prev = None
            for h in range(8):
                cur = (h, *a_stage(h))
                if prev:
                    b_stage(*prev)
                prev = cur
            b_stage(*prev)

        stick()
        mix_out(lambda c: k_("one"), ctok)
        n3.close()
        n2.close()

        m2 = ExitStack()
        qm = sb("qm", [P, 2, T], F32, m2)
        pr3 = sb("pr3", [P, 2, 4, LC], F32, m2)
        pt3 = sb("pt3", [P, 4 * T], F32, m2)
        oh = sb("oh", [P, 2, T], F32R, m2)
        ol = sb("ol", [P, 2, T], F32R, m2)
        after5 = fence()
        xn = norm(xT, T, lambda c: v_("memx", c), None, xh, xl, after5, ctok)
        hi, lo, wt, done, ahead = w_next()
        qmt = []
        for c in range(2):
            t = proj(c, hi, lo, c * P, wt, xh, xl, xn)
            a = S(lambda e, c=c: e.mul(qm[:, c, :], pb[c], 1.0), t, after5)
            bf[c] = [a]
            qmt.append(head_norm(qm[:, c, :], a, v_("gmq"), T, qm[:, c, :], None, 4 + c, []))
        done(t)
        ahead()
        use("prob0", *after5)
        use("prob1", *after5)
        use("pt", *after5)
        omt = [[], []]

        def memory():
            def a_stage(i):
                par = seq["n"] % 2

                def qk(g):
                    r = slice((g % 2) * 64, (g % 2) * 64 + 64)
                    return [(qm[r, g // 2, i * P:(i + 1) * P], kmT[r, g // 2, :], 0, LC)]

                return soft_a(4, qk, [], LC, lambda g: g * 512, pr3[:, par, :, :], [qmt, kmtok])

            def b_stage(i, par, tok):
                per = []
                prob = pr3[:, par, :, :]
                evs = []
                for b in range(2):
                    bank = 4 + b
                    for g in range(4):
                        t = M(lambda e, b=b, g=g, bank=bank: e.transpose(
                            pb[bank][:, g * P:(g + 1) * P], prob[:, g, b * P:(b + 1) * P], ident), tok, bf[bank])
                    dst = pt3[:, b * T:(b + 1) * T]
                    ev = (V if b else S)(lambda e, dst=dst, bank=bank, b=b: (e.tensor_copy if b else e.copy)(dst, pb[bank]),
                                         t, was("pt"))
                    bf[bank] = [ev]
                    evs.append(ev)
                use(f"prob{par}", t)
                for c in range(2):
                    ob = 6 + c
                    for b in range(2):
                        t = M(lambda e, b=b, c=c, ob=ob: e.matmul(
                            pb[ob][:, 0:256], vm[:, b, c * P:(c + 1) * P], pt3[:, b * T + c * 256:b * T + (c + 1) * 256],
                            start=b == 0, stop=b == 1), evs[b], vmtok, bf[ob] if b == 0 else None)
                    last = []
                    for o in range(2):
                        r = slice(o * 64, o * 64 + 64)
                        cols = slice(i * P, (i + 1) * P)
                        src = pb[ob][r, o * P:(o + 1) * P]
                        a = S(lambda e, r=r, c=c, cols=cols, src=src: e.copy(oh[r, c, cols], src), t, after5)
                        b_ = V(lambda e, r=r, c=c, cols=cols, src=src: e.tensor_tensor(
                            ol[r, c, cols], src, oh[r, c, cols].bitcast(F32), ALU.subtract), a)
                        last += [a, b_]
                    omt[c] += last
                    bf[ob] = last
                use("pt", t)

            prev = None
            for i in range(4):
                cur = (i, *a_stage(i))
                if prev:
                    b_stage(*prev)
                prev = cur
            b_stage(*prev)

        qmt = [V(lambda e: e.tensor_scalar(qm[:, :, :], qm[:, :, :], 0.125, None, ALU.mult), qmt)]
        memory()
        hi, lo, wt, done, ahead = w_next()
        for c in range(NC):
            t = proj(c % 2, hi, lo, c * P, wt, oh, ol, lambda k: omt[k], 2)
            residual(c, c % 2, k_("one"), t, ctok)
        done(t)
        ahead()
        m2.close()

        xn = norm(xT, T, lambda c: v_("n2", c), None, xh, xl, fence(), ctok)
        ov = out.rearrange("(c p) t -> p c t", p=P)
        outs = []

        def store(c, tok):
            outs.append(load(SP, "out", ov[:, c, :], xT[:, c, :], tok))

        ffn(lambda c: k_("half"), ctok, xn, fence(), keep=False, final=store)
        SP(lambda e: e.nop(), outs[-1])

        for q in (V, S, G, M, SP):
            q.number()
        block = ctx.enter_context(nc.Block())

        @block.sync
        def _(eng):
            SP.emit(eng)

        @block.gpsimd
        def _(eng):
            G.emit(eng)

        @block.scalar
        def _(eng):
            S.emit(eng)

        @block.vector
        def _(eng):
            V.emit(eng)

        @block.tensor
        def _(eng):
            M.emit(eng)


def parts_of(x, bits, n):
    out, rest = [], float(x)
    for _ in range(n - 1):
        m, e = np.frexp(rest)
        p = float(np.ldexp(np.floor(m * 2 ** bits), int(e) - bits))
        out.append(p)
        rest -= p
    return out + [rest]


def turns():
    return [[1.0 / (2 * np.pi * n)] + parts_of(2 * np.pi * n, 11, 3) for n in (4096, 1)]


def constants():
    f = np.float32
    r = np.arange(P)
    cst = np.zeros((P, NCST), f)
    cst[:, 0:128] = np.eye(P)
    cst[:, 128:256] = 1
    cst[:, 256:384] = (r[:, None] // 64) == (r[None] // 64)
    cst[:, CST["eps"]] = EPS
    cst[:, CST["one"]] = 1
    cst[:, CST["half"]] = 0.5
    freq = (np.float64(500000.0) ** (-np.arange(0, 16, 2, dtype=np.float32).astype(np.float64) / 16)).astype(f)
    d = r % 64
    cst[:, CST["freq"]] = np.where(d < 16, freq[d % 8], 0)
    cst[:, CST["valid"]] = r >= 31
    masks = np.zeros((P, NBCS), f)
    q, k = r[:, None], r[None]
    masks[:, 0:128] = np.eye(P)
    masks[:, BCS["diag"]:][:, :128] = np.where(k <= q, 0, NEG)
    masks[:, BCS["prev"]:][:, :128] = np.where(k >= q, 0, NEG)
    masks[:, BCS["sbm"]:][:, :128] = np.where(q < k, 0, NEG)
    for i in range(4):
        ends = np.arange(NCMP) * 16 + 31
        masks[:, BCS["cmp"] + 32 * i:][:, :NCMP] = np.where(ends[None] <= q + i * P, 0, NEG)
    b1 = np.zeros((P, NB1C), f)
    rot = np.zeros((P, P), f)
    rot[r[1::2], r[0::2]] = -1
    rot[r[0::2], r[1::2]] = 1
    b1[:, 0:128] = rot
    t = np.arange(T)
    inv = (np.float64(10000.0) ** (-np.arange(16, dtype=np.float64) / 16)).astype(f)
    ang = np.concatenate([(t // 64).astype(f)[:, None] * inv[None], (t % 64).astype(f)[:, None] * inv[None]], 1)
    ang = np.repeat(ang.T, 2, axis=0)
    ang = np.concatenate([ang, ang], 0).astype(np.float64)
    b1[:, 128:640] = np.cos(ang)
    b1[:, 640:1152] = np.sin(ang)
    w = 2 * np.pi * (np.outer(r, r) % P) / P
    b1[:, 1152:1280] = np.cos(w) / np.sqrt(P)
    b1[:, 1280:1408] = np.sin(w) / np.sqrt(P)
    w = 2 * np.pi * (np.outer(t, t) % T) / T
    cn, sn = np.cos(w) / np.sqrt(T), -np.sin(w) / np.sqrt(T)
    b1[:, B1C["cn"]:][:, :2048] = cn.reshape(4, P, T).transpose(1, 0, 2).reshape(P, 2048)
    b1[:, B1C["sn"]:][:, :2048] = sn.reshape(4, P, T).transpose(1, 0, 2).reshape(P, 2048)
    b2 = np.zeros((P, NB2C), f)
    rot = np.zeros((P, P), f)
    for o in (0, 64):
        for i in range(8):
            rot[o + 8 + i, o + i] = -1
            rot[o + i, o + 8 + i] = 1
    b2[:, 0:128] = rot
    b2[:, 128:256] = -(q >= k).astype(f)
    b2[:, 256:384] = -1
    b2[:, 384:512] = q < k
    cnt = np.stack([np.minimum(t + n // 2, T) - np.maximum(t - n // 2, 0) for n in (2, 4, 8, 16)])
    icnt = np.broadcast_to((1.0 / cnt).astype(f)[None], (P, 4, T))
    return {"consts": cst, "masks": masks, "b1c": b1, "b2c": b2, "icnt": np.ascontiguousarray(icnt)}


_WEIGHTS = ["ada_w", "mix_in_w", "mix_out_w", "pool_w", "ffn_w1", "ffn_w3", "ffn_w2", "positions_2", "ffn1_wg_2",
            "ffn1_wu_2", "ffn1_wd_2", "w_in_2", "cmp_w1_k_2", "cmp_w2_k_2", "cmp_w1_v_2", "cmp_w2_v_2", "w_out_2",
            "mem_wq_2", "mem_wk_2", "mem_wv_2", "mem_wo_2", "ffn2_wg_2", "ffn2_wu_2", "ffn2_wd_2"]


def kernel(**inputs):
    import concourse.bacc as bacc
    from concourse.bass_utils import run_bass_kernel_spmd

    a = {k: np.asarray(v) for k, v in inputs.items()}

    def col(v):
        return np.asarray(v).reshape(-1, P).T

    def two(v):
        return np.concatenate([v.reshape(64, 1)] * 2, 0)

    def pe(v):
        w = v.reshape(16, 2, 64).transpose(2, 1, 0).reshape(64, 32)
        return np.concatenate([w, w], 0)

    vecs = {
        "c": col(a["c"]), "cc": col(a["c_ctx"]), "ab0": col(a["ada_b"][0]), "ab1": col(a["ada_b"][1]),
        "gm0": col(a["norm_mix_g"][0]), "gm1": col(a["norm_mix_g"][1]),
        "gf0": col(a["norm_ffn_g"][0]), "gf1": col(a["norm_ffn_g"][1]),
        "pscale": col(a["pool_scale"]), "fin": col(a["final_g"]), "n1": col(a["ffn1_norm_2"]),
        "mixg": col(a["mix_norm_2"]), "memx": col(a["mem_x_norm_2"]), "memkv": col(a["mem_kv_norm_2"]),
        "n2": col(a["ffn2_norm_2"]), "gq": two(a["nsa_q_norm_2"]), "gkc": two(a["nsa_kc_norm_2"]),
        "gks": two(a["nsa_ks_norm_2"]), "gkw": two(a["nsa_kw_norm_2"]), "gmq": two(a["mem_q_norm_2"]),
        "gmk": two(a["mem_k_norm_2"]), "sink": np.broadcast_to(a["attn_sink"].reshape(1, 8), (P, 8)),
        "pek": pe(a["cmp_pos_k_2"]), "pev": pe(a["cmp_pos_v_2"]),
    }
    arrays = {n: np.ascontiguousarray(a[n]) for n in _WEIGHTS}
    arrays["vecs"] = np.ascontiguousarray(np.concatenate([vecs[n] for n in VEC], 1))
    arrays["xT"] = np.ascontiguousarray(a["x"][0].T)
    arrays["ctxT"] = np.ascontiguousarray(a["ctx"][0].T)
    arrays["memT"] = np.ascontiguousarray(a["mem_2"][0].T)
    arrays.update(constants())
    nc = bacc.Bacc("TRN2", target_bir_lowering=False, num_devices=1)
    ins = {n: nc.dram_tensor("in_" + n, v.shape, mybir.dt.from_np(v.dtype), kind="ExternalInput").ap()
           for n, v in arrays.items()}
    out = nc.dram_tensor("out", (D, T), F32, kind="ExternalOutput").ap()
    program(nc, ins, out)
    r = run_bass_kernel_spmd(nc, [{"in_" + n: v for n, v in arrays.items()}], core_ids=[0])
    return np.ascontiguousarray(r.results[0]["out"].T)[None]
```

```python
from contextlib import ExitStack

import numpy as np

import concourse.bass as bass
from concourse import mybir

ALU = mybir.AluOpType
ACT = mybir.ActivationFunctionType
AXX = mybir.AxisListType.X
F32 = mybir.dt.float32
F32R = mybir.dt.float32r
BF16 = mybir.dt.bfloat16
I32 = mybir.dt.int32

P = 128
T = 512
NC = 8
D = 1024
FF = 2816
NF = FF // P
LC = 256
NCMP = 31
SLOT = 2048
NEG = -1e30
EPS = 1e-6


class Tok:

    def __init__(self, sem, value=None):
        self.sem, self.value, self.used = sem, value, value is not None


class Queue:

    def __init__(self, sem):
        self.sem, self.ops, self.last = sem, [], None

    def __call__(self, fn, *after):
        tok = Tok(self.sem)
        need = []
        stack = list(after)
        while stack:
            x = stack.pop()
            if isinstance(x, Tok):
                x.used = True
                need.append(x)
            elif x:
                stack.extend(x)
        self.ops.append((fn, need, tok))
        self.last = tok
        return tok

    def number(self):
        n = 0
        for _, _, tok in self.ops:
            if tok.used and tok.value is None:
                n += 1
                tok.value = n

    def emit(self, eng):
        seen = {}
        for fn, need, tok in self.ops:
            most = {}
            for x in need:
                most[x.sem] = max(most.get(x.sem, 0), x.value)
            for sem, value in most.items():
                if seen.get(sem, 0) < value:
                    eng.wait_ge(sem, value)
                    seen[sem] = value
            ins = fn(eng)
            if tok.used and tok.sem is self.sem:
                ins.then_inc(self.sem, 1)


VEC = {}
_at = 0
for _n, _w in (("c", 8), ("cc", 8), ("ab0", 48), ("ab1", 48), ("gm0", 8), ("gm1", 8), ("gf0", 8), ("gf1", 8),
               ("pscale", 8), ("fin", 8), ("n1", 8), ("mixg", 8), ("memx", 8), ("memkv", 8), ("n2", 8),
               ("gq", 1), ("gkc", 1), ("gks", 1), ("gkw", 1), ("gmq", 1), ("gmk", 1), ("sink", 8),
               ("pek", 32), ("pev", 32)):
    VEC[_n] = (_at, _w)
    _at += _w
NVEC = _at

CST = {"ident": 0, "ones": 128, "bd": 256, "eps": 384, "one": 385, "freq": 386, "valid": 387, "zero": 388, "half": 389}
NCST = 390
BCS = {"ident": 0, "diag": 128, "prev": 256, "sbm": 384, "cmp": 512}
NBCS = 512 + 4 * 32
B1C = {"rot": 0, "cos": 128, "sin": 640, "cd": 1152, "cn": 1408, "sn": 1408 + 2048}
NB1C = 1408 + 4096
B2C = {"rot": 0, "tri": 128, "neg1": 256, "sb01": 384}
NB2C = 512


def program(nc, A, out):
    ctx = ExitStack()
    with ctx:
        def sem(name):
            return ctx.enter_context(nc.semaphore(name))

        V, S, G, M = (Queue(sem(n)) for n in ("s_vec", "s_act", "s_pool", "s_pe"))
        SP = Queue(sem("s_sp"))
        dsem = {}

        def load(q, key, dst, src, *after):
            if key not in dsem:
                dsem[key] = [sem("d_" + key), 0]
            s = dsem[key]
            s[1] += 16
            sm, val = s[0], s[1]
            last = q.last
            q(lambda e: e.dma_start(dst, src).then_inc(sm, 16), *after)
            q.last = last
            return Tok(sm, val)

        def sb(name, shape, dt=F32, stack=ctx):
            return stack.enter_context(nc.sbuf_tensor(name, shape, dt))

        ps = ctx.enter_context(nc.psum_tensor("ps", [P, 8 * 512], F32))
        pb = [ps[:, i * 512:(i + 1) * 512] for i in range(8)]
        bf = [[] for _ in range(8)]

        xT = sb("xT", [P, NC, T])
        xh = sb("xh", [P, NC, T], F32R)
        xl = sb("xl", [P, NC, T], F32R)
        raw = [sb(f"raw{i}", [P, SLOT]) for i in range(2)]
        wh = [sb(f"wh{i}", [P, SLOT], F32R) for i in range(2)]
        wl = [sb(f"wl{i}", [P, SLOT], F32R) for i in range(2)]
        acc = sb("acc", [P, 1024])
        vec = sb("vec", [P, NVEC])
        cst = sb("cst", [P, NCST])
        bcs = sb("bcs", [P, NBCS], BF16)
        ada = [sb("ada0", [P, 48]), sb("ada1", [P, 48])]
        adac = sb("adac", [P, 16])
        sc = sb("sc", [P, 8, 2])
        cf = sb("cf", [P, 48])
        kmT = sb("kmT", [P, 2, LC])
        vm = sb("vm", [P, 2, LC])
        tmp = [sb(f"tmp{i}", [P, 512]) for i in range(4)]
        ssum = sb("ssum", [P, 512])
        sm = sb("sm", [P, 2, 16])
        hs = sb("hs", [P, 4, 8])
        dum = sb("dum", [P, 1])
        free = {}

        ident = cst[:, 0:128]
        ones = cst[:, 128:256]
        bd = cst[:, 256:384]

        def v_(name, c=0, w=1):
            return vec[:, VEC[name][0] + c:VEC[name][0] + c + w]

        def k_(name):
            return cst[:, CST[name]:CST[name] + 1]

        def b_(name, w=128, o=0):
            return bcs[:, BCS[name] + o:BCS[name] + o + w]

        def fence():
            return [q.last for q in (V, S, G, M) if q.last]

        units = []

        def w_unit(src, kc, cols):
            units.append(("w", src, kc, cols))

        def w_cols(w, c0, cols, k0=0, kc=NC):
            w_unit(w[k0 * P:(k0 + kc) * P, c0:c0 + cols].rearrange("(k p) n -> p k n", p=P), kc, cols)

        ada_w = A["ada_w"]

        def ada_unit(layer, j, k, kind="ada"):
            src = ada_w[layer, k * 256:(k + 1) * 256, j * 1024:(j + 1) * 1024]
            units.append((kind, src.rearrange("(k p) n -> p k n", p=P), layer, j, k))

        for j in range(2):
            for k in range(4):
                ada_unit(0, j, k, "first")
        w_cols(A["mem_wk_2"][0], 0, 256)
        w_cols(A["mem_wv_2"][0], 0, 256)
        for c in range(5):
            w_cols(A["mix_in_w"][0], c * 256, 256)
        for j in range(2, 6):
            for k in range(4):
                ada_unit(0, j, k)
        for c in range(4):
            w_cols(A["mix_out_w"][0], c * 256, 256)

        def ffn_units(w1, w3, w2, extra=()):
            extra = list(extra)

            def between():
                if extra:
                    ada_unit(*extra.pop(0))

            for g in range(NF // 2):
                w_cols(w1, g * 256, 256)
                between()
                w_cols(w3, g * 256, 256)
                between()
            for g in range(4):
                for k0, kc in ((0, 8), (8, 7), (15, 7)):
                    w_cols(w2, g * 256, 256, k0, kc)
                    between()

        ffn_units(A["ffn_w1"][0], A["ffn_w3"][0], A["ffn_w2"][0],
                  [(1, j, k) for j in range(6) for k in range(4)])
        w_unit(A["pool_w"][0].rearrange("g (c p) n -> p (g c) n", p=P), 8, 256)
        ffn_units(A["ffn_w1"][1], A["ffn_w3"][1], A["ffn_w2"][1])
        ffn_units(A["ffn1_wg_2"][0], A["ffn1_wu_2"][0], A["ffn1_wd_2"][0])
        wi2 = A["w_in_2"][0]
        for c0, cols in ((0, 256), (256, 256), (512, 256)):
            w_cols(wi2, c0, cols)
        for k in range(2):
            w_cols(A["cmp_w1_k_2"][0], 0, 256, 8 * k)
        for k in range(2):
            w_cols(A["cmp_w1_v_2"][0], 0, 256, 8 * k)
        for c0, cols in ((768, 256), (1024, 128), (1152, 152), (1304, 256), (1560, 256), (1816, 256), (2072, 256),
                         (2328, 256), (2584, 256)):
            w_cols(wi2, c0, cols)
        for c in range(4):
            w_cols(A["w_out_2"][0], c * 256, 256)
        w_cols(A["mem_wq_2"][0], 0, 256)
        w_unit(A["mem_wo_2"][0].rearrange("(k p) n -> p k n", p=P), 2, 1024)
        ffn_units(A["ffn2_wg_2"][0], A["ffn2_wu_2"][0], A["ffn2_wd_2"][0])

        rawtok = {}
        rawfree = [[], []]
        ready = {}
        wdone = [[], []]
        st = {"dma": 0, "prep": 0, "w": 0, "use": 0}
        accdone = {"t": [], "a": [], "fin": []}
        adatok = {}
        worder = [i for i, u in enumerate(units) if u[0] == "w"]

        def dma_unit():
            u = st["dma"]
            if u >= len(units):
                return
            st["dma"] += 1
            src = units[u][1]
            kc, cols = src.shape[1], src.shape[2]
            dst = raw[u % 2][:, 0:kc * cols].rearrange("p (k n) -> p k n", k=kc)
            rawtok[u] = load(SP, f"raw{u % 2}", dst, src, rawfree[u % 2])

        def prep_unit():
            u = st["prep"]
            st["prep"] += 1
            r = raw[u % 2]
            if units[u][0] == "w":
                _, _, kc, cols = units[u]
                n, s = kc * cols, st["w"] % 2
                st["w"] += 1
                hi, lo = wh[s][:, 0:n], wl[s][:, 0:n]
                a = S(lambda e: e.copy(hi, r[:, 0:n]), rawtok[u], wdone[s])
                b = V(lambda e: e.tensor_tensor(lo, r[:, 0:n], hi.bitcast(F32), ALU.subtract), a, wdone[s])
                ready[u] = (s, [a, b])
                rawfree[u % 2] = [a, b]
            else:
                _, _, layer, j, k = units[u]
                if k == 0:
                    ada_flush()
                toks = []
                for kk in range(2):
                    kc = 2 * k + kk
                    w = r[:, kk * 1024:(kk + 1) * 1024]
                    col = sc[:, kc, 0:1]
                    if kc == 0:
                        t = V(lambda e, w=w, col=col: e.tensor_scalar(acc[:, :], w, col, None, ALU.mult),
                              rawtok[u], sctok, accdone["fin"])
                    else:
                        t = V(lambda e, w=w, col=col: e.scalar_tensor_tensor(
                            out=acc[:, :], in0=w, scalar=col, in1=acc[:, :], op0=ALU.mult, op1=ALU.add),
                            rawtok[u], adatok["acc"])
                    adatok["acc"] = t
                    toks.append(t)
                rawfree[u % 2] = toks
                if k == 3:
                    pending.append((layer, j))
            dma_unit()

        pending = []

        def ada_flush():
            while pending:
                ada_finish(*pending.pop(0))

        def ada_finish(layer, j):
            for c in range(8):
                t = M(lambda e, c=c: e.matmul(pb[7][:, c:c + 1], acc[:, c * P:(c + 1) * P], k_("one"),
                                              start=True, stop=True), adatok["acc"], bf[7], ctok)
            accdone["fin"] = [t]
            bias = v_("ab1" if layer else "ab0", j * 8, 8)
            t2 = V(lambda e: e.tensor_tensor(ada[layer][:, j * 8:j * 8 + 8], pb[7][:, 0:8], bias, ALU.add), t)
            bf[7] = [t2]
            adatok[("m", layer, j)] = t2

        def ada_step():
            if st["prep"] < len(units) and units[st["prep"]][0] == "ada":
                prep_unit()
                ada_flush()

        def ada_first():
            for u in range(8):
                _, _, layer, j, k = units[u]
                for kk in range(2):
                    for c in range(8):
                        o = (j * 8 + c) * 2
                        t = M(lambda e, u=u, kk=kk, c=c, o=o, k=k: e.matmul(
                            pb[7][:, o:o + 2], raw[u % 2][:, kk * 1024 + c * P:kk * 1024 + (c + 1) * P],
                            sc[:, 2 * k + kk, :], start=u == 0 and kk == 0 and c == 0, stop=k == 3 and kk == 1,
                            skip_group_check=True), rawtok[u], sctok)
                rawfree[u % 2] = [t]
                st["prep"] += 1
                dma_unit()
            for z, dst in ((0, ada[0]), (1, adac)):
                t2 = V(lambda e, z=z, dst=dst: e.tensor_tensor(
                    dst[:, 0:16], pb[7][:, 0:32].rearrange("p (a z) -> p z a", z=2)[:, z], v_("ab0", 0, 16), ALU.add), t)
                adatok[("first", z)] = t2
                bf[7] = bf[7] + [t2]

        def w_next():
            u = worder[st["use"]]
            st["use"] += 1
            while st["prep"] <= u:
                prep_unit()
            s, toks = ready[u]
            kc, cols = units[u][2], units[u][3]
            hi = wh[s][:, 0:kc * cols].rearrange("p (k n) -> p k n", k=kc)
            lo = wl[s][:, 0:kc * cols].rearrange("p (k n) -> p k n", k=kc)

            if st["use"] < len(worder) and worder[st["use"]] - u <= 2:
                while st["prep"] <= worder[st["use"]]:
                    prep_unit()

            def done(tok):
                wdone[s] = [tok]
                ada_flush()

            return hi, lo, toks, done

        def mm3(dst, ah, al, bh, bl, start, stop, *after, skip=False):
            M(lambda e: e.matmul(dst, ah, bh, start=start, stop=False, skip_group_check=skip), *after)
            M(lambda e: e.matmul(dst, ah, bl, start=False, stop=False, skip_group_check=skip))
            return M(lambda e: e.matmul(dst, al, bh, start=False, stop=stop, skip_group_check=skip))

        def proj(bank, hi, lo, col, toks, src_h, src_l, srctoks, nk=NC, k0=0, start=True, stop=True, n=T):
            t = None
            for k in range(nk):
                t = mm3(pb[bank][:, 0:n], hi[:, k, col:col + P], lo[:, k, col:col + P],
                        src_h[:, k0 + k, 0:n], src_l[:, k0 + k, 0:n],
                        start and k == 0, stop and k == nk - 1,
                        toks, srctoks(k0 + k), bf[bank] if start and k == 0 else None)
            return t

        def proj2(banks, hi, lo, toks, src_h, src_l, srctoks):
            t = [None, None]
            for k in range(NC):
                for cc in range(2):
                    t[cc] = mm3(pb[banks[cc]], hi[:, k, cc * P:(cc + 1) * P], lo[:, k, cc * P:(cc + 1) * P],
                                src_h[:, k, :], src_l[:, k, :], k == 0, k == NC - 1, toks, srctoks(k),
                                bf[banks[cc]] if k == 0 else None)
            return t

        def proj_tok(bank, hi, lo, c0, cols, toks, src_h, src_l, srctoks, tb, o=0):
            t = None
            for k in range(NC):
                sl = slice(tb * P, (tb + 1) * P)
                t = mm3(pb[bank][:, o:o + cols], src_h[:, k, sl], src_l[:, k, sl], hi[:, k, c0:c0 + cols],
                        lo[:, k, c0:c0 + cols], k == 0, k == NC - 1, toks, srctoks(k), bf[bank])
            return t

        def use(name, *toks):
            free[name] = list(toks)

        def was(name):
            return free.get(name, [])

        def square_in(c, src, n, after):
            if c == 0:
                t = S(lambda e: e.activation(ssum[:, 0:n], src, ACT.Square), after, was("ssum"))
            else:
                a = S(lambda e: e.activation(tmp[3][:, 0:n], src, ACT.Square), after, was("tmp3"))
                t = V(lambda e: e.tensor_tensor(ssum[:, 0:n], ssum[:, 0:n], tmp[3][:, 0:n], ALU.add), a, free["ss"])
                use("tmp3", t)
            free["ss"] = [t]
            return t

        def preload(func, *after):
            S(lambda e: e.activation(dum[:, :], k_("one"), func), ctok, after)

        ring = {"hs": 0}

        def inverse(src, tok, heads, n, mean):
            i = ring["hs"] % 4
            ring["hs"] += 1
            nb = (n + P - 1) // P
            last = n - (nb - 1) * P
            ind = cst[:, 256:384:64] if heads == 2 else k_("one")
            for b in range(nb):
                w = P if b < nb - 1 else last
                m = M(lambda e, b=b, w=w: e.matmul(pb[7][0:w, b * heads:(b + 1) * heads], src[:, b * P:b * P + w], ind,
                                                   start=True, stop=True), tok, bf[7], ctok)
            w = P if nb > 1 else last
            h = hs[0:w, i, 0:nb * heads]
            a = S(lambda e: e.activation(h, pb[7][0:w, 0:nb * heads], ACT.Sqrt, bias=cst[0:w, CST["eps"]:CST["eps"] + 1],
                                         scale=1.0 / mean), m, was(f"hs{i}"))
            bf[7] = [a]
            return m, (i, heads, n, V(lambda e: e.reciprocal(h, h), a))

        def spread(job, sq=None):
            i, heads, n, tok = job
            nb = (n + P - 1) // P
            if heads == 2:
                w = min(P, n)
                full = tmp[sq][0:w, 0:nb * P].rearrange("p (b d) -> p b d", d=64)
                each = hs[0:w, i, 0:nb * 2].unsqueeze(2).broadcast_to([w, nb * 2, 64])
                tok = V(lambda e: e.tensor_copy(full, each), tok, was(f"tmp{sq}"))
            for b in range(nb):
                w = min(P, n - b * P)
                r = tmp[sq][0:w, b * P:(b + 1) * P] if heads == 2 else hs[0:w, i, b:b + 1].broadcast_to([w, P])
                m = M(lambda e, b=b, w=w, r=r: e.matmul(pb[6][:, b * P:b * P + w], r, cst[0:w, 0:w], start=True, stop=True),
                      tok, bf[6])
            use(f"hs{i}", m)
            if heads == 2:
                use(f"tmp{sq}", m)
            return m

        def rstd_of(tok, n):
            m, job = inverse(ssum, tok, 1, n, D)
            use("ssum", m)
            return spread(job)

        def norm(src, n, factor, shift, dh, dl, after, ftoks, then=None):
            r = rstd_of(free["ss"], n)
            toks = []
            for c in range(NC):
                i = c % 3
                t = V(lambda e, c=c, i=i: e.scalar_tensor_tensor(
                    out=tmp[i][:, 0:n], in0=src[:, c, 0:n], scalar=factor(c), in1=pb[6][:, 0:n],
                    op0=ALU.mult, op1=ALU.mult), r, was(f"tmp{i}"), ftoks)
                if shift is None:
                    a = S(lambda e, c=c, i=i: e.copy(dh[:, c, 0:n], tmp[i][:, 0:n]), t, after)
                    b = V(lambda e, c=c, i=i: e.tensor_tensor(
                        dl[:, c, 0:n], tmp[i][:, 0:n], dh[:, c, 0:n].bitcast(F32), ALU.subtract), a)
                else:
                    a = S(lambda e, c=c, i=i: e.activation(dh[:, c, 0:n], tmp[i][:, 0:n], ACT.Identity,
                                                           bias=shift(c)), t, after)
                    b = V(lambda e, c=c, i=i: e.scalar_tensor_tensor(
                        out=dl[:, c, 0:n], in0=tmp[i][:, 0:n], scalar=shift(c), in1=dh[:, c, 0:n].bitcast(F32),
                        op0=ALU.add, op1=ALU.subtract), a)
                use(f"tmp{i}", a, b)
                toks.append([a, b])
            bf[6] = [t]
            if then is not None:
                preload(then)
            return lambda k: toks[k]

        xtok = [None] * NC

        def residual(c, bank, coef, tok, ctoks, keep=True):
            t = V(lambda e: e.scalar_tensor_tensor(out=xT[:, c, :], in0=pb[bank][:, :], scalar=coef, in1=xT[:, c, :],
                                                   op0=ALU.mult, op1=ALU.add), tok, ctoks, xtok[c])
            bf[bank] = [t]
            xtok[c] = t
            if keep:
                if c == NC - 1:
                    preload(ACT.Sqrt)
                square_in(c, xT[:, c, :], T, t)
            return t

        for name, dst, src in (("vec", vec, A["vecs"]), ("cst", cst, A["consts"])):
            load(SP, "c0", dst[:, :], src)
        ctok = [Tok(dsem["c0"][0], 32)]

        s0 = ExitStack()
        mh = sb("mh", [P, NC, LC], F32R, s0)
        ml = sb("ml", [P, NC, LC], F32R, s0)
        a1 = ExitStack()
        ctT = sb("ctT", [P, NC, LC], F32, a1)
        mmT = sb("mmT", [P, NC, LC], F32, a1)
        bst = sb("bst", [P, NBCS], F32, a1)
        dma_unit()
        dma_unit()
        xtk = load(SP, "x", xT[:, :, :], A["xT"].rearrange("(c p) t -> p c t", p=P))
        cttok = load(SP, "ct", ctT[:, :, :], A["ctxT"].rearrange("(c p) t -> p c t", p=P))
        for c in range(NC):
            xtok[c] = xtk
        sctok = [S(lambda e: e.activation(sc[:, :, :], vec[:, 0:16].rearrange("p (z k) -> p k z", z=2), ACT.Silu), ctok)]
        preload(ACT.Sqrt)
        ada_first()
        mtok = load(SP, "mm", mmT[:, :, :], A["memT"].rearrange("(c p) t -> p c t", p=P))
        btok = load(SP, "bs", bst[:, :], A["masks"])

        def factors(o, g, src, j, toks):
            return [V(lambda e: e.scalar_tensor_tensor(out=cf[:, o:o + 8], in0=src[:, j * 8:j * 8 + 8], scalar=1.0,
                                                       in1=g, op0=ALU.add, op1=ALU.mult), toks)]

        f0 = factors(0, v_("gm0", 0, 8), ada[0], 1, [adatok[("first", 0)]])
        fc = factors(8, v_("gm0", 0, 8), adac, 1, [adatok[("first", 1)]])
        for c in range(NC):
            square_in(c, mmT[:, c, :], LC, mtok)
        mt = norm(mmT, LC, lambda c: v_("memkv", c), None, mh, ml, [], ctok)
        for c in range(NC):
            square_in(c, xT[:, c, :], T, xtk)
        xt = norm(xT, T, lambda c: cf[:, c:c + 1], lambda c: ada[0][:, c:c + 1], xh, xl, [], f0)
        bctok = [V(lambda e: e.tensor_copy(bcs[:, :], bst[:, :]), btok)]

        jobs_ = []

        def start(gen):
            next(gen)
            jobs_.append(gen)

        def advance():
            for g in list(jobs_):
                if next(g, "end") == "end":
                    jobs_.remove(g)

        def drain():
            while jobs_:
                advance()

        def head_norm(src, srctok, sq, gain, n, dst, res):
            m, job = inverse(tmp[sq], srctok, 2, n, 64)
            use(f"tmp{sq}", m)
            yield
            m = spread(job, sq)
            t = V(lambda e: e.scalar_tensor_tensor(out=dst, in0=src, scalar=gain, in1=pb[6][:, 0:n],
                                                   op0=ALU.mult, op1=ALU.mult), m, srctok)
            bf[6] = [t]
            res.append(t)
            yield

        def km_job(c, t):
            a = S(lambda e: e.copy(kmT[:, c, :], pb[c][:, 0:LC]), t)
            q = S(lambda e: e.activation(tmp[c][:, 0:LC], pb[c][:, 0:LC], ACT.Square), t, was(f"tmp{c}"))
            bf[c] = [a, q]
            yield
            yield from head_norm(kmT[:, c, :], [a, q], c, v_("gmk"), LC, kmT[:, c, :], kmtok)

        hi, lo, wt, done = w_next()
        kmtok = []
        for c in range(2):
            t = proj(c, hi, lo, c * P, wt, mh, ml, mt, n=LC)
            advance()
            start(km_job(c, t))
        done(t)
        hi, lo, wt, done = w_next()
        vmtok = []
        for tb in range(2):
            t = proj_tok(2 + tb, hi, lo, 0, 256, wt, mh, ml, mt, tb)
            advance()
            a = S(lambda e, tb=tb: e.copy(vm[:, tb, :], pb[2 + tb][:, 0:256]), t)
            bf[2 + tb] = [a]
            vmtok.append(a)
        done(t)
        memlast = t
        drain()
        for c in range(NC):
            square_in(c, ctT[:, c, :], LC, cttok)
        ct = norm(ctT, LC, lambda c: cf[:, 8 + c:9 + c], lambda c: adac[:, c:c + 1], mh, ml, [memlast], fc)

        a1.close()
        a1 = ExitStack()
        b1c = sb("b1c", [P, NB1C], F32, a1)
        fab = sb("fab", [P, 3072], F32, a1)
        fT = fab[:, 0:2048].rearrange("p (c t) -> p c t", c=4)
        AB = fab[:, 2048:3072].rearrange("p (c t) -> p c t", c=4)
        qT = sb("qT", [P, 4, T], F32, a1)
        kT = sb("kT", [P, T], F32, a1)
        kTs = sb("kTs", [P, T], F32, a1)
        kcT = sb("kcT", [P, LC], F32, a1)
        kcTs = sb("kcTs", [P, LC], F32, a1)
        vt = sb("vt", [P, 4, 256], F32, a1)
        vct = sb("vct", [P, 2, 256], F32, a1)
        pr = sb("pr", [P, 2, 2, 640], F32, a1)
        pt = fab[:, 0:2560].rearrange("p (a b) -> p a b", a=2)
        b1tok = [load(G, "b1c", b1c[:, :], A["b1c"], fence())]

        def b1(name, w=128, o=0):
            return b1c[:, B1C[name] + o:B1C[name] + o + w]

        def rope(src, srctok, cos, sin, rot, scale, dst, bank, ctoks, res, n=T):
            i = 2 + ring["hs"] % 2
            ring["hs"] += 1
            m = M(lambda e: e.matmul(pb[bank][:, 0:n], rot, src, start=True, stop=True), srctok, bf[bank], ctoks)
            b = V(lambda e: e.scalar_tensor_tensor(out=tmp[i][:, 0:n], in0=pb[bank][:, 0:n], scalar=scale, in1=sin,
                                                   op0=ALU.mult, op1=ALU.mult), m, was(f"tmp{i}"), ctoks)
            bf[bank] = [b]
            a = V(lambda e: e.scalar_tensor_tensor(out=dst, in0=src, scalar=scale, in1=cos,
                                                   op0=ALU.mult, op1=ALU.mult), m, srctok)
            t = V(lambda e: e.tensor_tensor(dst, dst, tmp[i][:, 0:n], ALU.add), a, b)
            use(f"tmp{i}", t)
            res.append(t)

        def swap(dst, src, key, tok, after=()):
            load(G, key, dst[0:64], src[64:128], tok, after)
            return load(G, key, dst[64:128], src[0:64], tok, after)

        def twice(bank, o=0):
            return pb[bank][:, o:o + P].rearrange("p (j d) -> p j d", j=2).unsqueeze(2).broadcast_to([P, 2, 2, 64])

        def dup(dst):
            return dst.rearrange("p (j a d) -> p j a d", j=2, a=2)

        ft, qt = [], []

        def q_job(dst, a):
            yield
            rope(dst, a, b1("cos", T), b1("sin", T), b1("rot"), 0.125, dst, 5, b1tok, qt)

        for u in range(4):
            hi, lo, wt, done = w_next()
            ts = proj2((0, 1), hi, lo, wt, xh, xl, xt) if u == 0 else None
            for cc in range(2):
                c = 2 * u + cc
                b = c % 4
                t = ts[cc] if ts else proj(b, hi, lo, cc * P, wt, xh, xl, xt)
                advance()
                dst = fT[:, c, :] if c < 4 else qT[:, c - 4, :]
                a = S(lambda e, dst=dst, b=b: e.copy(dst, pb[b]), t, b1tok)
                bf[b] = [a]
                if c < 4:
                    ft.append(a)
                else:
                    start(q_job(dst, a))
            done(t)
        hi, lo, wt, done = w_next()
        t = proj(0, hi, lo, 0, wt, xh, xl, xt)
        advance()
        a = S(lambda e: e.copy(kT[:, :], pb[0]), t, b1tok)
        bf[0] = [a]
        t = proj(1, hi, lo, 0, wt, mh, ml, ct, n=LC)
        kt = []
        rope(kT[:, :], a, b1("cos", T), b1("sin", T), b1("rot"), 1.0, kT[:, :], 5, b1tok, kt)
        drain()
        kst = swap(kTs, kT, "kTs", kt)
        kct = S(lambda e: e.copy(kcT[:, :], pb[1][:, 0:LC]), t)
        bf[1] = [kct]
        kcst = swap(kcTs, kcT, "kcTs", kct)
        vtt, vctt = [], []
        for tb in range(4):
            bank = 3 + tb % 2
            t = proj_tok(bank, hi, lo, P, P, wt, xh, xl, xt, tb)
            a = S(lambda e, tb=tb, bank=bank: e.copy(dup(vt[:, tb, :]), twice(bank)), t)
            bf[bank] = [a]
            vtt.append(a)
        for tb in range(2):
            bank = 3 + tb % 2
            t = proj_tok(bank, hi, lo, P, P, wt, mh, ml, ct, tb)
            a = S(lambda e, tb=tb, bank=bank: e.copy(dup(vct[:, tb, :]), twice(bank)), t)
            bf[bank] = [a]
            vctt.append(a)
        done(t)
        xlast = t

        mixt = [[] for _ in range(NC)]

        def put(bank, rows, cols, dst_h, dst_l, tok, c):
            a = S(lambda e: e.copy(dst_h, cols), tok, xlast)
            b = V(lambda e: e.tensor_tensor(dst_l, cols, dst_h.bitcast(F32), ALU.subtract), a)
            mixt[c] += [a, b]
            return [a, b]

        for c in range(4):
            abt = []
            for tb in range(4):
                bank = 5 + tb % 2
                m = M(lambda e, c=c, tb=tb, bank=bank: e.matmul(
                    pb[bank][:, 0:256], fT[:, c, tb * P:(tb + 1) * P], b1("cd", 256), start=True, stop=True),
                    ft[c], bf[bank], b1tok)
                w = V(lambda e, tb=tb, bank=bank: e.tensor_copy(AB[:, tb, :], pb[bank][:, 0:256]), m, was("AB"))
                bf[bank] = [w]
                abt.append(w)
            bank = c % 2
            for tb in range(4):
                for z, tab in ((0, "cn"), (1, "sn")):
                    m = M(lambda e, tb=tb, z=z, tab=tab, bank=bank: e.matmul(
                        pb[bank], AB[:, tb, z * P:(z + 1) * P], b1(tab, T, tb * T),
                        start=(tb == 0 and z == 0), stop=(tb == 3 and z == 1)),
                        abt[tb], bf[bank] if tb == 0 and z == 0 else None)
            use("AB", m)
            bf[bank] = put(bank, None, pb[bank], xh[:, c, :], xl[:, c, :], m, c)
        use("pt0", m)
        use("pt1", m)

        seq = {"n": 0, "pt": 0}

        def soft_a(nh, qk, masks, width, span, prob, after, sink=None, gate=None, gtok=(), valid=None, wide=False):
            par = seq["n"] % 2
            seq["n"] += 1
            nm, rs, es = sm[:, par, 0:nh], sm[:, par, 4:4 + nh], sm[:, par, 8:8 + nh]
            base = {}
            toks = []
            for g in range(nh):
                o = span(g)
                banks = sorted({o // 512, (o + width - 1) // 512})
                t = None
                for q, k, col, w in qk(g):
                    mk = [x for x in masks if x[0] == col]
                    t = M(lambda e, q=q, k=k, a=o + col, w=w, mk=mk: e.matmul(
                        ps[:, a:a + w], q, k, start=True, stop=not mk, skip_group_check=True),
                        after, [bf[b] for b in banks])
                    for col2, w2, mask in mk:
                        t = M(lambda e, a=o + col2, w=w2, mask=mask: e.matmul(
                            ps[:, a:a + w], b_("ident"), mask, start=False, stop=True, skip_group_check=True), bctok)
                toks.append((t, banks, o))
            red = []
            for g in range(nh):
                t, banks, o = toks[g]
                red.append(V(lambda e, g=g, o=o: e.tensor_reduce(nm[:, g:g + 1], ps[:, o:o + width], AXX, ALU.max,
                                                                 negate=sink is None), t, was(f"sm{par}")))
            if sink is not None:
                red = [V(lambda e: e.tensor_tensor(nm, nm, sink, ALU.max), red)]
                red = [V(lambda e: e.tensor_scalar(nm, nm, -1.0, None, ALU.mult), red)]
            ex = []
            for g in range(nh):
                t, banks, o = toks[g]
                a = S(lambda e, g=g, o=o: e.activation(prob[:, g, 0:width], ps[:, o:o + width], ACT.Exp,
                                                       bias=nm[:, g:g + 1], accum_out=rs[:, g:g + 1]),
                      red, was(f"prob{par}"))
                for b in banks:
                    bf[b] = [x for x in bf[b] if x in ex] + [a]
                ex.append(a)
            last = ex
            if sink is not None:
                d = V(lambda e: e.tensor_tensor(es, sink, nm, ALU.add), red)
                d = S(lambda e: e.activation(es, es, ACT.Exp), d)
                last = [V(lambda e: e.tensor_tensor(rs, rs, es, ALU.add), d, ex)]
            r = V(lambda e: e.reciprocal(rs, rs), last)
            if gate is not None:
                r = V(lambda e: e.tensor_tensor(rs, rs, gate, ALU.mult), r, gtok)
            if valid is not None:
                r = V(lambda e: e.tensor_scalar(rs, rs, valid, None, ALU.mult), r)
            out = []
            for g in range(nh):
                out.append(V(lambda e, g=g: e.tensor_scalar(prob[:, g, 0:width], prob[:, g, 0:width], rs[:, g:g + 1],
                                                            None, ALU.mult), r))
            use(f"sm{par}", *out)
            return par, out

        def soft_b(nh, prob, ptok, par, blocks, ptile, pbanks=(4, 5)):
            per = max(1, 4 // nh)
            evs = []
            for b0 in range(0, len(blocks), per):
                grp = blocks[b0:b0 + per]
                bank = pbanks[seq["pt"] % len(pbanks)]
                for bi, (col, w, v, vtk) in enumerate(grp):
                    for g in range(nh):
                        o = (bi * nh + g) * P
                        t = M(lambda e, o=o, g=g, col=col, w=w, bank=bank: e.transpose(
                            pb[bank][0:w, o:o + P], prob[:, g, col:col + w], ident), ptok, bf[bank], ctok)
                w = grp[0][1]
                n = len(grp) * nh * P
                dst = ptile[0:w, b0 * nh * P:b0 * nh * P + n]
                if seq["pt"] % 2:
                    ev = V(lambda e, dst=dst, bank=bank, w=w, n=n: e.tensor_copy(dst, pb[bank][0:w, 0:n]), t, was(f"pt{par}"))
                else:
                    ev = S(lambda e, dst=dst, bank=bank, w=w, n=n: e.copy(dst, pb[bank][0:w, 0:n]), t, was(f"pt{par}"))
                bf[bank] = [ev]
                seq["pt"] += 1
                evs += [ev] * len(grp)
            use(f"prob{par}", t)
            return evs

        def soft_c(nh, evs, par, blocks, ptile, obank, first, last):
            for bi, (col, w, v, vtk) in enumerate(blocks):
                t = M(lambda e, bi=bi, v=v, w=w: e.matmul(
                    pb[obank][:, 0:nh * P], v, ptile[0:w, bi * nh * P:(bi + 1) * nh * P],
                    start=first and bi == 0, stop=last and bi == len(blocks) - 1),
                    evs[bi], vtk, bf[obank] if first and bi == 0 else None)
            use(f"pt{par}", t)
            return t

        def pipeline(jobs, a_stage, b_stage, c_stage, each=None):
            got = {}
            n = len(jobs)
            for s_ in range(n + 2):
                if s_ < n:
                    got[s_] = a_stage(s_, *jobs[s_])
                if 0 <= s_ - 1 < n:
                    got[s_ - 1] = (got[s_ - 1], b_stage(s_ - 1, *jobs[s_ - 1], got[s_ - 1]))
                if 0 <= s_ - 2 < n:
                    c_stage(s_ - 2, *jobs[s_ - 2], got[s_ - 2])
                if each:
                    each()

        def first_attention():
            jobs = [(i, j, h2) for i in range(4) for j in range(2) for h2 in range(2)]

            def a_stage(n_, i, j, h2):
                nb = [b for b in (i - 1, i, i + 1) if 0 <= b < 4]
                width = len(nb) * P + LC
                off = 512 - len(nb) * P

                def qk(g):
                    h = 4 * j + 2 * h2 + g
                    r = slice((h % 2) * 64, (h % 2) * 64 + 64)
                    kk, kc_ = (kT, kcT) if h % 2 == j else (kTs, kcTs)
                    q = qT[r, h // 2, i * P:(i + 1) * P]
                    return [(q, kk[r, b * P:(b + 1) * P], n * P, P) for n, b in enumerate(nb)] + \
                        [(q, kc_[r, :], len(nb) * P, LC)]

                masks = [(n * P, P, b_("prev") if b < i else b_("diag"))
                         for n, b in enumerate(nb) if b != i]
                par = seq["n"] % 2
                sink = v_("sink", 4 * j + 2 * h2, 2)
                par, tok = soft_a(2, qk, masks, width, lambda g: g * 1024 + off, pr[:, par, :, :],
                                  [qt, kt, kst, kct, kcst], sink=sink)
                return par, tok, nb, width

            def values(j, nb):
                vs = [(m * P, P, vt[:, b, j * P:(j + 1) * P], vtt[b]) for m, b in enumerate(nb)]
                return vs + [((len(nb) + m) * P, P, vct[:, m, j * P:(j + 1) * P], vctt[m]) for m in range(2)]

            def b_stage(n, i, j, h2, got):
                par, tok, nb, width = got
                return soft_b(2, pr[:, par, :, :], tok, par, values(j, nb), pt[:, par, :])

            def c_stage(n, i, j, h2, got):
                (par, tok, nb, width), evs = got
                ob = 6 + n % 2
                t = soft_c(2, evs, par, values(j, nb), pt[:, par, :], ob, True, True)
                last = []
                for g in range(2):
                    c = 4 + (4 * j + 2 * h2) // 2
                    r = slice(g * 64, g * 64 + 64)
                    cols = slice(i * P, (i + 1) * P)
                    last += put(ob, r, pb[ob][r, g * P:(g + 1) * P], xh[r, c, cols], xl[r, c, cols], t, c)
                bf[ob] = last

            pipeline(jobs, a_stage, b_stage, c_stage, ada_step)

        first_attention()

        def mix_out(coef, ctoks):
            for u in range(4):
                hi, lo, wt, done = w_next()
                for cc in range(2):
                    c = 2 * u + cc
                    t = proj(c % 2, hi, lo, cc * P, wt, xh, xl, lambda k: mixt[k])
                    residual(c, c % 2, coef(c), t, ctoks)
                done(t)
            return t

        mix_out(lambda c: ada[0][:, 16 + c:17 + c], adatok[("m", 0, 2)])
        a1.close()
        s0.close()

        names = {"n": 0}

        def ffn(coef, ctoks, xtoks, arena, keep=True, final=None):
            names["n"] += 1
            hst = ExitStack()
            hh = sb(f"hh{names['n']}", [P, NF, T], F32R, hst)
            hl = sb(f"hl{names['n']}", [P, NF, T], F32R, hst)
            ht = []
            for g in range(NF // 2):
                hi, lo, wt, done = w_next()
                sg = []
                ts = proj2((0, 1), hi, lo, wt, xh, xl, xtoks) if g == 0 else None
                for cc in range(2):
                    t = ts[cc] if ts else proj(cc, hi, lo, cc * P, wt, xh, xl, xtoks)
                    sg.append(S(lambda e, cc=cc: e.activation(tmp[cc][:, :], pb[cc], ACT.Silu), t, was(f"tmp{cc}")))
                    bf[cc] = [sg[-1]]
                done(t)
                hi, lo, wt, done = w_next()
                for cc in range(2):
                    f = 2 * g + cc
                    t = proj(2 + cc, hi, lo, cc * P, wt, xh, xl, xtoks)
                    m = V(lambda e, cc=cc: e.tensor_tensor(tmp[cc][:, :], pb[2 + cc], tmp[cc][:, :], ALU.mult), t, sg[cc])
                    bf[2 + cc] = [m]
                    a = S(lambda e, f=f, cc=cc: e.copy(hh[:, f, :], tmp[cc][:, :]), m, arena)
                    b = V(lambda e, f=f, cc=cc: e.tensor_tensor(hl[:, f, :], tmp[cc][:, :], hh[:, f, :].bitcast(F32),
                                                                ALU.subtract), a)
                    use(f"tmp{cc}", a, b)
                    ht.append([a, b])
                done(t)
            for g in range(4):
                b0 = 2 * (g % 2)
                for k0, kc in ((0, 8), (8, 7), (15, 7)):
                    hi, lo, wt, done = w_next()
                    for cc in range(2):
                        t = proj(b0 + cc, hi, lo, cc * P, wt, hh, hl, lambda k: ht[k], kc, k0, k0 == 0, k0 + kc == NF)
                        if k0 + kc == NF:
                            r = residual(2 * g + cc, b0 + cc, coef(2 * g + cc), t, ctoks, keep)
                            if final:
                                final(2 * g + cc, r)
                    done(t)
            hst.close()
            return t

        f1 = factors(16, v_("gf0", 0, 8), ada[0], 4, [adatok[("m", 0, 4)], adatok[("m", 0, 3)]])
        xn = norm(xT, T, lambda c: cf[:, 16 + c:17 + c], lambda c: ada[0][:, 24 + c:25 + c], xh, xl, fence(), f1, then=ACT.Silu)
        ffn(lambda c: ada[0][:, 40 + c:41 + c], adatok[("m", 0, 5)], xn, fence())

        pst = ExitStack()
        xp = sb("xp", [P, NC, T + 16], F32, pst)
        sa = sb("sa", [P, 2, T + 16], F32, pst)
        icnt = sb("icnt", [P, 4, T], F32, pst)
        f2 = factors(24, v_("gm1", 0, 8), ada[1], 1, [adatok[("m", 1, 1)], adatok[("m", 1, 0)]])
        f2g = [V(lambda e: e.tensor_tensor(cf[:, 40:48], ada[1][:, 16:24], v_("pscale", 0, 8), ALU.mult),
                 adatok[("m", 1, 2)])]
        after = fence()
        ictok = load(G, "icnt", icnt[:, :, :], A["icnt"], after)
        z = [G(lambda e: e.memset(xp[:, :, 0:8], 0.0), after), G(lambda e: e.memset(xp[:, :, T + 8:T + 16], 0.0), after)]
        r = rstd_of(free["ss"], T)
        pooled = []
        for c in range(NC):
            i = c % 2
            g = c // 2
            w = 2 << g
            t = V(lambda e, c=c, i=i: e.scalar_tensor_tensor(out=tmp[i][:, :], in0=xT[:, c, :], scalar=cf[:, 24 + c:25 + c],
                                                             in1=pb[6], op0=ALU.mult, op1=ALU.mult),
                  r, was(f"tmp{i}"), f2)
            bf[6] = [t]
            x_ = xp[:, c, :]
            a = S(lambda e, c=c, i=i: e.activation(xp[:, c, 8:T + 8], tmp[i][:, :], ACT.Identity,
                                                   bias=ada[1][:, c:c + 1]), t, after)
            use(f"tmp{i}", a)
            src, at, t, width = xp[:, c, :], 0, [a, z], 1
            step = 0
            while width < w:
                dst = sa[:, step % 2, :]
                n = T + 16 - 2 * width + 1
                t = [V(lambda e, src=src, dst=dst, width=width: e.tensor_tensor(
                    dst[:, 0:T + 17 - 2 * width], src[:, 0:T + 17 - 2 * width], src[:, width:T + 17 - width], ALU.add),
                    t, was(f"sa{step % 2}"), after)]
                src = dst
                width *= 2
                step += 1
            o = 8 - w // 2
            t = V(lambda e, src=src, o=o, g=g, i=i: e.tensor_tensor(tmp[i][:, :], src[:, o:o + T], icnt[:, g, :], ALU.mult),
                  t, ictok, was(f"tmp{i}"))
            use("sa0", t)
            use("sa1", t)
            t = V(lambda e, c=c, i=i: e.tensor_tensor(tmp[i][:, :], tmp[i][:, :], xp[:, c, 8:T + 8], ALU.subtract), t)
            a = S(lambda e, c=c, i=i: e.copy(xh[:, c, :], tmp[i][:, :]), t, after)
            b = V(lambda e, c=c, i=i: e.tensor_tensor(xl[:, c, :], tmp[i][:, :], xh[:, c, :].bitcast(F32), ALU.subtract), a)
            use(f"tmp{i}", a, b)
            pooled.append([a, b])
        hi, lo, wt, done = w_next()
        for c in range(NC):
            g = c // 2
            bank = c % 4
            for k in range(2):
                t = mm3(pb[bank], hi[:, 2 * g + k, (c % 2) * P:(c % 2 + 1) * P], lo[:, 2 * g + k, (c % 2) * P:(c % 2 + 1) * P],
                        xh[:, 2 * g + k, :], xl[:, 2 * g + k, :], k == 0, k == 1, wt, pooled[2 * g + k],
                        bf[bank] if k == 0 else None)
            residual(c, bank, cf[:, 40 + c:41 + c], t, f2g)
        done(t)
        pst.close()
        f3 = factors(32, v_("gf1", 0, 8), ada[1], 4, [adatok[("m", 1, 4)], adatok[("m", 1, 3)]])
        xn = norm(xT, T, lambda c: cf[:, 32 + c:33 + c], lambda c: ada[1][:, 24 + c:25 + c], xh, xl, fence(), f3, then=ACT.Silu)
        ffn(lambda c: ada[1][:, 40 + c:41 + c], adatok[("m", 1, 5)], xn, fence())

        r = rstd_of(free["ss"], T)
        for c in range(NC):
            xtok[c] = V(lambda e, c=c: e.scalar_tensor_tensor(out=xT[:, c, :], in0=xT[:, c, :], scalar=v_("fin", c),
                                                              in1=pb[6], op0=ALU.mult, op1=ALU.mult), r, xtok[c])
            square_in(c, xT[:, c, :], T, xtok[c])
        bf[6] = [xtok[NC - 1]]

        xn = norm(xT, T, lambda c: v_("n1", c), None, xh, xl, fence(), ctok, then=ACT.Silu)
        ffn(lambda c: k_("half"), ctok, xn, fence())

        n2 = ExitStack()
        w2c = acc[:, 0:512].rearrange("p (z c n) -> p z c n", z=2, c=2)
        b2c = acc[:, 512:1024]
        C2 = sb("C2", [P, T], F32, n2)
        S2 = sb("S2", [P, T], F32, n2)
        q2 = sb("q2", [P, 4, T], F32, n2)
        ksT = sb("ksT", [P, 2, T], F32, n2)
        kwT = sb("kwT", [P, 2, T], F32, n2)
        v2s = sb("v2s", [P, 4, 256], F32, n2)
        v2w = sb("v2w", [P, 4, 256], F32, n2)
        gts = sb("gts", [P, 4, 24], F32, n2)
        qsT = sb("qsT", [P, 4, T], F32, n2)
        ksbT = sb("ksbT", [P, 4, T], F32, n2)
        vsb = sb("vsb", [P, 4, T], F32, n2)
        kcC = sb("kcC", [P, 2 * NCMP], F32, n2)
        vcC = sb("vcC", [32, 256], F32, n2)
        hid = sb("hid", [P, 2, 2 * NCMP], F32, n2)
        n3 = ExitStack()
        kcr = sb("kcr", [P, 2, T], F32, n3)
        kb = sb("kb", [P, 16, 2 * NCMP], F32, n3)
        kbh = sb("kbh", [P, 16, 2 * NCMP], F32R, n3)
        kbl = sb("kbl", [P, 16, 2 * NCMP], F32R, n3)
        after2 = fence()
        b2tok = [load(G, "b2c", b2c[:, :], A["b2c"], after2)]
        w2tok = []
        for z, name in ((0, "cmp_w2_k_2"), (1, "cmp_w2_v_2")):
            for y in range(2):
                w2tok = [load(G, "w2c", w2c[:, z, :, y * 64:(y + 1) * 64],
                              A[name][0].rearrange("(c p) n -> p c n", p=P), after2)]

        def b2(name, w=128):
            return b2c[:, B2C[name]:B2C[name] + w]

        posi = kb[:, :, :].rearrange("p a b -> p (a b)")[:, 0:T].bitcast(I32)
        ang = kcr[:, 0, :]
        ni = kcr[:, 1, :].bitcast(I32)
        nf = C2[:, :]
        t = load(G, "pos", posi, A["positions_2"].partition_broadcast(P).rearrange("p a t -> p (a t)"), after2)
        t = V(lambda e: e.tensor_copy(ang, posi), t, after2)
        t = V(lambda e: e.tensor_scalar(ang, ang, k_("freq"), None, ALU.mult), t)
        for parts in turns():
            t = V(lambda e, parts=parts: e.tensor_scalar(ni, ang, float(parts[0]), None, ALU.mult), t)
            t = V(lambda e: e.tensor_copy(nf, ni), t)
            for p in parts[1:]:
                t = V(lambda e, p=p: e.scalar_tensor_tensor(out=ang, in0=nf, scalar=-float(p), in1=ang,
                                                            op0=ALU.mult, op1=ALU.add), t)
        pi = float(np.float32(3.1415925))
        t = V(lambda e: e.tensor_scalar(ang, ang, pi, -pi, ALU.min, ALU.max), t)
        s2t = S(lambda e: e.activation(S2[:, :], ang, ACT.Sin), t)
        t = V(lambda e: e.tensor_scalar(C2[:, :], ang, float(np.pi / 2), None, ALU.add), t)
        t = V(lambda e: e.tensor_scalar(kcr[:, 1, :], C2[:, :], pi, float(-2 * np.pi), ALU.is_gt, ALU.mult), t)
        t = V(lambda e: e.tensor_tensor(C2[:, :], C2[:, :], kcr[:, 1, :], ALU.add), t)
        t = V(lambda e: e.tensor_scalar(C2[:, :], C2[:, :], pi, -pi, ALU.min, ALU.max), t, s2t)
        c2t = S(lambda e: e.activation(C2[:, :], C2[:, :], ACT.Sin), t)
        cst2 = [s2t, c2t]

        xn = norm(xT, T, lambda c: v_("mixg", c), None, xh, xl, after2, ctok)

        def qk_job(bank, tok, gain, scale, dst, res, sq, n=T, cos=None, sin=None, then=None):
            a = S(lambda e: e.copy(dst, pb[bank][:, 0:n]), tok, after2)
            b = S(lambda e: e.activation(tmp[sq][:, 0:n], pb[bank][:, 0:n], ACT.Square), tok, was(f"tmp{sq}"))
            bf[bank] = [a, b]
            yield
            mid = []
            yield from head_norm(dst, [a, b], sq, gain, n, dst, mid)
            if cos is None:
                rope(dst, mid, C2[:, :], S2[:, :], b2("rot"), scale, dst, 5, [b2tok, cst2], res)
            else:
                for j in range(2):
                    part = dst[:, j * NCMP:(j + 1) * NCMP]
                    rope(part, mid, cos, sin, b2("rot"), scale, part, 5, [b2tok, cst2], res, n=NCMP)
            if then:
                then()

        q2t = []
        for u in range(2):
            hi, lo, wt, done = w_next()
            ts = proj2((0, 1), hi, lo, wt, xh, xl, xn) if u == 0 else None
            for cc in range(2):
                c = 2 * u + cc
                t = ts[cc] if ts else proj(c, hi, lo, cc * P, wt, xh, xl, xn)
                advance()
                start(qk_job(c, t, v_("gq"), 0.125, q2[:, c, :], q2t, cc))
            done(t)
        hi, lo, wt, done = w_next()
        kcrt = []
        for z in range(2):
            t = proj(z, hi, lo, z * P, wt, xh, xl, xn)
            advance()
            a = S(lambda e, z=z: e.copy(kcr[:, z, :], pb[z]), t, cst2)
            bf[z] = [a]
            kcrt.append(a)
        done(t)
        for z in range(2):
            bt = []
            for j in range(2):
                rows = slice(j * 64, (j + 1) * 64)
                for par in range(2):
                    for hh_ in range(2):
                        src = kcr[rows, z, hh_ * 16:hh_ * 16 + 496].rearrange("p (n l two) -> p two l n", n=NCMP, two=2)
                        o = VEC["pev" if z else "pek"][0] + par * 16 + hh_ * 8
                        pe = vec[rows, o:o + 8].unsqueeze(2).broadcast_to([64, 8, NCMP])
                        dst = kb[par * 64:(par + 1) * 64, hh_ * 8:hh_ * 8 + 8, j * NCMP:(j + 1) * NCMP]
                        bt.append(V(lambda e, dst=dst, src=src, par=par, pe=pe: e.tensor_tensor(dst, src[:, par], pe, ALU.add),
                                    kcrt[z], was("kb"), cst2))
            a = S(lambda e: e.copy(kbh[:, :, :], kb[:, :, :]), bt, was("kbh"))
            b = V(lambda e: e.tensor_tensor(kbl[:, :, :], kb[:, :, :], kbh[:, :, :].bitcast(F32), ALU.subtract), a, was("kbh"))
            use("kb", a, b)
            for u in range(2):
                hi, lo, wt, done = w_next()
                for f in range(2):
                    for k in range(8):
                        t = mm3(pb[2 + f][:, 0:2 * NCMP], hi[:, k, f * P:(f + 1) * P], lo[:, k, f * P:(f + 1) * P],
                                kbh[:, 8 * u + k, :], kbl[:, 8 * u + k, :], u == 0 and k == 0, u == 1 and k == 7,
                                wt, [a, b], bf[2 + f] if u == 0 and k == 0 else None)
                done(t)
                advance()
            use("kbh", t)
            ge = []
            for f in range(2):
                x = S(lambda e, f=f: e.activation(hid[:, f, :], pb[2 + f][:, 0:2 * NCMP], ACT.Gelu_apprx_tanh), t,
                      was("hid"), after2)
                bf[2 + f] = [x]
                ge.append(x)
            if z == 0:
                for f in range(2):
                    m = M(lambda e, f=f: e.matmul(pb[0][:, 0:2 * NCMP], w2c[:, 0, f, :], hid[:, f, :], start=f == 0,
                                                  stop=f == 1), ge, w2tok, bf[0])
                use("hid", m)
                kct2 = []
                start(qk_job(0, m, v_("gkc"), 1.0, kcC[:, :], kct2, 0, 2 * NCMP, C2[:, 31:T:16], S2[:, 31:T:16]))
            else:
                vct2 = []
                for j in range(2):
                    for f in range(2):
                        m = M(lambda e, f=f, j=j: e.matmul(pb[1][0:NCMP, j * P:(j + 1) * P], hid[:, f, j * NCMP:(j + 1) * NCMP],
                                                           w2c[:, 1, f, :], start=f == 0, stop=f == 1), ge, w2tok, bf[1])
                vct2 = [S(lambda e: e.copy(vcC[0:NCMP, :], pb[1][0:NCMP, 0:256]), m)]
                bf[1] = vct2

        hi, lo, wt, done = w_next()
        t = proj(0, hi, lo, 0, wt, xh, xl, xn)
        advance()
        kst2, kwt2 = [], []
        start(qk_job(0, t, v_("gks"), 1.0, ksT[:, 0, :], kst2, 0,
                     then=lambda: kst2.append(swap(ksT[:, 1, :], ksT[:, 0, :], "ksT", list(kst2)))))

        def tok_v(dst, c0):
            toks = []
            for tb in range(4):
                bank = 2 + tb % 2
                t = proj_tok(bank, hi, lo, c0, P, wt, xh, xl, xn, tb)
                if tb == 3:
                    advance()
                a = S(lambda e, tb=tb, bank=bank: e.copy(dup(dst[:, tb, :]), twice(bank)), t, after2)
                bf[bank] = [a]
                toks.append(a)
            return toks, t

        v2st, t = tok_v(v2s, P)
        done(t)
        hi, lo, wt, done = w_next()
        t = proj(1, hi, lo, 0, wt, xh, xl, xn)
        done(t)
        advance()
        start(qk_job(1, t, v_("gkw"), 1.0, kwT[:, 0, :], kwt2, 1,
                     then=lambda: kwt2.append(swap(kwT[:, 1, :], kwT[:, 0, :], "kwT", list(kwt2)))))
        hi, lo, wt, done = w_next()
        v2wt, t = tok_v(v2w, 0)
        gtt = []
        for tb in range(4):
            t = proj_tok(4, hi, lo, P, 24, wt, xh, xl, xn, tb, tb * 24)
        gtt = [S(lambda e: e.activation(gts[:, :, :], pb[4][:, 0:96].rearrange("p (a b) -> p a b", a=4), ACT.Sigmoid), t, after2)]
        bf[4] = gtt
        done(t)
        qst, ksbt = [], []
        for u in range(4):
            hi, lo, wt, done = w_next()
            for cc in range(2):
                c = 2 * (u % 2) + cc
                t = proj(cc, hi, lo, cc * P, wt, xh, xl, xn)
                advance()
                if u < 2:
                    a = S(lambda e, c=c, cc=cc: e.mul(qsT[:, c, :], pb[cc], 0.125), t, after2)
                    qst.append(a)
                else:
                    a = S(lambda e, c=c, cc=cc: e.copy(ksbT[:, c, :], pb[cc]), t, after2)
                    ksbt.append(a)
                bf[cc] = [a]
            done(t)
        vsbt = []
        for u in range(2):
            hi, lo, wt, done = w_next()
            for tb in range(4):
                bank = 2 + tb % 2
                t = proj_tok(bank, hi, lo, 0, 256, wt, xh, xl, xn, tb)
                a = S(lambda e, tb=tb, bank=bank, u=u: e.copy(vsb[:, tb, u * 256:(u + 1) * 256], pb[bank][:, 0:256]), t, after2)
                bf[bank] = [a]
                vsbt.append(a)
            done(t)
        xlast = t
        drain()
        n3.close()
        n3 = ExitStack()
        pr2 = sb("pr2", [P, 2, 4, T], F32, n3)
        pt2 = sb("pt2", [P, 2, 4 * T], F32, n3)
        after3 = fence()
        use("prob0", *after3)
        use("prob1", *after3)
        use("pt0", *after3)
        use("pt1", *after3)
        mixt = [[] for _ in range(NC)]

        def nsa():
            jobs = [(i, j, br) for i in range(4) for j in range(2) for br in range(3)]

            def a_stage(n_, i, j, br):
                par = seq["n"] % 2
                width = NCMP if br == 0 else (i + 1) * P

                def qk(g):
                    h = 4 * j + g
                    r = slice((h % 2) * 64, (h % 2) * 64 + 64)
                    q = q2[r, h // 2, i * P:(i + 1) * P]
                    if br == 0:
                        return [(q, kcC[r, j * NCMP:(j + 1) * NCMP], 0, NCMP)]
                    kk = ksT if br == 1 else kwT
                    sw = 0 if h % 2 == j else 1
                    full = [(q, kk[r, sw, 0:i * P], 0, i * P)] if i else []
                    return full + [(q, kk[r, sw, i * P:(i + 1) * P], i * P, P)]

                masks = [(0, NCMP, b_("cmp", NCMP, 32 * i))] if br == 0 else [(i * P, P, b_("diag"))]
                gate = gts[:, i, :].rearrange("p (j g b) -> p j b g", j=2, g=4)[:, j, br]
                return soft_a(4, qk, masks, width, lambda g: g * 512, pr2[:, par, :, :],
                              [q2t, kct2, kst2, kwt2], gate=gate, gtok=gtt,
                              valid=k_("valid") if br == 0 and i == 0 else None)

            def values(i, j, br):
                if br == 0:
                    return [(0, NCMP, vcC[0:NCMP, j * P:(j + 1) * P], vct2)]
                v, vtk = (v2s, v2st) if br == 1 else (v2w, v2wt)
                return [(b * P, P, v[:, b, j * P:(j + 1) * P], vtk[b]) for b in range(i + 1)]

            def b_stage(n, i, j, br, got):
                par, tok = got
                return soft_b(4, pr2[:, par, :, :], tok, par, values(i, j, br), pt2[:, par, :])

            def c_stage(n, i, j, br, got):
                (par, tok), evs = got
                ob = 6 + (2 * i + j) % 2
                t = soft_c(4, evs, par, values(i, j, br), pt2[:, par, :], ob, br == 0, br == 2)
                if br == 2:
                    last = []
                    for o in range(2):
                        r = slice(o * 64, o * 64 + 64)
                        cols = slice(i * P, (i + 1) * P)
                        src = pb[ob][r, :].rearrange("p (a o q) -> p o a q", o=2, q=P)[:, o]
                        tk = put(ob, r, src, xh[r, 2 * j:2 * j + 2, cols], xl[r, 2 * j:2 * j + 2, cols], t, 2 * j)
                        mixt[2 * j + 1] += tk
                        last += tk
                    bf[ob] = last

            pipeline(jobs, a_stage, b_stage, c_stage)

        nsa()
        n3.close()
        n3 = ExitStack()
        ze = sb("ze", [P, 1536], F32, n3)
        zs = sb("zs", [P, 2, 1536], F32, n3)
        za = sb("za", [P, 2, 1536], F32, n3)
        after4 = fence()
        ZC = [0, 512, 1024, 896]
        ZW = [512, 384, 256, 128]

        def stick():
            def a_stage(n, h):
                base = 3 * (h % 2)
                r = slice((h % 2) * 64, (h % 2) * 64 + 64)
                c = h // 2
                zo = base * 512
                banks = [base, base + 1, base + 2]
                for b in range(4):
                    m = M(lambda e, b=b: e.matmul(
                        ps[:, zo + ZC[b]:zo + ZC[b] + ZW[b]], ksbT[r, c, b * P:(b + 1) * P], qsT[r, c, b * P:T],
                        start=b < 3, stop=False, skip_group_check=True), qst, ksbt, [bf[x] for x in banks])
                zz = ps[:, zo:zo + 1280]
                par = h % 2
                e1 = S(lambda e: e.activation(ze[:, 0:1280], zz, ACT.Abs), m, was("ze"), after4)
                e1 = S(lambda e: e.activation(ze[:, 0:1280], ze[:, 0:1280], ACT.Exp, scale=-1.0), e1)
                e1 = S(lambda e: e.activation(ze[:, 0:1280], ze[:, 0:1280], ACT.Ln, bias=k_("one")), e1)
                s_ = V(lambda e: e.scalar_tensor_tensor(out=zs[:, par, 0:1280], in0=zz, scalar=0.0, in1=ze[:, 0:1280],
                                                        op0=ALU.max, op1=ALU.add), e1, was(f"zs{par}"), after4)
                use("ze", s_)
                return s_, [V(lambda e, b=b: e.tensor_tensor(zs[:, par, ZC[b]:ZC[b] + P], zs[:, par, ZC[b]:ZC[b] + P],
                                                             b2("sb01"), ALU.mult), s_, b2tok) for b in range(4)]

            def b_stage(n, h, got):
                s_, ms = got
                base = 3 * (h % 2)
                zo = base * 512
                par = h % 2
                for b in range(4):
                    for jb in range(b, 4):
                        M(lambda e, b=b, jb=jb: e.matmul(
                            ps[:, zo + ZC[b] + (jb - b) * P:zo + ZC[b] + ZW[b]], b2("tri") if jb == b else b2("neg1"),
                            zs[:, par, ZC[jb]:ZC[jb] + ZW[jb]], start=False, stop=False, skip_group_check=True), ms)
                    m = M(lambda e, b=b: e.matmul(ps[:, zo + ZC[b]:zo + ZC[b] + P], b_("ident"), b_("sbm"),
                                                  start=False, stop=True, skip_group_check=True))
                use(f"zs{par}", m)
                x = S(lambda e: e.activation(za[:, par, 0:1280], ps[:, zo:zo + 1280], ACT.Exp), m, was(f"za{par}"), after4)
                for k in range(base, base + 3):
                    bf[k] = [x, s_]
                return x

            def c_stage(n, h, got):
                par = h % 2
                ob = 6 + par
                r = slice((h % 2) * 64, (h % 2) * 64 + 64)
                c = h // 2
                for b in range(4):
                    t = M(lambda e, b=b: e.matmul(pb[ob][:, b * P:T], vsb[:, b, c * P:(c + 1) * P],
                                                  za[:, par, ZC[b]:ZC[b] + ZW[b]], start=b == 0, stop=b == 3,
                                                  skip_group_check=True), got[1], vsbt, bf[ob] if b == 0 else None)
                use(f"za{par}", t)
                bf[ob] = put(ob, r, pb[ob][r, :], xh[r, 4 + c, :], xl[r, 4 + c, :], t, 4 + c)

            pipeline([(h,) for h in range(8)], a_stage, b_stage, c_stage)

        stick()
        mix_out(lambda c: k_("one"), ctok)
        n3.close()
        n2.close()

        m2 = ExitStack()
        qm = sb("qm", [P, 2, T], F32, m2)
        pr3 = sb("pr3", [P, 2, 4, LC], F32, m2)
        pt3 = sb("pt3", [P, 2, 2 * T], F32, m2)
        oh = sb("oh", [P, 2, T], F32R, m2)
        ol = sb("ol", [P, 2, T], F32R, m2)
        after5 = fence()
        xn = norm(xT, T, lambda c: v_("memx", c), None, xh, xl, after5, ctok)
        hi, lo, wt, done = w_next()
        qmt = []

        def qm_job(c, t):
            a = S(lambda e: e.copy(qm[:, c, :], pb[c]), t, after5)
            q = S(lambda e: e.activation(tmp[c][:, :], pb[c], ACT.Square), t, was(f"tmp{c}"))
            bf[c] = [a, q]
            yield
            yield from head_norm(qm[:, c, :], [a, q], c, v_("gmq"), T, qm[:, c, :], qmt)

        ts = proj2((0, 1), hi, lo, wt, xh, xl, xn)
        for c in range(2):
            start(qm_job(c, ts[c]))
        done(ts[1])
        drain()
        use("prob0", *after5)
        use("prob1", *after5)
        use("pt0", *after5)
        use("pt1", *after5)
        omt = [[], []]

        def memory():
            def a_stage(n, i):
                par = seq["n"] % 2

                def qk(g):
                    r = slice((g % 2) * 64, (g % 2) * 64 + 64)
                    return [(qm[r, g // 2, i * P:(i + 1) * P], kmT[r, g // 2, :], 0, LC)]

                return soft_a(4, qk, [], LC, lambda g: g * 512, pr3[:, par, :, :], [qmt, kmtok])

            def b_stage(n, i, got):
                par, tok = got
                return soft_b(4, pr3[:, par, :, :], tok, par, [(b * P, P, None, None) for b in range(2)], pt3[:, par, :])

            def c_stage(n, i, got):
                (par, tok), evs = got
                for c in range(2):
                    ob = 6 + c
                    for b in range(2):
                        t = M(lambda e, b=b, c=c, ob=ob: e.matmul(
                            pb[ob][:, 0:256], vm[:, b, c * P:(c + 1) * P], pt3[:, par, b * T + c * 256:b * T + (c + 1) * 256],
                            start=b == 0, stop=b == 1), evs[b], vmtok, bf[ob] if b == 0 else None)
                    last = []
                    for o in range(2):
                        r = slice(o * 64, o * 64 + 64)
                        cols = slice(i * P, (i + 1) * P)
                        src = pb[ob][r, o * P:(o + 1) * P]
                        a = S(lambda e, r=r, c=c, cols=cols, src=src: e.copy(oh[r, c, cols], src), t, after5)
                        b_ = V(lambda e, r=r, c=c, cols=cols, src=src: e.tensor_tensor(
                            ol[r, c, cols], src, oh[r, c, cols].bitcast(F32), ALU.subtract), a)
                        last += [a, b_]
                    omt[c] += last
                    bf[ob] = last
                use(f"pt{par}", t)

            pipeline([(i,) for i in range(4)], a_stage, b_stage, c_stage)

        qmt = [V(lambda e: e.tensor_scalar(qm[:, :, :], qm[:, :, :], 0.125, None, ALU.mult), qmt)]
        memory()
        hi, lo, wt, done = w_next()
        for c in range(NC):
            t = proj(c % 2, hi, lo, c * P, wt, oh, ol, lambda k: omt[k], 2)
            residual(c, c % 2, k_("one"), t, ctok)
        done(t)
        m2.close()

        xn = norm(xT, T, lambda c: v_("n2", c), None, xh, xl, fence(), ctok, then=ACT.Silu)
        ov = out.rearrange("(c p) t -> p c t", p=P)
        outs = []

        def store(c, tok):
            outs.append(load(SP, "out", ov[:, c, :], xT[:, c, :], tok))

        ffn(lambda c: k_("half"), ctok, xn, fence(), keep=False, final=store)
        SP(lambda e: e.nop(), outs[-1])

        for q in (V, S, G, M, SP):
            q.number()
        block = ctx.enter_context(nc.Block())

        @block.sync
        def _(eng):
            SP.emit(eng)

        @block.gpsimd
        def _(eng):
            G.emit(eng)

        @block.scalar
        def _(eng):
            S.emit(eng)

        @block.vector
        def _(eng):
            V.emit(eng)

        @block.tensor
        def _(eng):
            M.emit(eng)


def parts_of(x, bits, n):
    out, rest = [], float(x)
    for _ in range(n - 1):
        m, e = np.frexp(rest)
        p = float(np.ldexp(np.floor(m * 2 ** bits), int(e) - bits))
        out.append(p)
        rest -= p
    return out + [rest]


def turns():
    return [[1.0 / (2 * np.pi * n)] + parts_of(2 * np.pi * n, 11, 3) for n in (4096, 1)]


def constants():
    f = np.float32
    r = np.arange(P)
    cst = np.zeros((P, NCST), f)
    cst[:, 0:128] = np.eye(P)
    cst[:, 128:256] = 1
    cst[:, 256:384] = (r[:, None] // 64) == (r[None] // 64)
    cst[:, CST["eps"]] = EPS
    cst[:, CST["one"]] = 1
    cst[:, CST["half"]] = 0.5
    freq = (np.float64(500000.0) ** (-np.arange(0, 16, 2, dtype=np.float32).astype(np.float64) / 16)).astype(f)
    d = r % 64
    cst[:, CST["freq"]] = np.where(d < 16, freq[d % 8], 0)
    cst[:, CST["valid"]] = r >= 31
    masks = np.zeros((P, NBCS), f)
    q, k = r[:, None], r[None]
    masks[:, 0:128] = np.eye(P)
    masks[:, BCS["diag"]:][:, :128] = np.where(k <= q, 0, NEG)
    masks[:, BCS["prev"]:][:, :128] = np.where(k >= q, 0, NEG)
    masks[:, BCS["sbm"]:][:, :128] = np.where(q < k, 0, NEG)
    for i in range(4):
        ends = np.arange(NCMP) * 16 + 31
        masks[:, BCS["cmp"] + 32 * i:][:, :NCMP] = np.where(ends[None] <= q + i * P, 0, NEG)
    b1 = np.zeros((P, NB1C), f)
    rot = np.zeros((P, P), f)
    rot[r[1::2], r[0::2]] = -1
    rot[r[0::2], r[1::2]] = 1
    b1[:, 0:128] = rot
    t = np.arange(T)
    inv = (np.float64(10000.0) ** (-np.arange(16, dtype=np.float64) / 16)).astype(f)
    ang = np.concatenate([(t // 64).astype(f)[:, None] * inv[None], (t % 64).astype(f)[:, None] * inv[None]], 1)
    ang = np.repeat(ang.T, 2, axis=0)
    ang = np.concatenate([ang, ang], 0).astype(np.float64)
    b1[:, 128:640] = np.cos(ang)
    b1[:, 640:1152] = np.sin(ang)
    w = 2 * np.pi * (np.outer(r, r) % P) / P
    b1[:, 1152:1280] = np.cos(w) / np.sqrt(P)
    b1[:, 1280:1408] = np.sin(w) / np.sqrt(P)
    w = 2 * np.pi * (np.outer(t, t) % T) / T
    cn, sn = np.cos(w) / np.sqrt(T), -np.sin(w) / np.sqrt(T)
    b1[:, B1C["cn"]:][:, :2048] = cn.reshape(4, P, T).transpose(1, 0, 2).reshape(P, 2048)
    b1[:, B1C["sn"]:][:, :2048] = sn.reshape(4, P, T).transpose(1, 0, 2).reshape(P, 2048)
    b2 = np.zeros((P, NB2C), f)
    rot = np.zeros((P, P), f)
    for o in (0, 64):
        for i in range(8):
            rot[o + 8 + i, o + i] = -1
            rot[o + i, o + 8 + i] = 1
    b2[:, 0:128] = rot
    b2[:, 128:256] = -(q >= k).astype(f)
    b2[:, 256:384] = -1
    b2[:, 384:512] = q < k
    cnt = np.stack([np.minimum(t + n // 2, T) - np.maximum(t - n // 2, 0) for n in (2, 4, 8, 16)])
    icnt = np.broadcast_to((1.0 / cnt).astype(f)[None], (P, 4, T))
    return {"consts": cst, "masks": masks, "b1c": b1, "b2c": b2, "icnt": np.ascontiguousarray(icnt)}


_WEIGHTS = ["ada_w", "mix_in_w", "mix_out_w", "pool_w", "ffn_w1", "ffn_w3", "ffn_w2", "positions_2", "ffn1_wg_2",
            "ffn1_wu_2", "ffn1_wd_2", "w_in_2", "cmp_w1_k_2", "cmp_w2_k_2", "cmp_w1_v_2", "cmp_w2_v_2", "w_out_2",
            "mem_wq_2", "mem_wk_2", "mem_wv_2", "mem_wo_2", "ffn2_wg_2", "ffn2_wu_2", "ffn2_wd_2"]


def kernel(**inputs):
    import concourse.bacc as bacc
    from concourse.bass_utils import run_bass_kernel_spmd

    a = {k: np.asarray(v) for k, v in inputs.items()}

    def col(v):
        return np.asarray(v).reshape(-1, P).T

    def two(v):
        return np.concatenate([v.reshape(64, 1)] * 2, 0)

    def pe(v):
        w = v.reshape(16, 2, 64).transpose(2, 1, 0).reshape(64, 32)
        return np.concatenate([w, w], 0)

    vecs = {
        "c": col(a["c"]), "cc": col(a["c_ctx"]), "ab0": col(a["ada_b"][0]), "ab1": col(a["ada_b"][1]),
        "gm0": col(a["norm_mix_g"][0]), "gm1": col(a["norm_mix_g"][1]),
        "gf0": col(a["norm_ffn_g"][0]), "gf1": col(a["norm_ffn_g"][1]),
        "pscale": col(a["pool_scale"]), "fin": col(a["final_g"]), "n1": col(a["ffn1_norm_2"]),
        "mixg": col(a["mix_norm_2"]), "memx": col(a["mem_x_norm_2"]), "memkv": col(a["mem_kv_norm_2"]),
        "n2": col(a["ffn2_norm_2"]), "gq": two(a["nsa_q_norm_2"]), "gkc": two(a["nsa_kc_norm_2"]),
        "gks": two(a["nsa_ks_norm_2"]), "gkw": two(a["nsa_kw_norm_2"]), "gmq": two(a["mem_q_norm_2"]),
        "gmk": two(a["mem_k_norm_2"]), "sink": np.broadcast_to(a["attn_sink"].reshape(1, 8), (P, 8)),
        "pek": pe(a["cmp_pos_k_2"]), "pev": pe(a["cmp_pos_v_2"]),
    }
    arrays = {n: np.ascontiguousarray(a[n]) for n in _WEIGHTS}
    arrays["vecs"] = np.ascontiguousarray(np.concatenate([vecs[n] for n in VEC], 1))
    arrays["xT"] = np.ascontiguousarray(a["x"][0].T)
    arrays["ctxT"] = np.ascontiguousarray(a["ctx"][0].T)
    arrays["memT"] = np.ascontiguousarray(a["mem_2"][0].T)
    arrays.update(constants())
    nc = bacc.Bacc("TRN2", target_bir_lowering=False, num_devices=1)
    ins = {n: nc.dram_tensor("in_" + n, v.shape, mybir.dt.from_np(v.dtype), kind="ExternalInput").ap()
           for n, v in arrays.items()}
    out = nc.dram_tensor("out", (D, T), F32, kind="ExternalOutput").ap()
    program(nc, ins, out)
    r = run_bass_kernel_spmd(nc, [{"in_" + n: v for n, v in arrays.items()}], core_ids=[0])
    return np.ascontiguousarray(r.results[0]["out"].T)[None]
```

```python
from contextlib import ExitStack

import numpy as np

import concourse.bass as bass
from concourse import mybir

ALU = mybir.AluOpType
ACT = mybir.ActivationFunctionType
AXX = mybir.AxisListType.X
F32 = mybir.dt.float32
F32R = mybir.dt.float32r
BF16 = mybir.dt.bfloat16
I32 = mybir.dt.int32

P = 128
T = 512
NC = 8
D = 1024
FF = 2816
NF = FF // P
LC = 256
NCMP = 31
SLOT = 2048
NEG = -1e30
EPS = 1e-6


class Tok:

    def __init__(self, sem, value=None):
        self.sem, self.value, self.used = sem, value, value is not None


class Queue:

    def __init__(self, sem):
        self.sem, self.ops, self.last = sem, [], None

    def __call__(self, fn, *after):
        tok = Tok(self.sem)
        need = []
        stack = list(after)
        while stack:
            x = stack.pop()
            if isinstance(x, Tok):
                x.used = True
                need.append(x)
            elif x:
                stack.extend(x)
        self.ops.append((fn, need, tok))
        self.last = tok
        return tok

    def number(self):
        n = 0
        for _, _, tok in self.ops:
            if tok.used and tok.value is None:
                n += 1
                tok.value = n

    def emit(self, eng):
        seen = {}
        for fn, need, tok in self.ops:
            most = {}
            for x in need:
                most[x.sem] = max(most.get(x.sem, 0), x.value)
            for sem, value in most.items():
                if seen.get(sem, 0) < value:
                    eng.wait_ge(sem, value)
                    seen[sem] = value
            ins = fn(eng)
            if tok.used and tok.sem is self.sem:
                ins.then_inc(self.sem, 1)


VEC = {}
_at = 0
for _n, _w in (("c", 8), ("cc", 8), ("ab0", 48), ("ab1", 48), ("gm0", 8), ("gm1", 8), ("gf0", 8), ("gf1", 8),
               ("pscale", 8), ("fin", 8), ("n1", 8), ("mixg", 8), ("memx", 8), ("memkv", 8), ("n2", 8),
               ("gq", 1), ("gkc", 1), ("gks", 1), ("gkw", 1), ("gmq", 1), ("gmk", 1), ("sink", 8),
               ("pek", 32), ("pev", 32)):
    VEC[_n] = (_at, _w)
    _at += _w
NVEC = _at

CST = {"ident": 0, "ones": 128, "bd": 256, "eps": 384, "one": 385, "freq": 386, "valid": 387, "zero": 388, "half": 389}
NCST = 390
BCS = {"ident": 0, "diag": 128, "prev": 256, "sbm": 384, "cmp": 512}
NBCS = 512 + 4 * 32
B1C = {"rot": 0, "cos": 128, "sin": 640, "cd": 1152, "cn": 1408, "sn": 1408 + 2048}
NB1C = 1408 + 4096
B2C = {"rot": 0, "tri": 128, "neg1": 256, "sb01": 384}
NB2C = 512


def program(nc, A, out):
    ctx = ExitStack()
    with ctx:
        def sem(name):
            return ctx.enter_context(nc.semaphore(name))

        V, S, G, M = (Queue(sem(n)) for n in ("s_vec", "s_act", "s_pool", "s_pe"))
        SP = Queue(sem("s_sp"))
        dsem = {}

        def load(q, key, dst, src, *after):
            if key not in dsem:
                dsem[key] = [sem("d_" + key), 0]
            s = dsem[key]
            s[1] += 16
            sm, val = s[0], s[1]
            last = q.last
            q(lambda e: e.dma_start(dst, src).then_inc(sm, 16), *after)
            q.last = last
            return Tok(sm, val)

        def sb(name, shape, dt=F32, stack=ctx):
            return stack.enter_context(nc.sbuf_tensor(name, shape, dt))

        ps = ctx.enter_context(nc.psum_tensor("ps", [P, 8 * 512], F32))
        pb = [ps[:, i * 512:(i + 1) * 512] for i in range(8)]
        bf = [[] for _ in range(8)]

        xT = sb("xT", [P, NC, T])
        xh = sb("xh", [P, NC, T], F32R)
        xl = sb("xl", [P, NC, T], F32R)
        raw = [sb(f"raw{i}", [P, SLOT]) for i in range(2)]
        wh = [sb(f"wh{i}", [P, SLOT], F32R) for i in range(2)]
        wl = [sb(f"wl{i}", [P, SLOT], F32R) for i in range(2)]
        acc = sb("acc", [P, 1024])
        vec = sb("vec", [P, NVEC])
        cst = sb("cst", [P, NCST])
        bcs = sb("bcs", [P, NBCS], BF16)
        ada = [sb("ada0", [P, 48]), sb("ada1", [P, 48])]
        adac = sb("adac", [P, 16])
        sc = sb("sc", [P, 8, 2])
        cf = sb("cf", [P, 48])
        kmT = sb("kmT", [P, 2, LC])
        vm = sb("vm", [P, 2, LC])
        tmp = [sb(f"tmp{i}", [P, 512]) for i in range(4)]
        ssum = sb("ssum", [P, 512])
        sm = sb("sm", [P, 2, 16])
        hs = sb("hs", [P, 4, 8])
        dum = sb("dum", [P, 1])
        free = {}

        ident = cst[:, 0:128]
        ones = cst[:, 128:256]
        bd = cst[:, 256:384]

        def v_(name, c=0, w=1):
            return vec[:, VEC[name][0] + c:VEC[name][0] + c + w]

        def k_(name):
            return cst[:, CST[name]:CST[name] + 1]

        def b_(name, w=128, o=0):
            return bcs[:, BCS[name] + o:BCS[name] + o + w]

        def fence():
            return [q.last for q in (V, S, G, M) if q.last]

        units = []

        def w_unit(src, kc, cols):
            units.append(("w", src, kc, cols))

        def w_cols(w, c0, cols, k0=0, kc=NC):
            w_unit(w[k0 * P:(k0 + kc) * P, c0:c0 + cols].rearrange("(k p) n -> p k n", p=P), kc, cols)

        ada_w = A["ada_w"]

        def ada_unit(layer, j, k, kind="ada"):
            src = ada_w[layer, k * 256:(k + 1) * 256, j * 1024:(j + 1) * 1024]
            units.append((kind, src.rearrange("(k p) n -> p k n", p=P), layer, j, k))

        w_cols(A["mem_wk_2"][0], 0, 256)
        w_cols(A["mem_wv_2"][0], 0, 256)
        for k in range(2, 4):
            ada_unit(0, 1, k, "first")
        ada0 = [(0, j, k) for j in range(2, 6) for k in range(4)]
        for c in range(5):
            w_cols(A["mix_in_w"][0], c * 256, 256)
            if c:
                ada_unit(*ada0.pop(0))
        for _ in range(5):
            ada_unit(*ada0.pop(0))
        for c in range(4):
            if c:
                ada_unit(*ada0.pop(0))
            w_cols(A["mix_out_w"][0], c * 256, 256)

        def ffn_units(w1, w3, w2, extra=()):
            extra = list(extra)

            def between():
                if extra:
                    ada_unit(*extra.pop(0))

            for g in range(NF // 2):
                w_cols(w1, g * 256, 256)
                between()
                w_cols(w3, g * 256, 256)
                between()
            for g in range(4):
                for k0, kc in ((0, 8), (8, 7), (15, 7)):
                    w_cols(w2, g * 256, 256, k0, kc)
                    between()

        ffn_units(A["ffn_w1"][0], A["ffn_w3"][0], A["ffn_w2"][0],
                  ada0 + [(1, j, k) for j in range(6) for k in range(4)])
        w_unit(A["pool_w"][0].rearrange("g (c p) n -> p (g c) n", p=P), 8, 256)
        ffn_units(A["ffn_w1"][1], A["ffn_w3"][1], A["ffn_w2"][1])
        ffn_units(A["ffn1_wg_2"][0], A["ffn1_wu_2"][0], A["ffn1_wd_2"][0])
        wi2 = A["w_in_2"][0]
        for c0, cols in ((0, 256), (256, 256), (512, 256)):
            w_cols(wi2, c0, cols)
        cw = [(A[n][0], 0, 256, 8 * k) for n in ("cmp_w1_k_2", "cmp_w1_v_2") for k in range(2)]
        for c0, cols in ((768, 256), (1024, 128), (1152, 152), (1304, 256), (1560, 256), (1816, 256), (2072, 256),
                         (2328, 256), (2584, 256)):
            w_cols(wi2, c0, cols)
            if cw:
                w_cols(*cw.pop(0))
        for c in range(4):
            w_cols(A["w_out_2"][0], c * 256, 256)
        w_cols(A["mem_wq_2"][0], 0, 256)
        w_unit(A["mem_wo_2"][0].rearrange("(k p) n -> p k n", p=P), 2, 1024)
        ffn_units(A["ffn2_wg_2"][0], A["ffn2_wu_2"][0], A["ffn2_wd_2"][0])

        rawtok = {}
        rawfree = [[], []]
        ready = {}
        wdone = [[], []]
        st = {"dma": 0, "prep": 0, "w": 0, "use": 0}
        accdone = {"t": [], "a": [], "fin": []}
        adatok = {}
        worder = [i for i, u in enumerate(units) if u[0] == "w"]

        def dma_unit():
            u = st["dma"]
            if u >= len(units):
                return
            st["dma"] += 1
            src = units[u][1]
            kc, cols = src.shape[1], src.shape[2]
            dst = raw[u % 2][:, 0:kc * cols].rearrange("p (k n) -> p k n", k=kc)
            rawtok[u] = load(SP, f"raw{u % 2}", dst, src, rawfree[u % 2])

        def prep_unit():
            u = st["prep"]
            st["prep"] += 1
            r = raw[u % 2]
            if units[u][0] == "w":
                _, _, kc, cols = units[u]
                n, s = kc * cols, st["w"] % 2
                st["w"] += 1
                hi, lo = wh[s][:, 0:n], wl[s][:, 0:n]
                a = S(lambda e: e.copy(hi, r[:, 0:n]), rawtok[u], wdone[s])
                b = V(lambda e: e.tensor_tensor(lo, r[:, 0:n], hi.bitcast(F32), ALU.subtract), a, wdone[s])
                ready[u] = (s, [a, b])
                rawfree[u % 2] = [a, b]
            else:
                _, _, layer, j, k = units[u]
                if k == 0:
                    ada_flush()
                toks = []
                for kk in range(2):
                    kc = 2 * k + kk
                    w = r[:, kk * 1024:(kk + 1) * 1024]
                    col = sc[:, kc, 0:1]
                    if kc == 0:
                        t = V(lambda e, w=w, col=col: e.tensor_scalar(acc[:, :], w, col, None, ALU.mult),
                              rawtok[u], sctok, accdone["fin"])
                    else:
                        t = V(lambda e, w=w, col=col: e.scalar_tensor_tensor(
                            out=acc[:, :], in0=w, scalar=col, in1=acc[:, :], op0=ALU.mult, op1=ALU.add),
                            rawtok[u], adatok["acc"])
                    adatok["acc"] = t
                    toks.append(t)
                rawfree[u % 2] = toks
                if k == 3:
                    pending.append((layer, j))
            dma_unit()

        pending = []

        def ada_flush():
            while pending:
                ada_finish(*pending.pop(0))

        def ada_finish(layer, j):
            for c in range(8):
                t = M(lambda e, c=c: e.matmul(pb[7][:, c:c + 1], acc[:, c * P:(c + 1) * P], k_("one"),
                                              start=True, stop=True), adatok["acc"], bf[7], ctok)
            accdone["fin"] = [t]
            bias = v_("ab1" if layer else "ab0", j * 8, 8)
            t2 = V(lambda e: e.tensor_tensor(ada[layer][:, j * 8:j * 8 + 8], pb[7][:, 0:8], bias, ALU.add), t)
            bf[7] = [t2]
            adatok[("m", layer, j)] = t2

        def ada_step():
            if st["prep"] < len(units) and units[st["prep"]][0] == "ada":
                ada_flush()
                prep_unit()

        def ada_first(n):
            j, k = n // 4, n % 4
            w, wtok = (fb[n], fbtok[n]) if n < 6 else (raw[n - 6][:, :].rearrange("p (a b) -> p a b", a=2), rawtok[n - 4])
            for kk in range(2):
                for h in range(2):
                    t = M(lambda e, kk=kk, h=h: e.matmul(
                        pb[4][0:8, :], scp[:, 2 * j + h, 2 * k + kk, :], w[:, kk, h * 512:(h + 1) * 512],
                        start=n == 0 and kk == 0 and h == 0, stop=n == 5 and kk == 1 and h == 1), wtok, sctok)
            if n >= 6:
                rawfree[n - 6] = [t]
                st["prep"] += 1
                dma_unit()
            return t

        def ada_first_end(t):
            a = V(lambda e: e.tensor_copy(ssum[0:8, :], pb[4][0:8, :]), t, was("ssum"))
            bf[4] = [a]
            for c in range(4):
                m = M(lambda e, c=c: e.transpose(pb[4][:, c * 8:(c + 1) * 8], ssum[0:8, c * P:(c + 1) * P], cst[0:8, 0:8]),
                      a, bf[4], ctok)
            use("ssum", m)
            bf[4] = []
            for z, dst in ((0, ada[0]), (1, adac)):
                t2 = V(lambda e, z=z, dst=dst: e.tensor_tensor(
                    dst[:, 0:16].rearrange("p (q c) -> p q c", q=4),
                    pb[4][:, 0:32].rearrange("p (c q z) -> p z q c", c=4, z=2)[:, z],
                    v_("ab0", 0, 16).rearrange("p (q c) -> p q c", q=4), ALU.add), m)
                adatok[("first", z)] = t2
                bf[4] = bf[4] + [t2]

        def w_ahead():
            while st["prep"] <= worder[st["use"]] and units[st["prep"]][0] != "first":
                prep_unit()

        def w_next():
            u = worder[st["use"]]
            st["use"] += 1
            while st["prep"] <= u:
                prep_unit()
            s, toks = ready[u]
            kc, cols = units[u][2], units[u][3]
            hi = wh[s][:, 0:kc * cols].rearrange("p (k n) -> p k n", k=kc)
            lo = wl[s][:, 0:kc * cols].rearrange("p (k n) -> p k n", k=kc)

            if st["use"] < len(worder) and worder[st["use"]] - u <= 3:
                w_ahead()

            def done(tok):
                wdone[s] = [tok]
                ada_flush()

            return hi, lo, toks, done

        def mm3(dst, ah, al, bh, bl, start, stop, *after, skip=False):
            M(lambda e: e.matmul(dst, ah, bh, start=start, stop=False, skip_group_check=skip), *after)
            M(lambda e: e.matmul(dst, ah, bl, start=False, stop=False, skip_group_check=skip))
            return M(lambda e: e.matmul(dst, al, bh, start=False, stop=stop, skip_group_check=skip))

        def proj(bank, hi, lo, col, toks, src_h, src_l, srctoks, nk=NC, k0=0, start=True, stop=True, n=T):
            t = None
            for k in range(nk):
                t = mm3(pb[bank][:, 0:n], hi[:, k, col:col + P], lo[:, k, col:col + P],
                        src_h[:, k0 + k, 0:n], src_l[:, k0 + k, 0:n],
                        start and k == 0, stop and k == nk - 1,
                        toks, srctoks(k0 + k), bf[bank] if start and k == 0 else None)
            return t

        def proj2(banks, hi, lo, toks, src_h, src_l, srctoks):
            t = [None, None]
            for k in range(NC):
                for cc in range(2):
                    t[cc] = mm3(pb[banks[cc]], hi[:, k, cc * P:(cc + 1) * P], lo[:, k, cc * P:(cc + 1) * P],
                                src_h[:, k, :], src_l[:, k, :], k == 0, k == NC - 1, toks, srctoks(k),
                                bf[banks[cc]] if k == 0 else None)
            return t

        def proj_tok(bank, hi, lo, c0, cols, toks, src_h, src_l, srctoks, tb, o=0):
            t = None
            for k in range(NC):
                sl = slice(tb * P, (tb + 1) * P)
                t = mm3(pb[bank][:, o:o + cols], src_h[:, k, sl], src_l[:, k, sl], hi[:, k, c0:c0 + cols],
                        lo[:, k, c0:c0 + cols], k == 0, k == NC - 1, toks, srctoks(k), bf[bank])
            return t

        def use(name, *toks):
            free[name] = list(toks)

        def was(name):
            return free.get(name, [])

        def square_in(c, src, n, after, adder=V, base=2):
            if c == 0:
                t = S(lambda e: e.activation(ssum[:, 0:n], src, ACT.Square), after, was("ssum"))
            else:
                i = base + c % 2
                a = S(lambda e: e.activation(tmp[i][:, 0:n], src, ACT.Square), after, was(f"tmp{i}"))
                t = adder(lambda e: e.tensor_tensor(ssum[:, 0:n], ssum[:, 0:n], tmp[i][:, 0:n], ALU.add), a, free["ss"])
                use(f"tmp{i}", t)
            free["ss"] = [t]
            return t

        def preload(func, *after):
            S(lambda e: e.activation(dum[:, :], k_("one"), func), ctok, after)

        ring = {"hs": 0}

        def inverse(src, tok, heads, n, mean):
            i = ring["hs"] % 4
            ring["hs"] += 1
            nb = (n + P - 1) // P
            last = n - (nb - 1) * P
            ind = cst[:, 256:384:64] if heads == 2 else k_("one")
            for b in range(nb):
                w = P if b < nb - 1 else last
                m = M(lambda e, b=b, w=w: e.matmul(pb[7][0:w, b * heads:(b + 1) * heads], src[:, b * P:b * P + w], ind,
                                                   start=True, stop=True), tok, bf[7], ctok)
            w = P if nb > 1 else last
            h = hs[0:w, i, 0:nb * heads]
            a = S(lambda e: e.activation(h, pb[7][0:w, 0:nb * heads], ACT.Sqrt, bias=cst[0:w, CST["eps"]:CST["eps"] + 1],
                                         scale=1.0 / mean), m, was(f"hs{i}"))
            bf[7] = [a]
            return m, (i, heads, n, V(lambda e: e.reciprocal(h, h), a))

        def spread(job, sq=None, bank=6, o=0):
            i, heads, n, tok = job
            nb = (n + P - 1) // P
            if heads == 2:
                w = min(P, n)
                full = tmp[sq][0:w, 0:nb * P].rearrange("p (b d) -> p b d", d=64)
                each = hs[0:w, i, 0:nb * 2].unsqueeze(2).broadcast_to([w, nb * 2, 64])
                tok = V(lambda e: e.tensor_copy(full, each), tok, was(f"tmp{sq}"))
            for b in range(nb):
                w = min(P, n - b * P)
                r = tmp[sq][0:w, b * P:(b + 1) * P] if heads == 2 else hs[0:w, i, o + b:o + b + 1].broadcast_to([w, P])
                m = M(lambda e, b=b, w=w, r=r: e.matmul(pb[bank][:, b * P:b * P + w], r, cst[0:w, 0:w], start=True, stop=True),
                      tok, bf[bank])
            use(f"hs{i}", m)
            if heads == 2:
                use(f"tmp{sq}", m)
            return m

        def rstd_of(tok, n, bank=6):
            m, job = inverse(ssum, tok, 1, n, D)
            use("ssum", m)
            return spread(job, bank=bank)

        def norm(src, n, factor, shift, dh, dl, after, ftoks, then=None, r=None, bank=6):
            if r is None:
                r = rstd_of(free["ss"], n, bank)
            toks = []

            def first(c):
                i = c % 3
                return V(lambda e: e.scalar_tensor_tensor(
                    out=tmp[i][:, 0:n], in0=src[:, c, 0:n], scalar=factor(c), in1=pb[bank][:, 0:n],
                    op0=ALU.mult, op1=ALU.mult), r, was(f"tmp{i}"), ftoks)

            t = first(0)
            for c in range(NC):
                i = c % 3
                if shift is None:
                    a = S(lambda e, c=c, i=i: e.copy(dh[:, c, 0:n], tmp[i][:, 0:n]), t, after)
                else:
                    a = S(lambda e, c=c, i=i: e.activation(dh[:, c, 0:n], tmp[i][:, 0:n], ACT.Identity,
                                                           bias=shift(c)), t, after)
                use(f"tmp{i}", a)
                if c < NC - 1:
                    t = first(c + 1)
                if shift is None:
                    b = V(lambda e, c=c, i=i: e.tensor_tensor(
                        dl[:, c, 0:n], tmp[i][:, 0:n], dh[:, c, 0:n].bitcast(F32), ALU.subtract), a)
                else:
                    b = V(lambda e, c=c, i=i: e.scalar_tensor_tensor(
                        out=dl[:, c, 0:n], in0=tmp[i][:, 0:n], scalar=shift(c), in1=dh[:, c, 0:n].bitcast(F32),
                        op0=ALU.add, op1=ALU.subtract), a)
                use(f"tmp{i}", a, b)
                toks.append([a, b])
            bf[bank] = [t]
            if then is not None:
                preload(then)
            return lambda k: toks[k]

        xtok = [None] * NC

        def residual(c, bank, coef, tok, ctoks, keep=True, early=None, adder=V, base=2):
            t = V(lambda e: e.scalar_tensor_tensor(out=xT[:, c, :], in0=pb[bank][:, :], scalar=coef, in1=xT[:, c, :],
                                                   op0=ALU.mult, op1=ALU.add), tok, ctoks, xtok[c])
            bf[bank] = [t]
            xtok[c] = t
            if early:
                early(c, t)
            if keep:
                if c == NC - 1:
                    preload(ACT.Sqrt)
                square_in(c, xT[:, c, :], T, t, adder, base)
            return t

        def split_x(c, gain, tok, after, toks, held=None):
            a = S(lambda e: e.activation(xh[:, c, :], xT[:, c, :], ACT.Identity, scale=gain(c)), tok, after)

            def low():
                b = V(lambda e: e.scalar_tensor_tensor(out=xl[:, c, :], in0=xT[:, c, :], scalar=gain(c),
                                                       in1=xh[:, c, :].bitcast(F32), op0=ALU.mult, op1=ALU.subtract), a)
                toks.append([a, b])

            if held is None:
                low()
                return
            while held:
                held.pop()()
            if c < NC - 1:
                held.append(low)
            else:
                low()

        def late_rstd(dst, after):
            m, job = inverse(ssum, free["ss"], 1, T, D)
            use("ssum", m)

            def end():
                m = spread(job)
                t = V(lambda e: e.tensor_copy(dst, pb[6]), m, after)
                bf[6] = [t]
                return [t], job

            return end

        for name, dst, src in (("vec", vec, A["vecs"]), ("cst", cst, A["consts"])):
            load(SP, "c0", dst[:, :], src)
        ctok = [Tok(dsem["c0"][0], 32)]

        s0 = ExitStack()
        mh = sb("mh", [P, NC, LC], F32R, s0)
        ml = sb("ml", [P, NC, LC], F32R, s0)
        a1 = ExitStack()
        fb = [sb(f"fb{n}", [P, 2, 1024], F32, a1) for n in range(6)]
        ctT = sb("ctT", [P, NC, LC], F32, a1)
        mmT = sb("mmT", [P, NC, LC], F32, a1)
        bst = sb("bst", [P, NBCS], F32, a1)
        scp = sb("scp", [P, 4, 8, 8], F32, a1)
        scz = G(lambda e: e.memset(scp[:, :, :, :], 0.0))
        mtok = load(SP, "mm", mmT[:, :, :], A["memT"].rearrange("(c p) t -> p c t", p=P))
        dma_unit()
        dma_unit()
        fbtok = []

        def load_first(n):
            j, k = n // 4, n % 4
            fbtok.append(load(SP, f"fb{n}", fb[n][:, :, :], ada_w[0, k * 256:(k + 1) * 256, j * 1024:(j + 1) * 1024]
                              .rearrange("(k p) n -> p k n", p=P)))

        for n in range(3):
            load_first(n)
        xtk = load(SP, "x", xT[:, :, :], A["xT"].rearrange("(c p) t -> p c t", p=P))
        for c in range(NC):
            xtok[c] = xtk
        sctok = []
        for q in range(4):
            sctok.append(S(lambda e, q=q: e.activation(scp[:, q, :, 2 * q:2 * q + 2], vec[:, 0:16].rearrange(
                "p (z k) -> p k z", z=2), ACT.Silu), ctok, scz))
        sctok = sctok + [S(lambda e: e.activation(sc[:, :, :], vec[:, 0:16].rearrange("p (z k) -> p k z", z=2), ACT.Silu), ctok)]
        preload(ACT.Sqrt)

        def factors(o, g, src, j, toks):
            return [V(lambda e: e.scalar_tensor_tensor(out=cf[:, o:o + 8], in0=src[:, j * 8:j * 8 + 8], scalar=1.0,
                                                       in1=g, op0=ALU.add, op1=ALU.mult), toks)]

        for c in range(NC):
            square_in(c, mmT[:, c, :], LC, mtok)
        w_ahead()
        mt = norm(mmT, LC, lambda c: v_("memkv", c), None, mh, ml, [], ctok)

        jobs_ = []

        def start(gen):
            next(gen)
            jobs_.append(gen)

        def advance():
            for g in list(jobs_):
                if next(g, "end") == "end":
                    jobs_.remove(g)

        def drain():
            while jobs_:
                advance()

        def head_norm(src, srctok, sq, gain, n, dst, res):
            m, job = inverse(tmp[sq], srctok, 2, n, 64)
            use(f"tmp{sq}", m)
            yield
            m = spread(job, sq)
            t = V(lambda e: e.scalar_tensor_tensor(out=dst, in0=src, scalar=gain, in1=pb[6][:, 0:n],
                                                   op0=ALU.mult, op1=ALU.mult), m, srctok)
            bf[6] = [t]
            res.append(t)
            yield

        def km_job(c, t):
            a = S(lambda e: e.copy(kmT[:, c, :], pb[c][:, 0:LC]), t)
            q = S(lambda e: e.activation(tmp[c][:, 0:LC], pb[c][:, 0:LC], ACT.Square), t, was(f"tmp{c}"))
            bf[c] = [a, q]
            yield
            yield from head_norm(kmT[:, c, :], [a, q], c, v_("gmk"), LC, kmT[:, c, :], kmtok)

        hi, lo, wt, done = w_next()
        for n in range(3, 6):
            load_first(n)
        cttok = load(SP, "ct", ctT[:, :, :], A["ctxT"].rearrange("(c p) t -> p c t", p=P))
        btok = load(SP, "bs", bst[:, :], A["masks"])
        kmtok = []
        for c in range(2):
            t = proj(c, hi, lo, c * P, wt, mh, ml, mt, n=LC)
            start(km_job(c, t))
        done(t)
        for c in range(NC):
            square_in(c, xT[:, c, :], T, xtk)
        hi, lo, wt, done = w_next()
        vmtok = []
        for tb in range(2):
            t = proj_tok(2 - tb, hi, lo, 0, 256, wt, mh, ml, mt, tb)
            advance()
            a = S(lambda e, tb=tb: e.copy(vm[:, tb, :], pb[2 - tb][:, 0:256]), t)
            bf[2 - tb] = [a]
            vmtok.append(a)
        done(t)
        memlast = t
        ada_first(0)
        advance()
        ada_first(1)
        drain()
        ada_first(2)
        xr = rstd_of(free["ss"], T, 5)
        for c in range(NC):
            square_in(c, ctT[:, c, :], LC, cttok)
        ada_first(6)
        ada_first(7)
        ada_first(3)
        cr = rstd_of(free["ss"], LC, 3)
        bctok = [V(lambda e: e.tensor_copy(bcs[:, :], bst[:, :]), btok)]
        w_ahead()
        ada_first(4)
        ada_first_end(ada_first(5))
        fbfree = fence()
        f0 = factors(0, v_("gm0", 0, 8), ada[0], 1, [adatok[("first", 0)]])
        fc = factors(8, v_("gm0", 0, 8), adac, 1, [adatok[("first", 1)]])
        xt = norm(xT, T, lambda c: cf[:, c:c + 1], lambda c: ada[0][:, c:c + 1], xh, xl, [], f0, r=xr, bank=5)
        unit0 = w_next()
        ct = norm(ctT, LC, lambda c: cf[:, 8 + c:9 + c], lambda c: adac[:, c:c + 1], mh, ml, [memlast], fc, r=cr, bank=3)
        a1free = fence()

        a1.close()
        a1 = ExitStack()
        b1c = sb("b1c", [P, NB1C], F32, a1)
        fab = sb("fab", [P, 3072], F32, a1)
        fT = fab[:, 0:2048].rearrange("p (c t) -> p c t", c=4)
        AB = fab[:, 2048:3072].rearrange("p (c t) -> p c t", c=4)
        qT = sb("qT", [P, 4, T], F32, a1)
        kT = sb("kT", [P, T], F32, a1)
        kTs = sb("kTs", [P, T], F32, a1)
        kcT = sb("kcT", [P, LC], F32, a1)
        kcTs = sb("kcTs", [P, LC], F32, a1)
        vt = sb("vt", [P, 4, 256], F32, a1)
        vct = sb("vct", [P, 2, 256], F32, a1)
        pr = sb("pr", [P, 2, 2, 640], F32, a1)
        pt = fab[:, 0:2560].rearrange("p (a b) -> p a b", a=2)
        b1tok = [load(G, "b1c", b1c[:, :], A["b1c"], fbfree)]

        def b1(name, w=128, o=0):
            return b1c[:, B1C[name] + o:B1C[name] + o + w]

        def rope(src, srctok, cos, sin, rot, scale, dst, bank, ctoks, res, n=T):
            i = 2 + ring["hs"] % 2
            ring["hs"] += 1
            m = M(lambda e: e.matmul(pb[bank][:, 0:n], rot, src, start=True, stop=True), srctok, bf[bank], ctoks)
            b = V(lambda e: e.scalar_tensor_tensor(out=tmp[i][:, 0:n], in0=pb[bank][:, 0:n], scalar=scale, in1=sin,
                                                   op0=ALU.mult, op1=ALU.mult), m, was(f"tmp{i}"), ctoks)
            bf[bank] = [b]
            a = V(lambda e: e.scalar_tensor_tensor(out=dst, in0=src, scalar=scale, in1=cos,
                                                   op0=ALU.mult, op1=ALU.mult), m, srctok)
            t = V(lambda e: e.tensor_tensor(dst, dst, tmp[i][:, 0:n], ALU.add), a, b)
            use(f"tmp{i}", t)
            res.append(t)

        def swap(dst, src, key, tok, after=()):
            load(G, key, dst[0:64], src[64:128], tok, after)
            return load(G, key, dst[64:128], src[0:64], tok, after)

        def v_job(bank, tok, n, i, tbank, dst, after, res, scale=None):
            nb = n // P
            if scale is None:
                a = S(lambda e: e.copy(tmp[i][:, 0:n], pb[bank][:, 0:n]), tok, was(f"tmp{i}"))
            else:
                a = V(lambda e: e.tensor_tensor(tmp[i][:, 0:n], pb[bank][:, 0:n], scale, ALU.mult), tok, was(f"tmp{i}"))
            bf[bank] = [a]
            yield
            for b in range(nb):
                m = M(lambda e, b=b: e.transpose(pb[tbank][:, b * P:(b + 1) * P], tmp[i][:, b * P:(b + 1) * P], ident),
                      a, bf[tbank], ctok)
            use(f"tmp{i}", m)
            full = dst.rearrange("p t (j a d) -> p (t j) a d", j=2, a=2)
            src = pb[tbank][:, 0:n].rearrange("p (t d) -> p t d", d=64).unsqueeze(2).broadcast_to([P, 2 * nb, 2, 64])
            c = S(lambda e: e.copy(full, src), m, after)
            bf[tbank] = [c]
            res += [c] * nb
            yield

        ft, qt = [], []

        def q_job(dst, a):
            yield
            rope(dst, a, b1("cos", T), b1("sin", T), b1("rot"), 0.125, dst, 5, b1tok, qt)

        for u in range(4):
            hi, lo, wt, done = w_next() if u else unit0
            ts = proj2((0, 1), hi, lo, wt, xh, xl, xt) if u == 0 else None
            for cc in range(2):
                c = 2 * u + cc
                b = c % 4
                t = ts[cc] if ts else proj(b, hi, lo, cc * P, wt, xh, xl, xt)
                advance()
                dst = fT[:, c, :] if c < 4 else qT[:, c - 4, :]
                a = S(lambda e, dst=dst, b=b: e.copy(dst, pb[b]), t, b1tok)
                bf[b] = [a]
                if c < 4:
                    ft.append(a)
                else:
                    start(q_job(dst, a))
            done(t)
        hi, lo, wt, done = w_next()
        t = proj(0, hi, lo, 0, wt, xh, xl, xt)
        advance()
        a = S(lambda e: e.copy(kT[:, :], pb[0]), t, b1tok, a1free)
        bf[0] = [a]
        t = proj(1, hi, lo, 0, wt, mh, ml, ct, n=LC)
        kt = []
        rope(kT[:, :], a, b1("cos", T), b1("sin", T), b1("rot"), 1.0, kT[:, :], 5, b1tok, kt)
        drain()
        kst = swap(kTs, kT, "kTs", kt)
        kct = S(lambda e: e.copy(kcT[:, :], pb[1][:, 0:LC]), t, a1free)
        bf[1] = [kct]
        kcst = swap(kcTs, kcT, "kcTs", kct)
        vtt, vctt = [], []
        t = proj(3, hi, lo, P, wt, xh, xl, xt)
        start(v_job(3, t, T, 0, 2, vt, a1free, vtt))
        xlast = t
        t = proj(4, hi, lo, P, wt, mh, ml, ct, n=LC)
        start(v_job(4, t, LC, 1, 7, vct, a1free, vctt))
        done(t)

        mixt = [[] for _ in range(NC)]

        def put(bank, rows, cols, dst_h, dst_l, tok, c):
            a = S(lambda e: e.copy(dst_h, cols), tok, xlast)
            b = V(lambda e: e.tensor_tensor(dst_l, cols, dst_h.bitcast(F32), ALU.subtract), a)
            mixt[c] += [a, b]
            return [a, b]

        ab = [AB, pr[:, :, :, :].rearrange("p a b c -> p (a b c)")[:, 0:1024].rearrange("p (t c) -> p t c", t=4)]

        def over_dims(c):
            out = []
            for tb in range(4):
                bank = 5 + tb % 2
                m = M(lambda e, tb=tb, bank=bank: e.matmul(
                    pb[bank][:, 0:256], fT[:, c, tb * P:(tb + 1) * P], b1("cd", 256), start=True, stop=True),
                    ft[c], bf[bank], b1tok)
                dst = ab[c % 2][:, tb, :]
                if tb % 2:
                    w = S(lambda e, dst=dst, bank=bank: e.copy(dst, pb[bank][:, 0:256]), m, was(f"AB{c % 2}"), a1free)
                else:
                    w = V(lambda e, dst=dst, bank=bank: e.tensor_copy(dst, pb[bank][:, 0:256]), m, was(f"AB{c % 2}"), a1free)
                bf[bank] = [w]
                out.append(w)
            return out

        abt = over_dims(0)
        for c in range(4):
            advance()
            nxt = over_dims(c + 1) if c < 3 else None
            ada_step()
            bank = c % 2
            for tb in range(4):
                for z, tab in ((0, "cn"), (1, "sn")):
                    m = M(lambda e, c=c, tb=tb, z=z, tab=tab, bank=bank: e.matmul(
                        pb[bank], ab[c % 2][:, tb, z * P:(z + 1) * P], b1(tab, T, tb * T),
                        start=(tb == 0 and z == 0), stop=(tb == 3 and z == 1)),
                        abt[tb], bf[bank] if tb == 0 and z == 0 else None)
            use(f"AB{c % 2}", m)
            bf[bank] = put(bank, None, pb[bank], xh[:, c, :], xl[:, c, :], m, c)
            abt = nxt
        for name in ("pt0", "pt1", "prob0", "prob1"):
            use(name, m, *a1free)

        seq = {"n": 0, "pt": 0}
        later = []

        def soft_a(nh, qk, masks, width, span, prob, after, sink=None, gate=None, gtok=(), valid=None, wide=False):
            par = seq["n"] % 2
            seq["n"] += 1
            nm, rs, es = sm[:, par, 0:nh], sm[:, par, 4:4 + nh], sm[:, par, 8:8 + nh]
            base = {}
            toks = []
            for g in range(nh):
                o = span(g)
                banks = sorted({o // 512, (o + width - 1) // 512})
                t = None
                for q, k, col, w in qk(g):
                    mk = [x for x in masks if x[0] == col]
                    t = M(lambda e, q=q, k=k, a=o + col, w=w, mk=mk: e.matmul(
                        ps[:, a:a + w], q, k, start=True, stop=not mk, skip_group_check=True),
                        after, [bf[b] for b in banks])
                    for col2, w2, mask in mk:
                        t = M(lambda e, a=o + col2, w=w2, mask=mask: e.matmul(
                            ps[:, a:a + w], b_("ident"), mask, start=False, stop=True, skip_group_check=True), bctok)
                toks.append((t, banks, o))
            ex, todo = [], []
            for g in range(nh):
                t, banks, o = toks[g]
                red = V(lambda e, g=g, o=o: e.tensor_reduce(nm[:, g:g + 1], ps[:, o:o + width], AXX, ALU.max,
                                                            negate=sink is None), t, was(f"sm{par}"))
                if sink is not None:
                    red = V(lambda e, g=g: e.tensor_scalar(nm[:, g:g + 1], nm[:, g:g + 1], sink[:, g:g + 1], -1.0,
                                                           ALU.max, ALU.mult), red)
                a = S(lambda e, g=g, o=o: e.activation(prob[:, g, 0:width], ps[:, o:o + width], ACT.Exp,
                                                       bias=nm[:, g:g + 1], accum_out=rs[:, g:g + 1]),
                      red, was(f"prob{par}"))
                for b in banks:
                    bf[b] = [x for x in bf[b] if x in ex] + [a]
                ex.append(a)
                if sink is not None:
                    todo.append(S(lambda e, g=g: e.activation(es[:, g:g + 1], nm[:, g:g + 1], ACT.Exp,
                                                              bias=sink[:, g:g + 1]), red))
            out = []

            def scale():
                last = ex
                if sink is not None:
                    last = [V(lambda e: e.tensor_tensor(rs, rs, es, ALU.add), todo, ex)]
                r = V(lambda e: e.reciprocal(rs, rs), last)
                if gate is not None:
                    r = V(lambda e: e.tensor_tensor(rs, rs, gate, ALU.mult), r, gtok)
                if valid is not None:
                    r = V(lambda e: e.tensor_scalar(rs, rs, valid, None, ALU.mult), r)
                for g in range(nh):
                    out.append(V(lambda e, g=g: e.tensor_scalar(prob[:, g, 0:width], prob[:, g, 0:width], rs[:, g:g + 1],
                                                                None, ALU.mult), r))
                use(f"sm{par}", *out)

            later.append(scale)
            return par, out

        def soft_b(nh, prob, ptok, par, blocks, ptile, pbanks=(4, 5, 7)):
            per = max(1, 4 // nh)
            evs = []
            for b0 in range(0, len(blocks), per):
                grp = blocks[b0:b0 + per]
                bank = pbanks[seq["pt"] % len(pbanks)]
                for bi, (col, w, v, vtk) in enumerate(grp):
                    for g in range(nh):
                        o = (bi * nh + g) * P
                        t = M(lambda e, o=o, g=g, col=col, w=w, bank=bank: e.transpose(
                            pb[bank][0:w, o:o + P], prob[:, g, col:col + w], ident), ptok[g], bf[bank], ctok)
                w = grp[0][1]
                n = len(grp) * nh * P
                dst = ptile[0:w, b0 * nh * P:b0 * nh * P + n]
                if seq["pt"] % 2:
                    ev = V(lambda e, dst=dst, bank=bank, w=w, n=n: e.tensor_copy(dst, pb[bank][0:w, 0:n]), t, was(f"pt{par}"))
                else:
                    ev = S(lambda e, dst=dst, bank=bank, w=w, n=n: e.copy(dst, pb[bank][0:w, 0:n]), t, was(f"pt{par}"))
                bf[bank] = [ev]
                seq["pt"] += 1
                evs += [ev] * len(grp)
            use(f"prob{par}", t)
            return evs

        def soft_c(nh, evs, par, blocks, ptile, obank, first, last):
            for bi, (col, w, v, vtk) in enumerate(blocks):
                t = M(lambda e, bi=bi, v=v, w=w: e.matmul(
                    pb[obank][:, 0:nh * P], v, ptile[0:w, bi * nh * P:(bi + 1) * nh * P],
                    start=first and bi == 0, stop=last and bi == len(blocks) - 1),
                    evs[bi], vtk, bf[obank] if first and bi == 0 else None)
            use(f"pt{par}", t)
            return t

        def pipeline(jobs, a_stage, b_stage, c_stage, each=None):
            got = {}
            n = len(jobs)
            for s_ in range(n + 2):
                if s_ < n:
                    got[s_] = a_stage(s_, *jobs[s_])
                if 0 <= s_ - 1 < n:
                    got[s_ - 1] = (got[s_ - 1], b_stage(s_ - 1, *jobs[s_ - 1], got[s_ - 1]))
                while later:
                    later.pop(0)()
                if 0 <= s_ - 2 < n:
                    c_stage(s_ - 2, *jobs[s_ - 2], got[s_ - 2])
                if each:
                    each(s_)

        def first_attention():
            jobs = [(i, j, h2) for i in range(4) for j in range(2) for h2 in range(2)]

            def a_stage(n_, i, j, h2):
                nb = [b for b in (i - 1, i, i + 1) if 0 <= b < 4]
                width = len(nb) * P + LC
                off = 512 - len(nb) * P

                def qk(g):
                    h = 4 * j + 2 * h2 + g
                    r = slice((h % 2) * 64, (h % 2) * 64 + 64)
                    kk, kc_ = (kT, kcT) if h % 2 == j else (kTs, kcTs)
                    q = qT[r, h // 2, i * P:(i + 1) * P]
                    return [(q, kk[r, b * P:(b + 1) * P], n * P, P) for n, b in enumerate(nb)] + \
                        [(q, kc_[r, :], len(nb) * P, LC)]

                masks = [(n * P, P, b_("prev") if b < i else b_("diag"))
                         for n, b in enumerate(nb) if b != i]
                par = seq["n"] % 2
                sink = v_("sink", 4 * j + 2 * h2, 2)
                par, tok = soft_a(2, qk, masks, width, lambda g: g * 1024 + off, pr[:, par, :, :],
                                  [qt, kt, kst, kct, kcst], sink=sink)
                return par, tok, nb, width

            def values(j, nb):
                vs = [(m * P, P, vt[:, b, j * P:(j + 1) * P], vtt[b]) for m, b in enumerate(nb)]
                return vs + [((len(nb) + m) * P, P, vct[:, m, j * P:(j + 1) * P], vctt[m]) for m in range(2)]

            def b_stage(n, i, j, h2, got):
                par, tok, nb, width = got
                return soft_b(2, pr[:, par, :, :], tok, par, values(j, nb), pt[:, par, :])

            def c_stage(n, i, j, h2, got):
                (par, tok, nb, width), evs = got
                ob = 6
                t = soft_c(2, evs, par, values(j, nb), pt[:, par, :], ob, True, True)
                last = []
                for g in range(2):
                    c = 4 + (4 * j + 2 * h2) // 2
                    r = slice(g * 64, g * 64 + 64)
                    cols = slice(i * P, (i + 1) * P)
                    last += put(ob, r, pb[ob][r, g * P:(g + 1) * P], xh[r, c, cols], xl[r, c, cols], t, c)
                bf[ob] = last

            pipeline(jobs, a_stage, b_stage, c_stage,
                     lambda s_: w_ahead() if s_ == 13 else ada_step() if s_ in (2, 7) else None)

        first_attention()

        def mix_out(coef, ctoks, early=None):
            for u in range(4):
                hi, lo, wt, done = w_next()
                for cc in range(2):
                    c = 2 * u + cc
                    t = proj(c % 2, hi, lo, cc * P, wt, xh, xl, lambda k: mixt[k])
                    residual(c, c % 2, coef(c), t, ctoks, early=early(t) if early and c == NC - 1 else None)
                done(t)

        mix_out(lambda c: ada[0][:, 16 + c:17 + c], adatok[("m", 0, 2)])
        a1.close()
        s0.close()

        names = {"n": 0}

        def ffn(coef, ctoks, xtoks, arena, keep=True, final=None, rstd=None, early=None):
            names["n"] += 1
            hst = ExitStack()
            hh = sb(f"hh{names['n']}", [P, NF, T], F32R, hst)
            hl = sb(f"hl{names['n']}", [P, NF, T], F32R, hst)
            ht = []
            rt = None

            def gate(cc, t):
                if rstd is None:
                    s_ = S(lambda e: e.activation(tmp[cc][:, :], pb[cc], ACT.Silu), t, was(f"tmp{cc}"))
                    bf[cc] = [s_]
                    return s_
                m = V(lambda e: e.tensor_tensor(tmp[cc][:, :], pb[cc], rsx, ALU.mult), t, rt, was(f"tmp{cc}"))
                bf[cc] = [m]
                s_ = S(lambda e: e.activation(tmp[cc][:, :], tmp[cc][:, :], ACT.Silu), m)
                return G(lambda e: e.tensor_tensor(tmp[cc][:, :], tmp[cc][:, :], rsx, ALU.mult), s_, rt)

            for g in range(NF // 2):
                hi, lo, wt, done = w_next()
                if g == 0:
                    ts = proj2((0, 1), hi, lo, wt, xh, xl, xtoks)
                    end = rstd() if rstd else None
                else:
                    ts = []
                    for cc in range(2):
                        ts.append(proj(cc, hi, lo, cc * P, wt, xh, xl, xtoks))
                        if cc == 0:
                            sg = [gate(0, ts[0])]
                    sg.append(gate(1, ts[1]))
                done(ts[1])
                hi, lo, wt, done = w_next()
                for cc in range(2):
                    f = 2 * g + cc
                    t = proj(2 + cc, hi, lo, cc * P, wt, xh, xl, xtoks)
                    if g == 0 and cc == 0:
                        if rstd:
                            rt = end()
                        sg = [gate(0, ts[0]), gate(1, ts[1])]
                    m = V(lambda e, cc=cc: e.tensor_tensor(tmp[cc][:, :], pb[2 + cc], tmp[cc][:, :], ALU.mult), t, sg[cc])
                    bf[2 + cc] = [m]
                    a = S(lambda e, f=f, cc=cc: e.copy(hh[:, f, :], tmp[cc][:, :]), m, arena)
                    b = V(lambda e, f=f, cc=cc: e.tensor_tensor(hl[:, f, :], tmp[cc][:, :], hh[:, f, :].bitcast(F32),
                                                                ALU.subtract), a)
                    use(f"tmp{cc}", a, b)
                    ht.append([a, b])
                done(t)
            xused = t
            if early:
                go_on = early(xused)
            for g in range(4):
                b0 = 2 * (g % 2)
                for k0, kc in ((0, 8), (8, 7), (15, 7)):
                    hi, lo, wt, done = w_next()
                    for cc in range(2):
                        t = proj(b0 + cc, hi, lo, cc * P, wt, hh, hl, lambda k: ht[k], kc, k0, k0 == 0, k0 + kc == NF)
                        if k0 + kc == NF:
                            r = residual(2 * g + cc, b0 + cc, coef(2 * g + cc), t, ctoks(), keep,
                                         go_on if early else None)
                            if final:
                                final(2 * g + cc, r)
                    done(t)
            hst.close()
            return t

        f1 = factors(16, v_("gf0", 0, 8), ada[0], 4, [adatok[("m", 0, 4)], adatok[("m", 0, 3)]])
        xn = norm(xT, T, lambda c: cf[:, 16 + c:17 + c], lambda c: ada[0][:, 24 + c:25 + c], xh, xl, fence(), f1, then=ACT.Silu)
        ffn(lambda c: ada[0][:, 40 + c:41 + c], lambda: adatok[("m", 0, 5)], xn, fence())

        pst = ExitStack()
        xp = sb("xp", [P, NC, T + 16], F32, pst)
        sa = sb("sa", [P, 2, T + 16], F32, pst)
        icnt = sb("icnt", [P, 4, 2, 8], F32, pst)
        f2 = factors(24, v_("gm1", 0, 8), ada[1], 1, [adatok[("m", 1, 1)], adatok[("m", 1, 0)]])
        f2g = [V(lambda e: e.tensor_tensor(cf[:, 40:48], ada[1][:, 16:24], v_("pscale", 0, 8), ALU.mult),
                 adatok[("m", 1, 2)])]
        after = fence()
        ictok = load(G, "icnt", icnt[:, :, :, :], A["icnt"], after)
        z = [G(lambda e: e.memset(xp[:, :, 0:8], 0.0), after), G(lambda e: e.memset(xp[:, :, T + 8:T + 16], 0.0), after)]
        r = rstd_of(free["ss"], T)
        pooled = []
        tmp.extend([acc[:, 0:512], acc[:, 512:1024]])
        use("tmp4", *accdone["fin"])
        use("tmp5", *accdone["fin"])

        def normed(c):
            i = c % 2
            t = V(lambda e: e.scalar_tensor_tensor(out=tmp[i][:, :], in0=xT[:, c, :], scalar=cf[:, 24 + c:25 + c],
                                                   in1=pb[6], op0=ALU.mult, op1=ALU.mult), r, was(f"tmp{i}"), f2)
            bf[6] = [t]
            a = S(lambda e: e.activation(xp[:, c, 8:T + 8], tmp[i][:, :], ACT.Identity, bias=ada[1][:, c:c + 1]), t, after)
            use(f"tmp{i}", a)
            return a

        def pool(c, a):
            i = 2 + c % 2
            g = c // 2
            w = 2 << g
            src, t, width, step = xp[:, c, :], [a, z], 1, 0
            while width < w:
                dst = sa[:, step % 2, :]
                t = [V(lambda e, src=src, dst=dst, width=width: e.tensor_tensor(
                    dst[:, 0:T + 17 - 2 * width], src[:, 0:T + 17 - 2 * width], src[:, width:T + 17 - width], ALU.add),
                    t, was(f"sa{step % 2}"), after)]
                src = dst
                width *= 2
                step += 1
            o = 8 - w // 2
            s_ = src[:, o:o + T]
            ends = s_.rearrange("p (a b) -> p a b", b=8)[:, ::T // 8 - 1, :]
            t = V(lambda e: e.tensor_tensor(ends, ends, icnt[:, g], ALU.mult), t, ictok)
            t = V(lambda e: e.scalar_tensor_tensor(out=tmp[i][:, :], in0=s_, scalar=1.0 / w, in1=xp[:, c, 8:T + 8],
                                                   op0=ALU.mult, op1=ALU.subtract), t, was(f"tmp{i}"))
            use("sa0", t)
            use("sa1", t)
            a = S(lambda e: e.copy(xh[:, c, :], tmp[i][:, :]), t, after)
            use(f"tmp{i}", a)
            return a

        def low(c, a):
            i = 2 + c % 2
            b = V(lambda e: e.tensor_tensor(xl[:, c, :], tmp[i][:, :], xh[:, c, :].bitcast(F32), ALU.subtract), a)
            use(f"tmp{i}", a, b)
            pooled.append([a, b])

        def mixed(g):
            for c in (2 * g, 2 * g + 1):
                bank = c % 4
                for k in range(2):
                    cols = slice((c % 2) * P, (c % 2 + 1) * P)
                    t = mm3(pb[bank], hi[:, 2 * g + k, cols], lo[:, 2 * g + k, cols],
                            xh[:, 2 * g + k, :], xl[:, 2 * g + k, :], k == 0, k == 1, wt, pooled[2 * g + k],
                            bf[bank] if k == 0 else None)
                residual(c, bank, cf[:, 40 + c:41 + c], t, f2g, adder=G if c < NC - 1 else V, base=4)
            return t

        a, h = normed(0), None
        for c in range(NC):
            nxt = normed(c + 1) if c < NC - 1 else None
            h2 = pool(c, a)
            if h:
                low(c - 1, h)
            if c == 3:
                hi, lo, wt, done = w_next()
            if c % 2 and c > 1:
                mixed(c // 2 - 1)
            a, h = nxt, h2
        low(NC - 1, h)
        done(mixed(3))
        pst.close()
        f3 = factors(32, v_("gf1", 0, 8), ada[1], 4, [adatok[("m", 1, 4)], adatok[("m", 1, 3)]])
        xn = norm(xT, T, lambda c: cf[:, 32 + c:33 + c], lambda c: ada[1][:, 24 + c:25 + c], xh, xl, fence(), f3, then=ACT.Silu)
        ss2, rsx = acc[:, 0:512], acc[:, 512:1024]
        gn = [V(lambda e: e.tensor_tensor(cf[:, 0:8], v_("fin", 0, 8), v_("n1", 0, 8), ALU.mult), ctok)]
        xn1, sq2 = [], []

        def both(after):
            def go_on(c, tok):
                if c == 0:
                    t = S(lambda e: e.activation(ss2, xT[:, 0, :], ACT.Square, scale=v_("fin")), tok, was("tmp4"))
                else:
                    i = c % 2
                    a = S(lambda e: e.activation(tmp[i][:, :], xT[:, c, :], ACT.Square, scale=v_("fin", c)), tok,
                          was(f"tmp{i}"))
                    t = V(lambda e: e.tensor_tensor(ss2, ss2, tmp[i][:, :], ALU.add), a, sq2)
                    use(f"tmp{i}", t)
                sq2[:] = [t]
                split_x(c, lambda k: cf[:, k:k + 1], tok, [after, gn], xn1)

            return go_on

        ffn(lambda c: ada[1][:, 40 + c:41 + c], lambda: adatok[("m", 1, 5)], xn, fence(), early=both)

        def both_rstd():
            i = ring["hs"] % 4
            ring["hs"] += 1
            for b in range(4):
                for z, src, tok in ((0, ssum, free["ss"]), (1, ss2, sq2)):
                    m = M(lambda e, b=b, z=z, src=src: e.matmul(pb[7][:, 4 * z + b:4 * z + b + 1], src[:, b * P:(b + 1) * P],
                                                                k_("one"), start=True, stop=True), tok, bf[7])
            use("ssum", m)
            h, h2 = hs[:, i, 0:4], hs[:, i, 4:8]
            a = S(lambda e: e.activation(h, pb[7][:, 0:4], ACT.Sqrt, bias=k_("eps"), scale=1.0 / D), m, was(f"hs{i}"))
            r1 = V(lambda e: e.reciprocal(h, h), a)
            t = V(lambda e: e.scalar_tensor_tensor(out=h2, in0=pb[7][:, 4:8], scalar=1.0 / D, in1=h, op0=ALU.mult,
                                                   op1=ALU.mult), r1, m)
            bf[7] = [a, t]
            t = V(lambda e: e.tensor_tensor(h2, h2, h, ALU.mult), t)
            t = S(lambda e: e.activation(h2, h2, ACT.Sqrt, bias=k_("eps")), t)
            t = V(lambda e: e.reciprocal(h2, h2), t)
            r2 = V(lambda e: e.tensor_tensor(h2, h2, h, ALU.mult), t)

            def end():
                m = spread((i, 1, T, r2), o=4)
                t = V(lambda e: e.tensor_copy(rsx, pb[6]), m)
                bf[6] = [t]
                m = spread((i, 1, T, r1), bank=5)
                for c in range(NC):
                    xtok[c] = V(lambda e, c=c: e.scalar_tensor_tensor(
                        out=xT[:, c, :], in0=xT[:, c, :], scalar=v_("fin", c), in1=pb[5], op0=ALU.mult, op1=ALU.mult),
                        m, xtok[c], xn1[c])
                bf[5] = [xtok[NC - 1]]
                return [t]

            return end

        xn2 = []

        def to_mix(after):
            return lambda c, tok: split_x(c, lambda k: v_("mixg", k), tok, after, xn2)

        ffn(lambda c: k_("half"), lambda: ctok, lambda k: xn1[k], fence(), rstd=both_rstd, early=to_mix)

        n2 = ExitStack()
        w2c = acc[:, 0:512].rearrange("p (z c n) -> p z c n", z=2, c=2)
        b2c = acc[:, 512:1024]
        C2S2 = sb("C2S2", [P, 1280], F32, n2)
        C2, S2 = C2S2[:, 0:T], C2S2[:, T:2 * T]
        q2 = sb("q2", [P, 4, T], F32, n2)
        ksT = sb("ksT", [P, 2, T], F32, n2)
        kwT = sb("kwT", [P, 2, T], F32, n2)
        v2s = sb("v2s", [P, 4, 256], F32, n2)
        v2w = sb("v2w", [P, 4, 256], F32, n2)
        gts = sb("gts", [P, 4, 24], F32, n2)
        qsT = sb("qsT", [P, 4, T], F32, n2)
        ksbT = sb("ksbT", [P, 4, T], F32, n2)
        vsb = sb("vsb", [P, 4, T], F32, n2)
        kcC = sb("kcC", [P, 2 * NCMP], F32, n2)
        vcC = sb("vcC", [32, 256], F32, n2)
        hid = sb("hid", [P, 2, 2 * NCMP], F32, n2)
        n3 = ExitStack()
        kcr = sb("kcr", [P, 2, T], F32, n3)
        kb = sb("kb", [P, 16, 2 * NCMP], F32, n3)
        kbh = sb("kbh", [P, 16, 2 * NCMP], F32R, n3)
        kbl = sb("kbl", [P, 16, 2 * NCMP], F32R, n3)
        after2 = fence()
        b2tok = [load(G, "b2c", b2c[:, :], A["b2c"][:, 0:NB2C], after2)]
        w2tok = []
        for z, name in ((0, "cmp_w2_k_2"), (1, "cmp_w2_v_2")):
            for y in range(2):
                w2tok = [load(G, "w2c", w2c[:, z, :, y * 64:(y + 1) * 64],
                              A[name][0].rearrange("(c p) n -> p c n", p=P), after2)]

        def b2(name, w=128):
            return b2c[:, B2C[name]:B2C[name] + w]

        rsm = sb("rsm", [P, T], F32, n3)
        rcol = sb("rcol", [P, 4], F32, n3)

        def xn(k):
            return xn2[k]

        hi, lo, wt, done = w_next()
        q01 = proj2((0, 1), hi, lo, wt, xh, xl, xn)
        done(q01[1])
        end = late_rstd(rsm[:, :], after2)
        hi, lo, wt, done = w_next()
        q2_ = proj(2, hi, lo, 0, wt, xh, xl, xn)
        rt, job = end()
        rct = [V(lambda e: e.tensor_copy(rcol[:, :], hs[:, job[0], 0:4]), job[3], after2)]
        use(f"hs{job[0]}", was(f"hs{job[0]}"), rct)

        def qk_job(bank, tok, gain, scale, dst, res, sq, n=T, cos=None, sin=None, then=None):
            if n == T:
                a = V(lambda e: e.tensor_tensor(dst, pb[bank], rsm[:, :], ALU.mult), tok, rt, after2)
            else:
                a = S(lambda e: e.copy(dst, pb[bank][:, 0:n]), tok, after2)
            bf[bank] = [a]
            b = S(lambda e: e.activation(tmp[sq][:, 0:n], dst, ACT.Square), a, was(f"tmp{sq}"))
            yield
            mid = []
            yield from head_norm(dst, [a, b], sq, gain, n, dst, mid)
            if cos is None:
                rope(dst, mid, C2[:, :], S2[:, :], b2("rot"), scale, dst, 5, [b2tok, cst2], res)
            else:
                for j in range(2):
                    part = dst[:, j * NCMP:(j + 1) * NCMP]
                    rope(part, mid, cos, sin, b2("rot"), scale, part, 5, [b2tok, cst2], res, n=NCMP)
            if then:
                then()

        q2t = []
        for c in range(2):
            start(qk_job(c, q01[c], v_("gq"), 0.125, q2[:, c, :], q2t, c))

        an = sb("an", [P, 4, P], F32, n3)
        sel = sb("sel", [P, 513], F32, n3)
        hidt = sb("hidt", [P, 256], F32, n3)
        seltok = load(G, "sel", sel[:, :], A["b2c"][:, NB2C:NB2C + 513], after2)
        rows = slice(0, 33)
        posi = an[rows, 3, :].bitcast(I32)
        for b in range(5):
            n = 8 if b < 4 else 1
            src = A["positions_2"][:, (b % 4) * P:(b % 4 + 1) * P].partition_broadcast(n).rearrange("p a t -> p (a t)")
            post = load(G, "pos", an[8 * b:8 * b + n, 3, :].bitcast(I32), src, after2)
        ang, ni, nf = an[rows, 0, :], an[rows, 1, :].bitcast(I32), an[rows, 2, :]
        t = V(lambda e: e.tensor_copy(ang, posi), post, after2)
        t = V(lambda e: e.tensor_scalar(ang, ang, sel[rows, 512:513], None, ALU.mult), t, seltok)
        for parts in turns():
            t = V(lambda e, parts=parts: e.tensor_scalar(ni, ang, float(parts[0]), None, ALU.mult), t)
            t = V(lambda e: e.tensor_copy(nf, ni), t)
            for p in parts[1:]:
                t = V(lambda e, p=p: e.scalar_tensor_tensor(out=ang, in0=nf, scalar=-float(p), in1=ang,
                                                            op0=ALU.mult, op1=ALU.add), t)
        pi = float(np.float32(3.1415925))
        t = V(lambda e: e.tensor_scalar(ang, ang, pi, -pi, ALU.min, ALU.max), t)
        t = V(lambda e: e.tensor_scalar(nf, ang, float(np.pi / 2), None, ALU.add), t)
        t = V(lambda e: e.tensor_scalar(an[rows, 3, :], nf, pi, float(-2 * np.pi), ALU.is_gt, ALU.mult), t)
        t = V(lambda e: e.tensor_tensor(nf, nf, an[rows, 3, :], ALU.add), t)
        t = V(lambda e: e.tensor_scalar(nf, nf, pi, -pi, ALU.min, ALU.max), t)
        scs = [S(lambda e: e.activation(ang, ang, ACT.Sin), t), S(lambda e: e.activation(nf, nf, ACT.Sin), t)]

        def angles():
            out = []
            for dst, src, bank in ((S2, ang, 4), (C2, nf, 3)):
                for b in range(4):
                    m = M(lambda e, b=b, src=src, bank=bank: e.matmul(
                        pb[bank][:, b * P:(b + 1) * P], sel[rows, b * P:(b + 1) * P], src, start=True, stop=True),
                        scs, bf[bank], seltok)
                t = S(lambda e, dst=dst, bank=bank: e.copy(dst[:, :], pb[bank]), m, after2)
                bf[bank] = [t]
                out.append(t)
            return out

        t = proj(0, hi, lo, P, wt, xh, xl, xn)
        done(t)
        cst2 = angles()
        advance()
        advance()
        start(qk_job(2, q2_, v_("gq"), 0.125, q2[:, 2, :], q2t, 0))
        advance()
        start(qk_job(0, t, v_("gq"), 0.125, q2[:, 3, :], q2t, 1))
        hi, lo, wt, done = w_next()
        kcrt = []
        for z in range(2):
            t = proj(z, hi, lo, z * P, wt, xh, xl, xn)
            advance()
            a = V(lambda e, z=z: e.tensor_tensor(kcr[:, z, :], pb[z], rsm[:, :], ALU.mult), t, cst2, rt)
            bf[z] = [a]
            kcrt.append(a)
        done(t)

        def cmp_blocks(z):
            bt = []
            for j in range(2):
                rows = slice(j * 64, (j + 1) * 64)
                for par in range(2):
                    for hh_ in range(2):
                        src = kcr[rows, z, hh_ * 16:hh_ * 16 + 496].rearrange("p (n l two) -> p two l n", n=NCMP, two=2)
                        o = VEC["pev" if z else "pek"][0] + par * 16 + hh_ * 8
                        pe = vec[rows, o:o + 8].unsqueeze(2).broadcast_to([64, 8, NCMP])
                        dst = kb[par * 64:(par + 1) * 64, hh_ * 8:hh_ * 8 + 8, j * NCMP:(j + 1) * NCMP]
                        bt.append(V(lambda e, dst=dst, src=src, par=par, pe=pe: e.tensor_tensor(dst, src[:, par], pe, ALU.add),
                                    kcrt[z], was("kb"), cst2))
            a = S(lambda e: e.copy(kbh[:, :, :], kb[:, :, :]), bt, was("kbh"))
            b = V(lambda e: e.tensor_tensor(kbl[:, :, :], kb[:, :, :], kbh[:, :, :].bitcast(F32), ALU.subtract), a, was("kbh"))
            use("kb", a, b)
            return [a, b]

        def cmp_unit(u, kt_):
            hi, lo, wt, done = w_next()
            for k in range(8):
                t = mm3(pb[3][0:2 * NCMP, 0:256], kbh[:, 8 * u + k, :], kbl[:, 8 * u + k, :], hi[:, k, :], lo[:, k, :],
                        u == 0 and k == 0, u == 1 and k == 7, wt, kt_, bf[3] if u == 0 and k == 0 else None)
            done(t)
            use("kbh", t)
            return t

        def cmp_gelu(t):
            return S(lambda e: e.activation(hidt[0:2 * NCMP, :], pb[3][0:2 * NCMP, 0:256], ACT.Gelu_apprx_tanh), t,
                     was("hidt"), after2)

        def cmp_turn(x):
            for f in range(2):
                m = M(lambda e, f=f: e.transpose(pb[3][:, f * 64:f * 64 + 2 * NCMP], hidt[0:2 * NCMP, f * P:(f + 1) * P],
                                                 cst[0:2 * NCMP, 0:2 * NCMP]), x, ctok)
            use("hidt", m)
            c = S(lambda e: e.copy(hid[:, :, :], pb[3][:, 0:128].rearrange("p (f n) -> p f n", f=2)[:, :, 0:2 * NCMP]), m,
                  was("hid"), after2)
            bf[3] = [c]
            return c

        kbt = cmp_blocks(0)
        hi, lo, wt, done = w_next()
        t = proj(0, hi, lo, 0, wt, xh, xl, xn)
        advance()
        kst2, kwt2 = [], []
        start(qk_job(0, t, v_("gks"), 1.0, ksT[:, 0, :], kst2, 0,
                     then=lambda: kst2.append(swap(ksT[:, 1, :], ksT[:, 0, :], "ksT", list(kst2)))))

        v2st, v2wt, gtt = [], [], []
        t = proj(2, hi, lo, P, wt, xh, xl, xn)
        done(t)
        advance()
        start(v_job(2, t, T, 1, 4, v2s, after2, v2st, rsm[:, :]))
        cmp_unit(0, kbt)
        hi, lo, wt, done = w_next()
        t = proj(1, hi, lo, 0, wt, xh, xl, xn)
        done(t)
        advance()
        start(qk_job(1, t, v_("gkw"), 1.0, kwT[:, 0, :], kwt2, 1,
                     then=lambda: kwt2.append(swap(kwT[:, 1, :], kwT[:, 0, :], "kwT", list(kwt2)))))
        ge = cmp_gelu(cmp_unit(1, kbt))
        kbt = cmp_blocks(1)
        hi, lo, wt, done = w_next()
        t = proj(2, hi, lo, 0, wt, xh, xl, xn)
        ge = cmp_turn(ge)
        advance()
        start(v_job(2, t, T, 0, 4, v2w, after2, v2wt, rsm[:, :]))
        for k in range(NC):
            t = mm3(pb[0][0:24, :], hi[:, k, P:P + 24], lo[:, k, P:P + 24], xh[:, k, :], xl[:, k, :], k == 0, k == NC - 1,
                    wt, xn(k), bf[0] if k == 0 else None)
        done(t)

        def gate_job(t):
            a = V(lambda e: e.tensor_tensor(tmp[1][0:24, :], pb[0][0:24, :], rsm[0:24, :], ALU.mult), t, was("tmp1"))
            bf[0] = [a]
            yield
            for b in range(4):
                m = M(lambda e, b=b: e.transpose(pb[2][:, b * 24:(b + 1) * 24], tmp[1][0:24, b * P:(b + 1) * P],
                                                 cst[0:24, 0:24]), a, bf[2], ctok)
            use("tmp1", m)
            gtt.append(S(lambda e: e.activation(gts[:, :, :], pb[2][:, 0:96].rearrange("p (a b) -> p a b", a=4),
                                                ACT.Sigmoid), m, after2))
            bf[2] = list(gtt)
            yield

        advance()
        start(gate_job(t))
        for f in range(2):
            m = M(lambda e, f=f: e.matmul(pb[1][:, 0:2 * NCMP], w2c[:, 0, f, :], hid[:, f, :], start=f == 0,
                                          stop=f == 1), ge, w2tok, bf[1])
        use("hid", m)
        kct2 = []
        start(qk_job(1, m, v_("gkc"), 1.0, kcC[:, :], kct2, 0, 2 * NCMP, C2[:, 31:T:16], S2[:, 31:T:16]))
        cmp_unit(0, kbt)
        qst, ksbt = [], []
        for u in range(4):
            hi, lo, wt, done = w_next()
            for cc in range(2):
                c = 2 * (u % 2) + cc
                t = proj(cc, hi, lo, cc * P, wt, xh, xl, xn)
                if u == 1 and cc == 0:
                    ge = cmp_turn(ge)
                advance()
                if u < 2:
                    a = V(lambda e, c=c, cc=cc: e.scalar_tensor_tensor(out=qsT[:, c, :], in0=pb[cc], scalar=0.125,
                                                                       in1=rsm[:, :], op0=ALU.mult, op1=ALU.mult), t, after2)
                    qst.append(a)
                else:
                    a = V(lambda e, c=c, cc=cc: e.tensor_tensor(ksbT[:, c, :], pb[cc], rsm[:, :], ALU.mult), t, after2)
                    ksbt.append(a)
                bf[cc] = [a]
            done(t)
            if u == 0:
                ge = cmp_gelu(cmp_unit(1, kbt))
            elif u == 1:
                for j in range(2):
                    for f in range(2):
                        m = M(lambda e, f=f, j=j: e.matmul(pb[1][0:NCMP, j * P:(j + 1) * P],
                                                           hid[:, f, j * NCMP:(j + 1) * NCMP],
                                                           w2c[:, 1, f, :], start=f == 0, stop=f == 1), ge, w2tok, bf[1])
                vct2 = [S(lambda e: e.copy(vcC[0:NCMP, :], pb[1][0:NCMP, 0:256]), m)]
                bf[1] = vct2
        vsbt = []
        for u in range(2):
            hi, lo, wt, done = w_next()
            for tb in range(4):
                bank = 2 + tb % 3
                t = proj_tok(bank, hi, lo, 0, 256, wt, xh, xl, xn, tb)
                a = S(lambda e, tb=tb, bank=bank, u=u: e.activation(vsb[:, tb, u * 256:(u + 1) * 256], pb[bank][:, 0:256],
                                                                     ACT.Identity, scale=rcol[:, tb:tb + 1]), t, after2, rct)
                bf[bank] = [a]
                vsbt.append(a)
            done(t)
        xlast = t
        drain()
        n3.close()
        n3 = ExitStack()
        pr2 = sb("pr2", [P, 2, 4, T], F32, n3)
        pt2 = sb("pt2", [P, 2, 4 * T], F32, n3)
        after3 = fence()
        use("prob0", *after3)
        use("prob1", *after3)
        use("pt0", *after3)
        use("pt1", *after3)
        mixt = [[] for _ in range(NC)]

        def nsa():
            jobs = [(i, j, br) for i in range(4) for j in range(2) for br in range(3)]

            def a_stage(n_, i, j, br):
                par = seq["n"] % 2
                width = NCMP if br == 0 else (i + 1) * P

                def qk(g):
                    h = 4 * j + g
                    r = slice((h % 2) * 64, (h % 2) * 64 + 64)
                    q = q2[r, h // 2, i * P:(i + 1) * P]
                    if br == 0:
                        return [(q, kcC[r, j * NCMP:(j + 1) * NCMP], 0, NCMP)]
                    kk = ksT if br == 1 else kwT
                    sw = 0 if h % 2 == j else 1
                    full = [(q, kk[r, sw, 0:i * P], 0, i * P)] if i else []
                    return full + [(q, kk[r, sw, i * P:(i + 1) * P], i * P, P)]

                masks = [(0, NCMP, b_("cmp", NCMP, 32 * i))] if br == 0 else [(i * P, P, b_("diag"))]
                gate = gts[:, i, :].rearrange("p (j g b) -> p j b g", j=2, g=4)[:, j, br]
                return soft_a(4, qk, masks, width, lambda g: g * 512, pr2[:, par, :, :],
                              [q2t, kct2, kst2, kwt2], gate=gate, gtok=gtt,
                              valid=k_("valid") if br == 0 and i == 0 else None)

            def values(i, j, br):
                if br == 0:
                    return [(0, NCMP, vcC[0:NCMP, j * P:(j + 1) * P], vct2)]
                v, vtk = (v2s, v2st) if br == 1 else (v2w, v2wt)
                return [(b * P, P, v[:, b, j * P:(j + 1) * P], vtk[b]) for b in range(i + 1)]

            def b_stage(n, i, j, br, got):
                par, tok = got
                return soft_b(4, pr2[:, par, :, :], tok, par, values(i, j, br), pt2[:, par, :])

            def c_stage(n, i, j, br, got):
                (par, tok), evs = got
                ob = 6
                t = soft_c(4, evs, par, values(i, j, br), pt2[:, par, :], ob, br == 0, br == 2)
                if br == 2:
                    last = []
                    for o in range(2):
                        r = slice(o * 64, o * 64 + 64)
                        cols = slice(i * P, (i + 1) * P)
                        src = pb[ob][r, :].rearrange("p (a o q) -> p o a q", o=2, q=P)[:, o]
                        tk = put(ob, r, src, xh[r, 2 * j:2 * j + 2, cols], xl[r, 2 * j:2 * j + 2, cols], t, 2 * j)
                        mixt[2 * j + 1] += tk
                        last += tk
                    bf[ob] = last

            return [((a_stage, b_stage, c_stage), job) for job in jobs]

        ze = C2S2[:, 0:1280]
        zs = [pr2[:, par].rearrange("p g t -> p (g t)")[:, 0:1280] for par in range(2)]
        za = [pt2[:, par, 0:1280] for par in range(2)]
        use("ze", *after3)
        ZC = [0, 512, 1024, 896]
        ZW = [512, 384, 256, 128]

        def zb(par):
            return [zs[par][:, ZC[b]:ZC[b] + ZW[b]] for b in range(4)]

        def zu(par):
            rest = pr2[:, par].rearrange("p g t -> p (g t)")[:, 1280:1920]
            return [rest[:, 0:384], rest[:, 384:640], zb(par)[3]]

        def stick():
            def a_stage(n, h):
                base = 3 * (h % 2)
                r = slice((h % 2) * 64, (h % 2) * 64 + 64)
                c = h // 2
                zo = base * 512
                m = []
                for b in (0, 1, 3, 2):
                    m.append(M(lambda e, b=b: e.matmul(
                        ps[:, zo + ZC[b]:zo + ZC[b] + ZW[b]], ksbT[r, c, b * P:(b + 1) * P], qsT[r, c, b * P:T],
                        start=b < 3, stop=False, skip_group_check=True), qst, ksbt, bf[base + ZC[b] // 512]))
                zz = ps[:, zo:zo + 1280]
                par = h % 2
                e0 = S(lambda e: e.activation(ze[:, 0:512], zz[:, 0:512], ACT.Abs), m[0], was("ze"))
                e1 = S(lambda e: e.activation(ze[:, 512:1280], zz[:, 512:1280], ACT.Abs), m, was("ze"))
                e1 = S(lambda e: e.activation(ze, ze, ACT.Exp, scale=-1.0), e0, e1)
                e1 = S(lambda e: e.activation(ze, ze, ACT.Ln, bias=k_("one")), e1)
                s_ = V(lambda e: e.scalar_tensor_tensor(out=zs[par], in0=zz, scalar=0.0, in1=ze,
                                                        op0=ALU.max, op1=ALU.add), e1, was(f"prob{par}"))
                use("ze", s_)
                z_ = zb(par)
                ms = [V(lambda e, b=b: e.tensor_tensor(z_[b][:, 0:P], z_[b][:, 0:P], b2("sb01"), ALU.mult), s_, b2tok)
                      for b in range(4)]
                u = zu(par)
                t1 = V(lambda e: e.tensor_copy(u[1][:, 0:P], z_[2][:, 0:P]), ms)
                t2 = V(lambda e: e.tensor_tensor(u[1][:, P:256], z_[2][:, P:256], z_[3], ALU.add), ms)
                t3 = V(lambda e: e.tensor_copy(u[0][:, 0:P], z_[1][:, 0:P]), ms)
                t4 = V(lambda e: e.tensor_tensor(u[0][:, P:384], z_[1][:, P:384], u[1], ALU.add), t1, t2)
                return s_, [t3, t4]

            def b_stage(n, h, got):
                s_, ms = got
                base = 3 * (h % 2)
                zo = base * 512
                par = h % 2
                z_, u = zb(par), zu(par)
                for b in range(4):
                    M(lambda e, b=b: e.matmul(ps[:, zo + ZC[b]:zo + ZC[b] + ZW[b]], b2("tri"), z_[b],
                                              start=False, stop=False, skip_group_check=True), ms)
                    if b < 3:
                        M(lambda e, b=b: e.matmul(ps[:, zo + ZC[b] + P:zo + ZC[b] + ZW[b]], b2("neg1"), u[b],
                                                  start=False, stop=False, skip_group_check=True), ms)
                    m = M(lambda e, b=b: e.matmul(ps[:, zo + ZC[b]:zo + ZC[b] + P], b_("ident"), b_("sbm"),
                                                  start=False, stop=True, skip_group_check=True))
                use(f"prob{par}", m)
                x = [S(lambda e, a=a, z=z: e.activation(za[par][:, a:z], ps[:, zo + a:zo + z], ACT.Exp), m, was(f"pt{par}"))
                     for a, z in ((0, 512), (512, 1280))]
                for k in range(3):
                    bf[base + k] = [x[min(k, 1)], s_]
                return x

            def c_stage(n, h, got):
                par = h % 2
                ob = 6 + par
                r = slice((h % 2) * 64, (h % 2) * 64 + 64)
                c = h // 2
                for b in range(4):
                    t = M(lambda e, b=b: e.matmul(pb[ob][:, b * P:T], vsb[:, b, c * P:(c + 1) * P],
                                                  za[par][:, ZC[b]:ZC[b] + ZW[b]], start=b == 0, stop=b == 3,
                                                  skip_group_check=True), got[1], vsbt, bf[ob] if b == 0 else None)
                use(f"pt{par}", t)
                bf[ob] = put(ob, r, pb[ob][r, :], xh[r, 4 + c, :], xl[r, 4 + c, :], t, 4 + c)

            return [((a_stage, b_stage, c_stage), (h,)) for h in range(8)]

        both_kinds = nsa() + stick()
        pipeline([job for _, job in both_kinds], *(
            lambda n, *job, k=k: both_kinds[n][0][k](n, *job) for k in range(3)))
        xn3 = []

        def to_memory(after):
            def go_on(c, tok):
                for k in range(NC):
                    split_x(k, lambda k: v_("memx", k), xtok[k], after, xn3)

            return go_on

        mix_out(lambda c: k_("one"), ctok, to_memory)
        n3.close()
        n2.close()

        m2 = ExitStack()
        qm = sb("qm", [P, 2, T], F32, m2)
        pr3 = sb("pr3", [P, 2, 4, LC], F32, m2)
        pt3 = sb("pt3", [P, 2, 2 * T], F32, m2)
        oh = sb("oh", [P, 2, T], F32R, m2)
        ol = sb("ol", [P, 2, T], F32R, m2)
        after5 = fence()
        hi, lo, wt, done = w_next()
        qmt = []
        gq8 = cf[:, 0:1]
        V(lambda e: e.tensor_scalar(gq8, v_("gmq"), 0.125, None, ALU.mult), ctok)

        def qm_job(c, t):
            a = V(lambda e: e.tensor_tensor(qm[:, c, :], pb[c], rsx, ALU.mult), t, rt, after5)
            bf[c] = [a]
            q = S(lambda e: e.activation(tmp[c][:, :], qm[:, c, :], ACT.Square), a, was(f"tmp{c}"))
            yield
            yield from head_norm(qm[:, c, :], [a, q], c, gq8, T, qm[:, c, :], qmt)

        ts = [proj(0, hi, lo, 0, wt, xh, xl, lambda k: xn3[k])]
        end = late_rstd(rsx, after5)
        last_q = proj(1, hi, lo, P, wt, xh, xl, lambda k: xn3[k])
        done(last_q)
        rt, _ = end()
        start(qm_job(0, ts[0]))
        start(qm_job(1, last_q))
        drain()
        use("prob0", *after5)
        use("prob1", *after5)
        use("pt0", *after5)
        use("pt1", *after5)
        omt = [[], []]

        def memory():
            def a_stage(n, i):
                par = seq["n"] % 2

                def qk(g):
                    r = slice((g % 2) * 64, (g % 2) * 64 + 64)
                    return [(qm[r, g // 2, i * P:(i + 1) * P], kmT[r, g // 2, :], 0, LC)]

                return soft_a(4, qk, [], LC, lambda g: g * 512, pr3[:, par, :, :], [qmt, kmtok])

            def b_stage(n, i, got):
                par, tok = got
                return soft_b(4, pr3[:, par, :, :], tok, par, [(b * P, P, None, None) for b in range(2)], pt3[:, par, :], (4, 5))

            def c_stage(n, i, got):
                (par, tok), evs = got
                for c in range(2):
                    ob = 6 + c
                    for b in range(2):
                        t = M(lambda e, b=b, c=c, ob=ob: e.matmul(
                            pb[ob][:, 0:256], vm[:, b, c * P:(c + 1) * P], pt3[:, par, b * T + c * 256:b * T + (c + 1) * 256],
                            start=b == 0, stop=b == 1), evs[b], vmtok, bf[ob] if b == 0 else None)
                    last = []
                    for o in range(2):
                        r = slice(o * 64, o * 64 + 64)
                        cols = slice(i * P, (i + 1) * P)
                        src = pb[ob][r, o * P:(o + 1) * P]
                        a = S(lambda e, r=r, c=c, cols=cols, src=src: e.copy(oh[r, c, cols], src), t, after5)
                        b_ = V(lambda e, r=r, c=c, cols=cols, src=src: e.tensor_tensor(
                            ol[r, c, cols], src, oh[r, c, cols].bitcast(F32), ALU.subtract), a)
                        last += [a, b_]
                    omt[c] += last
                    bf[ob] = last
                use(f"pt{par}", t)

            pipeline([(i,) for i in range(4)], a_stage, b_stage, c_stage)

        memory()
        hi, lo, wt, done = w_next()
        xn4, held = [], []
        for c in range(NC):
            t = proj(c % 4, hi, lo, c * P, wt, oh, ol, lambda k: omt[k], 2)
            residual(c, c % 4, k_("one"), t, ctok, adder=G if c < NC - 1 else V,
                     early=lambda c, tok: split_x(c, lambda k: v_("n2", k), tok, last_q, xn4, held))
        done(t)
        m2.close()

        ov = out.rearrange("(c p) t -> p c t", p=P)
        outs = []

        def store(c, tok):
            outs.append(load(SP, "out", ov[:, c, :], xT[:, c, :], tok))

        def last_rstd():
            end = late_rstd(rsx, rt)
            return lambda: end()[0]

        ffn(lambda c: k_("half"), lambda: ctok, lambda k: xn4[k], fence(), keep=False, final=store, rstd=last_rstd)
        SP(lambda e: e.nop(), outs[-1])

        for q in (V, S, G, M, SP):
            q.number()
        block = ctx.enter_context(nc.Block())

        @block.sync
        def _(eng):
            SP.emit(eng)

        @block.gpsimd
        def _(eng):
            G.emit(eng)

        @block.scalar
        def _(eng):
            S.emit(eng)

        @block.vector
        def _(eng):
            V.emit(eng)

        @block.tensor
        def _(eng):
            M.emit(eng)


def parts_of(x, bits, n):
    out, rest = [], float(x)
    for _ in range(n - 1):
        m, e = np.frexp(rest)
        p = float(np.ldexp(np.floor(m * 2 ** bits), int(e) - bits))
        out.append(p)
        rest -= p
    return out + [rest]


def turns():
    return [[1.0 / (2 * np.pi * n)] + parts_of(2 * np.pi * n, 11, 3) for n in (4096, 1)]


def constants():
    f = np.float32
    r = np.arange(P)
    cst = np.zeros((P, NCST), f)
    cst[:, 0:128] = np.eye(P)
    cst[:, 128:256] = 1
    cst[:, 256:384] = (r[:, None] // 64) == (r[None] // 64)
    cst[:, CST["eps"]] = EPS
    cst[:, CST["one"]] = 1
    cst[:, CST["half"]] = 0.5
    freq = (np.float64(500000.0) ** (-np.arange(0, 16, 2, dtype=np.float32).astype(np.float64) / 16)).astype(f)
    d = r % 64
    cst[:, CST["freq"]] = np.where(d < 16, freq[d % 8], 0)
    cst[:, CST["valid"]] = r >= 31
    masks = np.zeros((P, NBCS), f)
    q, k = r[:, None], r[None]
    masks[:, 0:128] = np.eye(P)
    masks[:, BCS["diag"]:][:, :128] = np.where(k <= q, 0, NEG)
    masks[:, BCS["prev"]:][:, :128] = np.where(k >= q, 0, NEG)
    masks[:, BCS["sbm"]:][:, :128] = np.where(q < k, 0, NEG)
    for i in range(4):
        ends = np.arange(NCMP) * 16 + 31
        masks[:, BCS["cmp"] + 32 * i:][:, :NCMP] = np.where(ends[None] <= q + i * P, 0, NEG)
    b1 = np.zeros((P, NB1C), f)
    rot = np.zeros((P, P), f)
    rot[r[1::2], r[0::2]] = -1
    rot[r[0::2], r[1::2]] = 1
    b1[:, 0:128] = rot
    t = np.arange(T)
    inv = (np.float64(10000.0) ** (-np.arange(16, dtype=np.float64) / 16)).astype(f)
    ang = np.concatenate([(t // 64).astype(f)[:, None] * inv[None], (t % 64).astype(f)[:, None] * inv[None]], 1)
    ang = np.repeat(ang.T, 2, axis=0)
    ang = np.concatenate([ang, ang], 0).astype(np.float64)
    b1[:, 128:640] = np.cos(ang)
    b1[:, 640:1152] = np.sin(ang)
    w = 2 * np.pi * (np.outer(r, r) % P) / P
    b1[:, 1152:1280] = np.cos(w) / np.sqrt(P)
    b1[:, 1280:1408] = np.sin(w) / np.sqrt(P)
    w = 2 * np.pi * (np.outer(t, t) % T) / T
    cn, sn = np.cos(w) / np.sqrt(T), -np.sin(w) / np.sqrt(T)
    b1[:, B1C["cn"]:][:, :2048] = cn.reshape(4, P, T).transpose(1, 0, 2).reshape(P, 2048)
    b1[:, B1C["sn"]:][:, :2048] = sn.reshape(4, P, T).transpose(1, 0, 2).reshape(P, 2048)
    b2 = np.zeros((P, NB2C + 513), f)
    rot = np.zeros((P, P), f)
    for o in (0, 64):
        for i in range(8):
            rot[o + 8 + i, o + i] = -1
            rot[o + i, o + 8 + i] = 1
    b2[:, 0:128] = rot
    b2[:, 128:256] = -(q >= k).astype(f)
    b2[:, 256:384] = -1
    b2[:, 384:512] = q < k
    for i in range(4):
        b2[:, NB2C + i * P:][:, :P] = np.where(d[None] < 16, q == 8 * i + d[None] % 8, q == 32)
    b2[:32, NB2C + 512] = np.tile(freq, 4)
    cnt = np.stack([np.minimum(t + n // 2, T) - np.maximum(t - n // 2, 0) for n in (2, 4, 8, 16)])
    icnt = np.stack([(2 << g) / cnt[g].reshape(T // 8, 8)[[0, -1]] for g in range(4)])
    icnt = np.broadcast_to(icnt.astype(f)[None], (P, 4, 2, 8))
    return {"consts": cst, "masks": masks, "b1c": b1, "b2c": b2, "icnt": np.ascontiguousarray(icnt)}


_WEIGHTS = ["ada_w", "mix_in_w", "mix_out_w", "pool_w", "ffn_w1", "ffn_w3", "ffn_w2", "positions_2", "ffn1_wg_2",
            "ffn1_wu_2", "ffn1_wd_2", "w_in_2", "cmp_w1_k_2", "cmp_w2_k_2", "cmp_w1_v_2", "cmp_w2_v_2", "w_out_2",
            "mem_wq_2", "mem_wk_2", "mem_wv_2", "mem_wo_2", "ffn2_wg_2", "ffn2_wu_2", "ffn2_wd_2"]


def kernel(**inputs):
    import concourse.bacc as bacc
    from concourse.bass_utils import run_bass_kernel_spmd

    a = {k: np.asarray(v) for k, v in inputs.items()}

    def col(v):
        return np.asarray(v).reshape(-1, P).T

    def two(v):
        return np.concatenate([v.reshape(64, 1)] * 2, 0)

    def pe(v):
        w = v.reshape(16, 2, 64).transpose(2, 1, 0).reshape(64, 32)
        return np.concatenate([w, w], 0)

    vecs = {
        "c": col(a["c"]), "cc": col(a["c_ctx"]), "ab0": col(a["ada_b"][0]), "ab1": col(a["ada_b"][1]),
        "gm0": col(a["norm_mix_g"][0]), "gm1": col(a["norm_mix_g"][1]),
        "gf0": col(a["norm_ffn_g"][0]), "gf1": col(a["norm_ffn_g"][1]),
        "pscale": col(a["pool_scale"]), "fin": col(a["final_g"]), "n1": col(a["ffn1_norm_2"]),
        "mixg": col(a["mix_norm_2"]), "memx": col(a["mem_x_norm_2"]), "memkv": col(a["mem_kv_norm_2"]),
        "n2": col(a["ffn2_norm_2"]), "gq": two(a["nsa_q_norm_2"]), "gkc": two(a["nsa_kc_norm_2"]),
        "gks": two(a["nsa_ks_norm_2"]), "gkw": two(a["nsa_kw_norm_2"]), "gmq": two(a["mem_q_norm_2"]),
        "gmk": two(a["mem_k_norm_2"]), "sink": np.broadcast_to(a["attn_sink"].reshape(1, 8), (P, 8)),
        "pek": pe(a["cmp_pos_k_2"]), "pev": pe(a["cmp_pos_v_2"]),
    }
    arrays = {n: np.ascontiguousarray(a[n]) for n in _WEIGHTS}
    arrays["vecs"] = np.ascontiguousarray(np.concatenate([vecs[n] for n in VEC], 1))
    arrays["xT"] = np.ascontiguousarray(a["x"][0].T)
    arrays["ctxT"] = np.ascontiguousarray(a["ctx"][0].T)
    arrays["memT"] = np.ascontiguousarray(a["mem_2"][0].T)
    arrays.update(constants())
    nc = bacc.Bacc("TRN2", target_bir_lowering=False, num_devices=1)
    ins = {n: nc.dram_tensor("in_" + n, v.shape, mybir.dt.from_np(v.dtype), kind="ExternalInput").ap()
           for n, v in arrays.items()}
    out = nc.dram_tensor("out", (D, T), F32, kind="ExternalOutput").ap()
    program(nc, ins, out)
    r = run_bass_kernel_spmd(nc, [{"in_" + n: v for n, v in arrays.items()}], core_ids=[0])
    return np.ascontiguousarray(r.results[0]["out"].T)[None]
```
